# Optimizing a Trainium2 kernel written in Bass

```python
import jax, jax.numpy as jnp
from jax import lax
import numpy as np

D_MODEL = 1024
BATCH = 1
SEQ = 256
DEPTH = 2

GRID_W = 64
HEAD_DIM = 64
ROPE_THETA = 10000.0
PLE_DIM = 256
NORM_EPS = 1e-6
NEG_INF = -1e30
Q_BLOCK = 128

A_HEADS = 4
A_Q_RANK = 256
A_KV_RANK = 128
A_NOPE = 64
A_ROPE = 32
A_V = 64
B_HEADS = 4
B_KV_HEADS = 2
C_PATTERNS = ((128, 1), (512, 4), (2048, 16))
C_HEADS_PER_GROUP = 4
C_BLOCK = 64
D_HEADS = 4
D_KV_HEADS = 2
D_HALF_WINDOW = 128
D_BLOCK = 128

N_BRANCHES = 4
BRANCH_WIDTH = 256

A_COLS = A_Q_RANK + A_KV_RANK + A_ROPE
B_COLS = (B_HEADS + 2 * B_KV_HEADS) * HEAD_DIM
C_COLS = len(C_PATTERNS) * 3 * C_HEADS_PER_GROUP * HEAD_DIM
D_COLS = (D_HEADS + 2 * D_KV_HEADS) * HEAD_DIM
GATE_COLS = N_BRANCHES * D_MODEL
IN_COLS = A_COLS + B_COLS + C_COLS + D_COLS + GATE_COLS
SPLIT_POINTS = (A_COLS, A_COLS + B_COLS, A_COLS + B_COLS + C_COLS, A_COLS + B_COLS + C_COLS + D_COLS)

D_FF = 4096
N_EXPERTS = 8
TOP_K = 2
MOE_FF = 3584
MOE_BLOCK = 128
N_DENSE = (DEPTH + 1) // 2
N_MOE = DEPTH // 2

kernel_name = "hybrid_gated_parallel_mixers_encoder"

def rms_norm(x, g):
    xf = x.astype(jnp.float32)
    y = xf * lax.rsqrt(jnp.mean(xf * xf, axis=-1, keepdims=True) + NORM_EPS)
    return (y * g.astype(jnp.float32)).astype(x.dtype)

def rope_tables(pos, dim):
    half = dim // 2
    inv = jnp.power(ROPE_THETA, -jnp.arange(half, dtype=jnp.float32) / half)
    ang = pos.astype(jnp.float32)[:, None] * inv[None, :]
    return jnp.cos(ang), jnp.sin(ang)

def apply_rope(x, cos, sin):
    half = x.shape[-1] // 2
    x1 = x[..., :half].astype(jnp.float32)
    x2 = x[..., half:].astype(jnp.float32)
    c = cos[:, None, :]
    s = sin[:, None, :]
    return jnp.concatenate([x1 * c - x2 * s, x2 * c + x1 * s], axis=-1).astype(x.dtype)

def axial_rope(x, row_tab, col_tab):
    half = x.shape[-1] // 2
    return jnp.concatenate([apply_rope(x[..., :half], *row_tab), apply_rope(x[..., half:], *col_tab)], axis=-1)

def dense_attention(q, k, v):
    bsz, seq, n_heads, dq = q.shape
    n_kv = k.shape[2]
    rep = n_heads // n_kv
    dv = v.shape[-1]
    nb = seq // Q_BLOCK
    qb = q.reshape(bsz, nb, Q_BLOCK, n_kv, rep, dq).transpose(1, 0, 2, 3, 4, 5)
    scale = dq ** -0.5

    def block(qblk):
        s = jnp.einsum('bqgrd,bkgd->bgrqk', qblk, k).astype(jnp.float32) * scale
        p = jax.nn.softmax(s, axis=-1).astype(v.dtype)
        return jnp.einsum('bgrqk,bkgd->bqgrd', p, v)

    o = lax.map(block, qb)
    return o.transpose(1, 0, 2, 3, 4, 5).reshape(bsz, seq, n_heads, dv)

def banded_attention(q, k, v, half_w, blk, sink):
    bsz, length, n_heads, dim = q.shape
    n_kv = k.shape[2]
    rep = n_heads // n_kv
    nb = -(-length // blk)
    lp = nb * blk
    qp = jnp.pad(q, ((0, 0), (0, lp - length), (0, 0), (0, 0)))
    kv_pad = ((0, 0), (half_w, lp - length + half_w), (0, 0), (0, 0))
    kp = jnp.pad(k, kv_pad)
    vp = jnp.pad(v, kv_pad)
    kw = blk + 2 * half_w
    idx = jnp.arange(nb)[:, None] * blk + jnp.arange(kw)[None, :]
    kb = kp[:, idx]
    vb = vp[:, idx]
    qb = qp.reshape(bsz, nb, blk, n_kv, rep, dim)
    s = jnp.einsum('bnqgrd,bnkgd->bngrqk', qb, kb).astype(jnp.float32) * (dim ** -0.5)
    qpos = jnp.arange(nb)[:, None] * blk + jnp.arange(blk)[None, :]
    kpos = idx - half_w
    valid = ((jnp.abs(qpos[:, :, None] - kpos[:, None, :]) <= half_w)
             & (kpos[:, None, :] >= 0) & (kpos[:, None, :] < length))
    s = jnp.where(valid[None, :, None, None], s, NEG_INF)
    m = jnp.max(s, axis=-1)
    if sink is not None:
        sink_logit = sink.astype(jnp.float32).reshape(n_kv, rep)[None, None, :, :, None]
        m = jnp.maximum(m, sink_logit)
    e = jnp.exp(s - m[..., None])
    l = jnp.sum(e, axis=-1)
    if sink is not None:
        l = l + jnp.exp(sink_logit - m)
    o = jnp.einsum('bngrqk,bnkgd->bnqgrd', e.astype(v.dtype), vb).astype(jnp.float32)
    o = o / jnp.transpose(l, (0, 1, 4, 2, 3))[..., None]
    o = o.reshape(bsz, lp, n_heads, dim)[:, :length].astype(q.dtype)
    lse = jnp.transpose(m + jnp.log(l), (0, 1, 4, 2, 3)).reshape(bsz, lp, n_heads)[:, :length]
    return o, lse

def dilated_attention(q, k, v, window, dilation):
    bsz, seq, n_heads, dim = q.shape
    ls = seq // dilation

    def to_classes(x):
        return x.reshape(bsz, ls, dilation, n_heads, dim).transpose(0, 2, 1, 3, 4).reshape(bsz * dilation, ls, n_heads, dim)

    o, lse = banded_attention(to_classes(q), to_classes(k), to_classes(v), window // (2 * dilation), C_BLOCK, None)
    o = o.reshape(bsz, dilation, ls, n_heads, dim).transpose(0, 2, 1, 3, 4).reshape(bsz, seq, n_heads, dim)
    lse = lse.reshape(bsz, dilation, ls, n_heads).transpose(0, 2, 1, 3).reshape(bsz, seq, n_heads)
    return o, lse

def token_mixers(h, tabs, w_in, a_qa_g, a_kva_g, a_w_uq, a_w_ukv, b_q_g, b_k_g, d_sink, w_branch, w_out):
    bsz, seq, _ = h.shape
    rope_a, rope_row, rope_col, rope_full = tabs
    z = h @ w_in
    z_a, z_b, z_c, z_d, z_gate = jnp.split(z, list(SPLIT_POINTS), axis=-1)

    c_q, c_kv, k_r = jnp.split(z_a, [A_Q_RANK, A_Q_RANK + A_KV_RANK], axis=-1)
    q_a = (rms_norm(c_q, a_qa_g) @ a_w_uq).reshape(bsz, seq, A_HEADS, A_NOPE + A_ROPE)
    q_a = jnp.concatenate([q_a[..., :A_NOPE], apply_rope(q_a[..., A_NOPE:], *rope_a)], axis=-1)
    kv_a = (rms_norm(c_kv, a_kva_g) @ a_w_ukv).reshape(bsz, seq, A_HEADS, A_NOPE + A_V)
    k_rope = apply_rope(k_r[:, :, None, :], *rope_a)
    k_a = jnp.concatenate([kv_a[..., :A_NOPE], jnp.broadcast_to(k_rope, (bsz, seq, A_HEADS, A_ROPE))], axis=-1)
    o_a = dense_attention(q_a, k_a, kv_a[..., A_NOPE:])

    q_b, k_b, v_b = jnp.split(z_b, [B_HEADS * HEAD_DIM, (B_HEADS + B_KV_HEADS) * HEAD_DIM], axis=-1)
    q_b = axial_rope(rms_norm(q_b.reshape(bsz, seq, B_HEADS, HEAD_DIM), b_q_g), rope_row, rope_col)
    k_b = axial_rope(rms_norm(k_b.reshape(bsz, seq, B_KV_HEADS, HEAD_DIM), b_k_g), rope_row, rope_col)
    o_b = dense_attention(q_b, k_b, v_b.reshape(bsz, seq, B_KV_HEADS, HEAD_DIM))

    zc = z_c.reshape(bsz, seq, len(C_PATTERNS), 3, C_HEADS_PER_GROUP, HEAD_DIM)
    outs, lses = [], []
    for gi, (win, dil) in enumerate(C_PATTERNS):
        og, lg = dilated_attention(apply_rope(zc[:, :, gi, 0], *rope_full), apply_rope(zc[:, :, gi, 1], *rope_full),
                                   zc[:, :, gi, 2], win, dil)
        outs.append(og)
        lses.append(lg)
    alpha = jax.nn.softmax(jnp.stack(lses, axis=0), axis=0)
    o_c = jnp.einsum('gbsh,gbshd->bshd', alpha, jnp.stack(outs, axis=0).astype(jnp.float32)).astype(h.dtype)

    q_d, k_d, v_d = jnp.split(z_d, [D_HEADS * HEAD_DIM, (D_HEADS + D_KV_HEADS) * HEAD_DIM], axis=-1)
    q_d = apply_rope(q_d.reshape(bsz, seq, D_HEADS, HEAD_DIM), *rope_full)
    k_d = apply_rope(k_d.reshape(bsz, seq, D_KV_HEADS, HEAD_DIM), *rope_full)
    o_d, _ = banded_attention(q_d, k_d, v_d.reshape(bsz, seq, D_KV_HEADS, HEAD_DIM), D_HALF_WINDOW, D_BLOCK, d_sink)

    gates = jax.nn.sigmoid(z_gate.astype(jnp.float32)).astype(h.dtype).reshape(bsz, seq, N_BRANCHES, D_MODEL)
    merged = jnp.zeros((bsz, seq, D_MODEL), h.dtype)
    for n, o in enumerate((o_a, o_b, o_c, o_d)):
        merged = merged + gates[:, :, n] * (o.reshape(bsz, seq, BRANCH_WIDTH) @ w_branch[n])
    return merged @ w_out

def swiglu(h, wg, wu, wd):
    return (jax.nn.silu(h @ wg) * (h @ wu)) @ wd

def moe_swiglu(h, w_router, b_router, wg, wu, wd):
    bsz, seq, dm = h.shape
    n_tok = bsz * seq
    xf = h.reshape(n_tok, dm)
    logits = (xf @ w_router).astype(jnp.float32) + b_router.astype(jnp.float32)
    top_v, top_e = lax.top_k(logits, TOP_K)
    gate = jax.nn.softmax(top_v, axis=-1)
    n_asg = n_tok * TOP_K
    e_flat = top_e.reshape(n_asg)
    tok_flat = jnp.repeat(jnp.arange(n_tok, dtype=jnp.int32), TOP_K)
    g_flat = gate.reshape(n_asg)
    order = jnp.argsort(e_flat)
    e_s, tok_s, g_s = e_flat[order], tok_flat[order], g_flat[order]
    counts = jnp.bincount(e_flat, length=N_EXPERTS)
    start = jnp.cumsum(counts) - counts
    padded = ((counts + MOE_BLOCK - 1) // MOE_BLOCK) * MOE_BLOCK
    pend = jnp.cumsum(padded)
    pstart = pend - padded
    dest = pstart[e_s] + (jnp.arange(n_asg) - start[e_s])
    nb = -(-n_asg // MOE_BLOCK) + N_EXPERTS
    n_rows = nb * MOE_BLOCK
    buf_tok = jnp.zeros((n_rows,), jnp.int32).at[dest].set(tok_s)
    buf_g = jnp.zeros((n_rows,), jnp.float32).at[dest].set(g_s)
    blk_e = jnp.clip(jnp.searchsorted(pend, jnp.arange(nb) * MOE_BLOCK, side='right'), 0, N_EXPERTS - 1)
    xb = xf[buf_tok].reshape(nb, MOE_BLOCK, dm)

    def expert_block(args):
        xblk, e = args
        return swiglu(xblk, wg[e], wu[e], wd[e])

    yb = lax.map(expert_block, (xb, blk_e)).reshape(n_rows, dm)
    out = jnp.zeros((n_tok, dm), h.dtype).at[buf_tok].add(yb * buf_g[:, None].astype(h.dtype))
    return out.reshape(bsz, seq, dm)

def setup_inputs(seed: int = 0) -> dict:
    key = jax.random.key(seed)
    ks = iter(jax.random.split(key, 32))
    f32 = jnp.float32

    def w(shape, fan_in):
        return jax.random.normal(next(ks), shape, f32) * (fan_in ** -0.5)

    def gain(shape):
        return 1.0 + 0.05 * jax.random.normal(next(ks), shape, f32)

    return {
        "x": jax.random.normal(next(ks), (BATCH, SEQ, D_MODEL), f32),
        "p": jax.random.normal(next(ks), (DEPTH, BATCH, SEQ, PLE_DIM), f32),
        "w_in": w((DEPTH, D_MODEL, IN_COLS), D_MODEL),
        "a_qa_g": gain((DEPTH, A_Q_RANK)),
        "a_kva_g": gain((DEPTH, A_KV_RANK)),
        "a_w_uq": w((DEPTH, A_Q_RANK, A_HEADS * (A_NOPE + A_ROPE)), A_Q_RANK),
        "a_w_ukv": w((DEPTH, A_KV_RANK, A_HEADS * (A_NOPE + A_V)), A_KV_RANK),
        "b_q_g": gain((DEPTH, HEAD_DIM)),
        "b_k_g": gain((DEPTH, HEAD_DIM)),
        "d_sink": 0.5 * jax.random.normal(next(ks), (DEPTH, D_HEADS), f32),
        "w_branch": w((DEPTH, N_BRANCHES, BRANCH_WIDTH, D_MODEL), BRANCH_WIDTH),
        "w_out": w((DEPTH, D_MODEL, D_MODEL), D_MODEL),
        "mix_pre_g": gain((DEPTH, D_MODEL)),
        "mix_post_g": gain((DEPTH, D_MODEL)),
        "ffn_pre_g": gain((DEPTH, D_MODEL)),
        "ffn_post_g": gain((DEPTH, D_MODEL)),
        "ffn_w_gate": w((N_DENSE, D_MODEL, D_FF), D_MODEL),
        "ffn_w_up": w((N_DENSE, D_MODEL, D_FF), D_MODEL),
        "ffn_w_down": w((N_DENSE, D_FF, D_MODEL), D_FF),
        "router_w": w((N_MOE, D_MODEL, N_EXPERTS), D_MODEL),
        "router_b": 0.01 * jax.random.normal(next(ks), (N_MOE, N_EXPERTS), f32),
        "moe_w_gate": w((N_MOE, N_EXPERTS, D_MODEL, MOE_FF), D_MODEL),
        "moe_w_up": w((N_MOE, N_EXPERTS, D_MODEL, MOE_FF), D_MODEL),
        "moe_w_down": w((N_MOE, N_EXPERTS, MOE_FF, D_MODEL), MOE_FF),
        "ple_w_proj": w((DEPTH, PLE_DIM, D_MODEL), PLE_DIM),
        "ple_w_gate": w((DEPTH, D_MODEL, D_MODEL), D_MODEL),
        "ple_post_g": gain((DEPTH, D_MODEL)),
    }

def reference(x, p, w_in, a_qa_g, a_kva_g, a_w_uq, a_w_ukv, b_q_g, b_k_g, d_sink, w_branch, w_out,
              mix_pre_g, mix_post_g, ffn_pre_g, ffn_post_g, ffn_w_gate, ffn_w_up, ffn_w_down,
              router_w, router_b, moe_w_gate, moe_w_up, moe_w_down, ple_w_proj, ple_w_gate, ple_post_g):
    seq = x.shape[1]
    rows = seq // GRID_W
    pos = jnp.arange(seq, dtype=jnp.int32)
    row_idx = jnp.repeat(jnp.arange(rows, dtype=jnp.int32), GRID_W)
    col_idx = jnp.tile(jnp.arange(GRID_W, dtype=jnp.int32), rows)
    tabs = (rope_tables(pos, A_ROPE), rope_tables(row_idx, HEAD_DIM // 2),
            rope_tables(col_idx, HEAD_DIM // 2), rope_tables(pos, HEAD_DIM))

    for i in range(DEPTH):
        h = rms_norm(x, mix_pre_g[i])
        mix = token_mixers(h, tabs, w_in[i], a_qa_g[i], a_kva_g[i], a_w_uq[i], a_w_ukv[i],
                           b_q_g[i], b_k_g[i], d_sink[i], w_branch[i], w_out[i])
        x = x + rms_norm(mix, mix_post_g[i])

        h = rms_norm(x, ffn_pre_g[i])
        j = i // 2
        if i % 2 == 0:
            f = swiglu(h, ffn_w_gate[j], ffn_w_up[j], ffn_w_down[j])
        else:
            f = moe_swiglu(h, router_w[j], router_b[j], moe_w_gate[j], moe_w_up[j], moe_w_down[j])
        x = x + rms_norm(f, ffn_post_g[i])

        gate = jax.nn.sigmoid((x @ ple_w_gate[i]).astype(jnp.float32)).astype(x.dtype)
        e = (p[i] @ ple_w_proj[i]) * gate
        x = x + rms_norm(e, ple_post_g[i])
    return x


_drawn_inputs = setup_inputs


def setup_inputs(seed=0):
    import zlib

    import numpy as np

    out = dict(_drawn_inputs(seed))
    spreads = {}
    factors = {'d_sink': 3.395, 'router_b': 8.0}
    for name, (base, spread) in spreads.items():
        noise = np.random.default_rng([zlib.crc32(name.encode()), seed]).standard_normal(out[name].shape)
        drawn = base * np.exp(spread * noise) if base else spread * noise
        out[name] = __import__('jax').numpy.asarray(drawn.astype(out[name].dtype))
    for name, factor in factors.items():
        out[name] = (out[name] * factor).astype(out[name].dtype)
    return out
```

```python
from contextlib import ExitStack

import numpy as np

import concourse.bass as bass
from concourse import mybir

ALU = mybir.AluOpType
ACT = mybir.ActivationFunctionType
AX = mybir.AxisListType
F32 = mybir.dt.float32
I32 = mybir.dt.int32

P = 128
D_MODEL, SEQ, DEPTH = 1024, 256, 2
NT = SEQ // P
NK = D_MODEL // P
HD = 64
GRID_W, ROPE_THETA = 64, 10000.0
EPS, MASKED = 1e-6, -1e30
A_Q_RANK, A_KV_RANK, A_ROPE, A_NOPE, A_HEADS = 256, 128, 32, 64, 4
A_QK = A_NOPE + A_ROPE
PATTERNS = ((128, 1), (512, 4), (2048, 16))
D_HALF_WINDOW = 128
A0 = 0
B0 = A_Q_RANK + A_KV_RANK + A_ROPE
C0 = B0 + 8 * HD
D0 = C0 + len(PATTERNS) * 12 * HD
GATE0 = D0 + 8 * HD
D_FF, MOE_FF, N_EXPERTS = 4096, 3584, 8
CAP = P
PLE_DIM = 256

RING = 6
SLOT = 2048
CW = SLOT // NK

CONST_FIELDS = (("ident", P), ("upper", P), ("ones", P), ("iota", P), ("iota8", NT * 8),
                ("mask", 4 * NT * SEQ), ("full", 2 * NT * HD), ("axial", 2 * NT * HD), ("rope_a", 2 * NT * A_ROPE))
CONST_AT, _n = {}, 0
for _name, _w in CONST_FIELDS:
    CONST_AT[_name] = _n
    _n += _w
CONST_W = _n


def constants():
    c = np.zeros((P, CONST_W), np.float32)

    def put(name, a):
        c[:, CONST_AT[name]:CONST_AT[name] + a.reshape(P, -1).shape[1]] = a.reshape(P, -1)

    p = np.arange(P)
    put("ident", np.eye(P, dtype=np.float32))
    put("upper", (p[:, None] < p[None, :]).astype(np.float32))
    put("ones", np.ones((P, P), np.float32))
    put("iota", np.broadcast_to(p.astype(np.float32), (P, P)))
    put("iota8", np.broadcast_to(np.tile(np.arange(8, dtype=np.float32), NT), (P, NT * 8)))
    q = (np.arange(NT)[None, :] * P + p[:, None])[:, :, None]
    k = np.arange(SEQ)[None, None, :]
    masks = []
    for window, dil in PATTERNS:
        masks.append((q % dil == k % dil) & (np.abs(q - k) <= window // 2))
    masks.append(np.abs(q - k) <= D_HALF_WINDOW)
    put("mask", np.stack([np.where(m, 0.0, MASKED) for m in masks], 1).astype(np.float32))

    def table(pos, dim):
        half = dim // 2
        inv = np.power(np.float32(ROPE_THETA), -np.arange(half, dtype=np.float32) / np.float32(half))
        ang = pos.astype(np.float32)[..., None] * inv.astype(np.float32)
        cos, sin = np.cos(ang.astype(np.float64)), np.sin(ang.astype(np.float64))
        return np.concatenate([cos, cos], -1), np.concatenate([-sin, sin], -1)

    pos = np.arange(NT)[None, :] * P + p[:, None]
    put("full", np.stack(table(pos, HD), 1).astype(np.float32))
    row, col = table(pos // GRID_W, HD // 2), table(pos % GRID_W, HD // 2)
    put("axial", np.stack([np.concatenate([row[i], col[i]], -1) for i in range(2)], 1).astype(np.float32))
    put("rope_a", np.stack(table(pos, A_ROPE), 1).astype(np.float32))
    return c


BRANCH_ORDER = "BADC"
BRANCH_ID = {"A": 0, "B": 1, "C": 2, "D": 3}
Z_SLOTS = {"B": [(B0, 256), (B0 + 256, 256)], "A": [(A0, 256), (A0 + 256, 160)],
           "D": [(D0, 256), (D0 + 256, 256)], "C": [(C0 + 256 * i, 256) for i in range(9)]}


def mixer_steps():
    steps = [("z", s) for b in "BAD" for s in Z_SLOTS[b]]
    steps += [("norm_b",), ("rope", "Bq"), ("rope", "Bk"), ("swap", "Bq"), ("swap", "Bk"),
              ("norm_a",), ("swap", "An")]
    late = {
        ("B", 0): [("z", s) for s in Z_SLOTS["C"][0:2]],
        ("B", 1): [("project_a",), ("z", Z_SLOTS["C"][2]), ("z", Z_SLOTS["C"][3])],
        ("B", 2): [("z", s) for s in Z_SLOTS["C"][4:6]],
        ("B", 3): [("z", s) for s in Z_SLOTS["C"][6:9]],
    }
    before = {
        "A": [("rope", "Aq"), ("rope", "Ak"), ("swap", "Aq"), ("swap", "Ak")],
        "D": [("rope", "Dq"), ("rope", "Dk"), ("swap", "Dq"), ("swap", "Dk")],
        "C": [(kind, f"C{g}{w}") for g in range(3) for w in "qk" for kind in ("rope", "swap")],
    }
    job = fill = 0
    for n, b in enumerate(BRANCH_ORDER):
        steps += before.get(b, [])
        for h in range(4):
            filler = late[(b, h)] if n == 0 else [("fill", fill), ("fill", fill + 1)]
            if n:
                fill += 2
            steps += [("score", job, b, h)] + filler[:-1] + [("turn", job, b, h)] + filler[-1:] + [("pv", job, b, h)]
            job += 1
    steps += [("fill", u) for u in range(fill, 32)]
    return steps


MIXER = mixer_steps()
ROPES = [s[1] for s in MIXER if s[0] == "rope"]
NSETS = {"A": 1, "B": 1, "C": 3, "D": 1}
JOBS = [(s[2], s[3]) for s in MIXER if s[0] == "score"]
SET0 = [sum(NSETS[b] for b, _ in JOBS[:j]) for j in range(len(JOBS) + 1)]
SETS = SET0[-1]
UNITS = 32
STAGED = [s[1] for s in MIXER if s[0] == "rope" or s == ("swap", "An")]
STATS = 14
ST_PRE, ST_A, ST_POST, ST_FPRE, ST_FPOST, ST_PLE = 0, 2, 6, 8, 10, 12


def exchange_uses():
    uses = []

    def add(layer, *name):
        uses.append((layer,) + name)

    for layer in range(DEPTH):
        for t in range(NT):
            for b in range(2):
                add(layer, "pre", t, b)
        for s in MIXER:
            if s[0] == "z":
                add(layer, "z", s[1][0])
            elif s[0] == "swap":
                for i in range(2 if s[1] in ("Aq", "Ak", "An") else 1):
                    add(layer, "swap", s[1], i)
            elif s[0] == "project_a":
                for t in range(NT):
                    add(layer, "qa", t)
                    add(layer, "kva", t)
            elif s[0] == "turn":
                for g in range(NSETS[s[2]]):
                    add(layer, "turn", s[1], g)
        for t in range(NT):
            for b in range(2):
                add(layer, "fpre", t, b)
        if layer % 2:
            add(layer, "logits")
            add(layer, "rank")
            for u in dispatch_uses():
                add(layer, *u)
        for t in range(NT):
            for b in range(2):
                add(layer, "xt", t, b)
        add(layer, "pt")
    return {u: n for n, u in enumerate(uses)}


def dispatch_uses():
    return [("gcol",)] + [("spread", i) for i in range(4)] + [("gather", e, b) for e in range(8) for b in range(2)]


USE = exchange_uses()
DISPATCH = {u: n for n, u in enumerate(dispatch_uses())}
EXCHANGE = 3


class Count:

    def __init__(self, sem, at=0):
        self.sem, self.at = sem, at

    def up(self, ins):
        ins.then_inc(self.sem, 1)
        self.at = self.at + 1

    def wait(self, eng):
        eng.wait_ge(self.sem, self.at)


def X_COUNT(layer, which, t):
    return NT * (3 * layer + which) + t + 1


def PARAMS(layer):
    return 16 * (11 * (layer + 1) + 3)


def wait_from(eng, sem, value):
    if not isinstance(value, int) or value > 0:
        eng.wait_ge(sem, value)


class FeedForward:

    def __init__(self, gu_ready, silu_ready, hidden_ready, down_done, before):
        self.gu_ready, self.silu_ready, self.hidden_ready, self.down_done = gu_ready, silu_ready, hidden_ready, down_done
        self.before = before


def ring_plan():
    plan, at, loops = {}, 0, {}
    for layer in range(DEPTH):
        z = [s[1] for s in MIXER if s[0] == "z"]
        seen = 0
        for s in MIXER:
            if s[0] == "z":
                plan[at] = (layer, "z") + s[1]
                at += 1
            if s[0] == "fill" and s[1] % 8 == 0:
                b = BRANCH_ID[BRANCH_ORDER[s[1] // 8]]
                for i in range(4):
                    plan[at] = (layer, "gate", b, i)
                    at += 1
                plan[at] = (layer, "branch", b)
                at += 1
        for i in range(4):
            plan[at] = (layer, "out", i)
            at += 1
        loops[layer] = at
        at += (D_FF if layer % 2 == 0 else N_EXPERTS * MOE_FF) // CW * 3
        plan[at] = (layer, "proj")
        at += 1
        for i in range(4):
            plan[at] = (layer, "ple", i)
            at += 1
    return plan, loops, at


PLAN, LOOPS, _ = ring_plan()
WHERE = {v: k for k, v in PLAN.items()}
FF_BODIES = {0: D_FF // (2 * CW), 1: MOE_FF // (2 * CW)}
FF_BLOCKS = 2 * CW // P
N_FFN_BLOCKS = D_FF // P
N_MOE_BLOCKS = MOE_FF // P


def trunk(nc, args):
    (x_in, p_in, w_in, a_qa_g, a_kva_g, a_w_uq, a_w_ukv, b_q_g, b_k_g, d_sink, w_branch, w_out,
     mix_pre_g, mix_post_g, ffn_pre_g, ffn_post_g, ffn_w_gate, ffn_w_up, ffn_w_down,
     router_w, router_b, moe_w_gate, moe_w_up, moe_w_down, ple_w_proj, ple_w_gate, ple_post_g,
     const_in, out) = args
    ctx = ExitStack()
    with ctx:
        def sb(name, shape, dt=F32):
            return ctx.enter_context(nc.sbuf_tensor(name, shape, dt))

        def sem(name):
            return ctx.enter_context(nc.semaphore(name))

        ring = sb("ring", [P, RING, SLOT])
        x = sb("x", [P, NT, D_MODEL])
        xn = sb("xn", [P, NT, D_MODEL])
        hT = sb("hT", [P, NK, SEQ])
        work = sb("work", [P, 20288])
        kz = sb("kz", [P, 14, SEQ])
        staged = sb("staged", [P, 2, NT, 384])
        rot = sb("rot", [P, 2, 384])
        cn = sb("cn", [P, CONST_W])
        gain = sb("gain", [P, 2, D_MODEL])
        gain_a = sb("gain_a", [P, 384])
        gain_b = sb("gain_b", [P, 6, HD])
        sink = sb("sink", [P, 4])
        w_uq = sb("w_uq", [P, 2, 384])
        w_ukv = sb("w_ukv", [P, 512])
        rtr_w = sb("rtr_w", [P, NK, 8])
        rtr_b = sb("rtr_b", [P, NT, 8])
        sumsq = sb("sumsq", [P, DEPTH * STATS])
        var = sb("var", [P, DEPTH * STATS])
        rstd = sb("rstd", [P, DEPTH * STATS])
        sumsq_b = sb("sumsq_b", [P, NT, 6])
        var_b = sb("var_b", [P, NT, 6])
        rstd_b = sb("rstd_b", [P, NT, 6])
        minus_half = sb("minus_half", [P, NT * 6])
        peak = sb("peak", [P, 2, NT, 3])
        top = sb("top", [P, 2, NT])
        bias = sb("bias", [P, 2, NT])
        total = sb("total", [P, 2, NT])
        sunk = sb("sunk", [P, 2, NT])
        inv = sb("inv", [P, 2, NT])
        egate = sb("egate", [P, 2, SEQ])

        def carve():
            at = [0]

            def take(n):
                at[0] += n
                assert at[0] <= 20288
                return work[:, at[0] - n:at[0]]
            return take

        take = carve()
        z = take(NT * GATE0).rearrange("p (t c) -> p t c", t=NT)
        qT = take(8 * SEQ).rearrange("p (b s) -> p b s", b=8)
        qaT = take(4 * SEQ).rearrange("p (b s) -> p b s", b=4)
        kaT = take(4 * SEQ).rearrange("p (b s) -> p b s", b=4)
        probs = take(2 * NT * 3 * SEQ).rearrange("p (j t g s) -> p j t g s", j=2, t=NT, g=3)
        NPT = 3
        pT = take(NPT * 2 * SEQ).rearrange("p (n k s) -> p n k s", n=NPT, k=NT)
        kva = take(NT * 512).rearrange("p (t c) -> p t c", t=NT)
        lowT = take(3 * SEQ).rearrange("p (b s) -> p b s", b=3)
        oT = take(NK * SEQ)
        post_tmp = oT.rearrange("p (t d) -> p t d", t=NT)
        oT = oT.rearrange("p (b s) -> p b s", b=NK)
        qa_sb = xn[:, :, 0:384]
        mergedT = xn[:, :, :].rearrange("p t (b s) -> p (t b) s", s=SEQ)

        take = carve()
        p_sb = take(NT * PLE_DIM).rearrange("p (t c) -> p t c", t=NT)
        pleT = take(2 * SEQ).rearrange("p (k s) -> p k s", k=2)
        hidden = take(4 * SEQ).rearrange("p (n s) -> p n s", n=4)
        silu = take(4 * SEQ).rearrange("p (n s) -> p n s", n=4)
        xg = take(N_EXPERTS * D_MODEL).rearrange("p (e m) -> p e m", e=N_EXPERTS)
        junk = xg[:, 0, :]
        pick = take(NT * 8 * CAP).rearrange("p (t e n) -> p t e n", t=NT, e=8)
        spread = take(8 * SEQ).rearrange("p (e s) -> p e s", e=8)
        ys = take(D_MODEL)
        fsum = take(NT * D_MODEL).rearrange("p (t d) -> p t d", t=NT)
        cur_x = take(D_MODEL).rearrange("p (k n) -> p k n", k=NK)
        cur_spread = take(SEQ)
        lg = take(NT * 8).rearrange("p (t e) -> p t e", t=NT)
        eq = take(NT * 8).rearrange("p (t e) -> p t e", t=NT)
        idx = take(NT * 8).rearrange("p (t e) -> p t e", t=NT)
        first = take(NT * 8).rearrange("p (t e) -> p t e", t=NT)
        second = take(NT * 8).rearrange("p (t e) -> p t e", t=NT)
        chosen = take(NT * 8).rearrange("p (t e) -> p t e", t=NT)
        weight = take(NT * 8).rearrange("p (t e) -> p t e", t=NT)
        rank = take(3 * 8).rearrange("p (t e) -> p t e", t=3)
        gcol = take(8)
        cur_g = take(1)
        rt = take(NT * 8).rearrange("p (n t) -> p n t", t=NT)
        overflow_f = take(8)
        overflow = sb("overflow", [P, 1], I32)

        ps = ctx.enter_context(nc.psum_tensor("ps", [P, 8, 512], F32))
        O_BANK = ps[:, 3, 0:SEQ]

        def acc(t):
            return ps[:, 4 + 2 * t:6 + 2 * t, :]

        def const(name, n):
            return cn[:, CONST_AT[name]:CONST_AT[name] + n]

        ident, upper, ones = const("ident", P), const("upper", P), const("ones", P)
        iota = const("iota", P)
        iota8 = const("iota8", NT * 8).rearrange("p (t e) -> p t e", t=NT)
        mask = const("mask", 4 * NT * SEQ).rearrange("p (m t s) -> p m t s", m=4, t=NT)
        tab = {"full": const("full", 2 * NT * HD).rearrange("p (f t d) -> p f t d", f=2, t=NT),
               "axial": const("axial", 2 * NT * HD).rearrange("p (f t d) -> p f t d", f=2, t=NT),
               "a": const("rope_a", 2 * NT * A_ROPE).rearrange("p (f t d) -> p f t d", f=2, t=NT)}

        const_in_s, x_in_s = sem("const_loaded"), sem("x_loaded")
        slot_in = [sem(f"slot{i}_loaded") for i in range(RING)]
        gain_in = [sem(f"gain{i}_loaded") for i in range(2)]
        params_in, p_loaded = sem("params_loaded"), sem("p_loaded")
        kz_zero = sem("kz_zeroed")
        ex_ready, ex_done = sem("exchange_ready"), sem("exchange_emptied")
        sq_done, rstd_done = sem("sumsq_done"), sem("rstd_done")
        sqb_done, rstdb_done = sem("sumsq_b_done"), sem("rstd_b_done")
        xn_done, x_done = sem("normed_ready"), sem("residual_ready")
        staged_done = sem("staged_ready")
        qa_read = sem("a_projections_read")
        scored, score_read = sem("scores_ready"), sem("scores_read")
        bias_done, exp_done, prob_done = sem("bias_ready"), sem("exp_ready"), sem("probs_ready")
        pv_done, o_done = sem("pv_done"), sem("o_emptied")
        unit_ready, egate_done, unit_done = sem("unit_ready"), sem("gate_exp_ready"), sem("unit_merged")
        mix_done = sem("mix_ready")
        ple_done, ple_exp, ple_prod = sem("ple_ready"), sem("ple_gate_exp_ready"), sem("ple_product_ready")
        route_exp_in, route_exp, routed = sem("route_difference_ready"), sem("route_exp_ready"), sem("routed")
        overflow_ready, moe_done = sem("overflow_known"), sem("moe_done")
        dve_step, act_step, pool_step = sem("vector_step"), sem("scalar_step"), sem("pool_step")
        stored = sem("stored")

        def ff_sems(tag, before):
            return FeedForward(sem(f"{tag}_gate_up_ready"), sem(f"{tag}_silu_ready"), sem(f"{tag}_hidden_ready"),
                               sem(f"{tag}_down_done"), before)

        ffn = ff_sems("ff", 0)
        moe = FeedForward(ffn.gu_ready, ffn.silu_ready, ffn.hidden_ready, ffn.down_done, N_FFN_BLOCKS)

        class Pass:

            def __init__(self, tag, ff, ex, ex0, slots, pos0, loads0):
                self.ff, self.ex_ready, self.ex_done, self.ex0 = ff, ex[0], ex[1], ex0
                self.slots, self.pos0, self.loads0 = slots, pos0, loads0
                self.picked = sem(f"{tag}_pick_ready")
                self.cur_x_ready, self.cur_s_ready = sem(f"{tag}_tokens_ready"), sem(f"{tag}_spread_ready")
                self.ys_act, self.ys_dve = sem(f"{tag}_y_low_ready"), sem(f"{tag}_y_high_ready")
                self.back, self.added = sem(f"{tag}_scatter_ready"), sem(f"{tag}_scatter_added")

        main_pass = Pass("moe", moe, (ex_ready, ex_done), USE[(1, "gcol")], slot_in, LOOPS[1],
                         [(LOOPS[1] + j) // RING for j in range(RING)])
        over = FeedForward(*[sem(f"over_{n}") for n in ("gate_up_ready", "silu_ready", "hidden_ready", "down_done")], 4)
        over_pass = Pass("over", over, (sem("over_exchange_ready"), sem("over_exchange_emptied")), 0,
                         [sem(f"over_slot{i}_loaded") for i in range(RING)], LOOPS[1], [0] * RING)
        over_ranked = sem("over_ranks_ready")

        def slot_of(pos):
            return ring[:, pos % RING, :]

        def loaded(eng, pos):
            eng.wait_ge(slot_in[pos % RING], 16 * (pos // RING + 1))

        def released(pos):
            what = PLAN[pos]
            layer, kind = what[0], what[1]
            if kind == "z":
                return ex_ready, USE[(layer, "z", what[2])] + 1
            if kind == "gate":
                order = BRANCH_ORDER.index("ABCD"[what[2]])
                return unit_ready, UNITS * layer + 8 * order + 2 * what[3] + 2
            if kind == "branch":
                return unit_ready, UNITS * layer + 8 * BRANCH_ORDER.index("ABCD"[what[2]]) + 8
            if kind == "out":
                return mix_done, NT * (layer + 1)
            return ple_done, NT * (layer + 1)

        def blocks_before(layer):
            return 0 if layer == 0 else N_FFN_BLOCKS

        def blocks_after(layer):
            return N_FFN_BLOCKS if layer == 0 else N_FFN_BLOCKS + N_EXPERTS * N_MOE_BLOCKS

        block = ctx.enter_context(nc.Block())

        @block.sync
        def _(sp):
            w_in_v = [w_in[l].rearrange("(k p) c -> p k c", p=P) for l in range(DEPTH)]

            def load(pos):
                layer, kind, *r = PLAN[pos]
                dst, wide = slot_of(pos), None
                if kind == "z":
                    c, w = r
                    dst = dst.rearrange("p (k c) -> p k c", k=NK)[:, :, 0:w]
                    src = w_in_v[layer][:, :, c:c + w]
                elif kind == "gate":
                    c = GATE0 + r[0] * D_MODEL + r[1] * CW
                    dst = dst.rearrange("p (k c) -> p k c", k=NK)
                    src = w_in_v[layer][:, :, c:c + CW]
                else:
                    dst = dst.rearrange("p (k c) -> p k c", k=2)
                    if kind == "branch":
                        src = w_branch[layer, r[0]].rearrange("(k p) c -> p k c", p=P)
                    elif kind == "out":
                        src = w_out[layer].rearrange("(i k p) c -> i p k c", p=P, k=2)[r[0]]
                    elif kind == "proj":
                        src = ple_w_proj[layer].rearrange("(k p) c -> p k c", p=P)
                    else:
                        src = ple_w_gate[layer].rearrange("(i k p) c -> i p k c", p=P, k=2)[r[0]]
                prior = pos - RING
                if prior >= 0:
                    if prior in PLAN:
                        sp.wait_ge(*released(prior))
                    else:
                        looped = 0 if prior < LOOPS[1] else 1
                        sp.wait_ge(ffn.gu_ready, blocks_after(looped))
                        sp.wait_ge(ffn.down_done, blocks_after(looped))
                sp.dma_start(dst, src).then_inc(slot_in[pos % RING], 16)

            def ff_loads(views, chunk, pos0, slots, ff, block0, prior=None):
                for i in range(2):
                    for j in range(3):
                        pos = pos0 + 3 * i + j
                        if prior is not None:
                            if prior + 3 * i + j >= 0:
                                sp.wait_ge(*released(prior + 3 * i + j))
                        elif j < 2:
                            sp.wait_ge(ff.gu_ready, block0 - FF_BLOCKS + 2 * (i + 1))
                        else:
                            sp.wait_ge(ff.down_done, block0 - FF_BLOCKS + 2 * (i + 1))
                        dst = ring[:, pos % RING, :].rearrange("p (k c) -> p k c", k=NK if j < 2 else 2)
                        sp.dma_start(dst, views[j][chunk + i]).then_inc(slots[pos % RING], 16)

            def up_gate_view(w):
                return w.rearrange("(k p) (c f) -> c p k f", p=P, f=CW)

            def moe_view(w):
                return w.rearrange("e (k p) (c f) -> e c p k f", p=P, f=CW)

            def expert_views(e):
                return [moe_view(moe_w_up[0])[e], moe_view(moe_w_gate[0])[e],
                        moe_w_down[0].rearrange("e (c k p) d -> e c p k d", p=P, k=2)[e]]

            sp.dma_start(cn[:, :], const_in).then_inc(const_in_s, 16)
            sp.dma_start(x[:, :, :], x_in[0].rearrange("(t p) d -> p t d", p=P)).then_inc(x_in_s, 16)
            n = FF_BODIES[1]
            for layer in range(DEPTH):
                start = 0 if layer == 0 else WHERE[(0, "ple", 3)] + 1
                for pos in range(start, LOOPS[layer]):
                    load(pos)
                pos0 = LOOPS[layer]
                if layer == 0:
                    views = [up_gate_view(ffn_w_up[0]), up_gate_view(ffn_w_gate[0]),
                             ffn_w_down[0].rearrange("(c k p) d -> c p k d", p=P, k=2)]
                    ff_loads(views, 0, pos0, slot_in, ffn, 0, prior=pos0 - RING)
                    with sp.Fori(1, FF_BODIES[0]) as c:
                        ff_loads(views, 2 * c, pos0, slot_in, ffn, FF_BLOCKS * c)
                else:
                    before = moe.before
                    ff_loads(expert_views(0), 0, pos0, slot_in, moe, before, prior=pos0 - RING)
                    with sp.Fori(1, n) as c:
                        ff_loads(expert_views(0), 2 * c, pos0, slot_in, moe, FF_BLOCKS * c + before)
                    with sp.Fori(1, N_EXPERTS) as e:
                        with sp.Fori(0, n) as c:
                            ff_loads(expert_views(e), 2 * c, pos0, slot_in, moe, (e * n + c) * FF_BLOCKS + before)
                    sp.wait_ge(overflow_ready, 1)
                    more = sp.value_load(overflow[0:1, 0:1], min_val=0, max_val=1)
                    with sp.If(more > 0):
                        sp.wait_ge(ffn.gu_ready, blocks_after(1))
                        sp.wait_ge(ffn.down_done, blocks_after(1))
                        with sp.Fori(0, N_EXPERTS) as e:
                            with sp.Fori(0, n) as c:
                                ff_loads(expert_views(e), 2 * c, over_pass.pos0, over_pass.slots, over,
                                         (e * n + c) * FF_BLOCKS + over.before)
                        total_blocks = over.before + N_EXPERTS * N_MOE_BLOCKS
                        sp.wait_ge(over.gu_ready, total_blocks)
                        sp.wait_ge(over.down_done, total_blocks)
                for pos in range(WHERE[(layer, "proj")], WHERE[(layer, "ple", 3)] + 1):
                    load(pos)
            out_v = out[0].rearrange("(t p) d -> p t d", p=P)
            for t in range(NT):
                sp.wait_ge(x_done, X_COUNT(DEPTH - 1, 2, t))
                sp.dma_start(out_v[:, t, :], x[:, t, :]).then_inc(stored, 16)
            sp.wait_ge(stored, 16 * NT)

        @block.gpsimd
        def _(pool):
            step = Count(pool_step)
            gains = [g for l in range(DEPTH) for g in (mix_pre_g[l], mix_post_g[l], ffn_pre_g[l], ffn_post_g[l], ple_post_g[l])]

            def load_gain(n):
                if n >= len(gains):
                    return
                if n >= 2:
                    last_layer, last = divmod(n - 2, 5)
                    if last in (0, 2):
                        pool.wait_ge(xn_done, 2 * NT * last_layer + NT * (last // 2) + NT)
                    else:
                        pool.wait_ge(x_done, X_COUNT(last_layer, {1: 0, 3: 1, 4: 2}[last], NT - 1))
                pool.dma_start(gain[:, n % 2, :], gains[n].partition_broadcast(P)).then_inc(gain_in[n % 2], 16)

            def load_params(layer):
                if layer:
                    pool.wait_ge(staged_done, len(STAGED) * layer)
                    pool.wait_ge(ex_done, USE[(layer - 1, "kva", NT - 1)] + 1)
                    pool.wait_ge(prob_done, len(JOBS) * layer)
                    pool.wait_ge(exp_done, len(JOBS) * layer)
                pool.dma_start(gain_a[:, 0:256], a_qa_g[layer].partition_broadcast(P)).then_inc(params_in, 16)
                pool.dma_start(gain_a[:, 256:384], a_kva_g[layer].partition_broadcast(P)).then_inc(params_in, 16)
                for h in range(6):
                    g = b_q_g if h < 4 else b_k_g
                    pool.dma_start(gain_b[:, h, :], g[layer].partition_broadcast(P)).then_inc(params_in, 16)
                pool.dma_start(sink[:, :], d_sink[layer].partition_broadcast(P)).then_inc(params_in, 16)
                pool.dma_start(w_uq[:, :, :], a_w_uq[layer].rearrange("(k p) c -> p k c", p=P)).then_inc(params_in, 16)
                pool.dma_start(w_ukv[:, :], a_w_ukv[layer]).then_inc(params_in, 16)

            def stat(n, width):
                pool.wait_ge(sq_done, n + 1)
                step.up(nc.gpsimd.tensor_scalar(var[:, n:n + 1], sumsq[:, n:n + 1], 1.0 / width, EPS, ALU.mult, ALU.add))
                step.wait(pool)
                nc.gpsimd.tensor_tensor(rstd[:, n:n + 1], var[:, n:n + 1], minus_half[:, 0:1], ALU.pow).then_inc(rstd_done, 1)

            load_gain(0)
            load_gain(1)
            load_params(0)
            nc.gpsimd.memset(minus_half[:, :], -0.5).then_inc(pool_step, 1)
            step.at += 1
            nc.gpsimd.memset(kz[:, :, :], 0.0).then_inc(kz_zero, 1)
            step.wait(pool)
            for t in range(NT):
                pool.dma_start(rtr_b[:, t, :], router_b[0].partition_broadcast(P)).then_inc(params_in, 16)
            pool.dma_start(rtr_w[:, :, :], router_w[0].rearrange("(k p) e -> p k e", p=P)).then_inc(params_in, 16)
            for layer in range(DEPTH):
                s0 = STATS * layer
                for t in range(NT):
                    stat(s0 + ST_PRE + t, D_MODEL)
                load_gain(5 * layer + 2)
                for s in MIXER:
                    if s[0] == "norm_b":
                        pool.wait_ge(sqb_done, layer + 1)
                        fl = lambda a: a[:, :, :].rearrange("p t h -> p (t h)")
                        step.up(nc.gpsimd.tensor_scalar(fl(var_b), fl(sumsq_b), 1.0 / HD, EPS, ALU.mult, ALU.add))
                        step.wait(pool)
                        nc.gpsimd.tensor_tensor(fl(rstd_b), fl(var_b), minus_half[:, :], ALU.pow).then_inc(rstdb_done, 1)
                    if s[0] == "norm_a":
                        for i, width in enumerate((A_Q_RANK, A_KV_RANK)):
                            for t in range(NT):
                                stat(s0 + ST_A + NT * i + t, width)
                for t in range(NT):
                    stat(s0 + ST_POST + t, D_MODEL)
                load_gain(5 * layer + 3)
                if layer + 1 < DEPTH:
                    load_params(layer + 1)
                for t in range(NT):
                    stat(s0 + ST_FPRE + t, D_MODEL)
                load_gain(5 * layer + 4)
                pool.wait_ge(mix_done, NT * (layer + 1))
                pool.wait_ge(x_done, X_COUNT(layer, 0, NT - 1))
                pool.dma_start(p_sb, p_in[layer, 0].rearrange("(t p) c -> p t c", p=P)).then_inc(p_loaded, 16)
                for t in range(NT):
                    stat(s0 + ST_FPOST + t, D_MODEL)
                load_gain(5 * layer + 5)
                for t in range(NT):
                    stat(s0 + ST_PLE + t, D_MODEL)
                load_gain(5 * layer + 6)

        @block.tensor
        def _(pe):
            mm = nc.tensor.matmul

            def bank_for(layer, *name):
                n = USE[(layer,) + name]
                if n >= EXCHANGE:
                    pe.wait_ge(ex_done, n - EXCHANGE + 1)
                return ps[:, n % EXCHANGE, :]

            def emptied(layer, *name):
                pe.wait_ge(ex_done, USE[(layer,) + name] + 1)

            def turn_tile(layer, kind, src, t):
                for b in range(2):
                    bank = bank_for(layer, kind, t, b)
                    for i in range(4):
                        c = (4 * b + i) * P
                        m = nc.tensor.transpose(bank[:, i * P:(i + 1) * P], src[:, t, c:c + P], ident)
                    m.then_inc(ex_ready, 1)

            def swap(layer, item):
                pe.wait_ge(staged_done, len(STAGED) * layer + STAGED.index(item) + 1)
                r = staged[:, (len(STAGED) * layer + STAGED.index(item)) % 2]
                if item in ("Aq", "Ak"):
                    for u in range(2):
                        bank = bank_for(layer, "swap", item, u)
                        for h in range(2):
                            for t in range(NT):
                                c = (2 * u + h) * A_QK
                                m = nc.tensor.transpose(bank[0:A_QK, h * SEQ + t * P:h * SEQ + (t + 1) * P],
                                                        r[:, t, c:c + A_QK], ident)
                        m.then_inc(ex_ready, 1)
                    return
                if item == "An":
                    groups = [[0, 1], [2]]
                else:
                    groups = [[0]] if item in ("Bk", "Dk") else [[0, 1]]
                for u, g in enumerate(groups):
                    bank = bank_for(layer, "swap", item, u)
                    for i, b in enumerate(g):
                        for t in range(NT):
                            m = nc.tensor.transpose(bank[:, i * SEQ + t * P:i * SEQ + (t + 1) * P],
                                                    r[:, t, b * P:(b + 1) * P], ident)
                    m.then_inc(ex_ready, 1)

            def score_operands(b, h, g):
                if b == "A":
                    return qaT[0:A_QK, h, :], kaT[0:A_QK, h, :]
                if b in "BD":
                    return qT[:, h % 2, :], kz[:, h // 2, :]
                return qT[:, 2 + 2 * g + h // 2, :], kz[:, 2 + 4 * g + h, :]

            def values(b, h, g, kt):
                if b == "A":
                    return kva[:, kt, h * P + A_NOPE:(h + 1) * P]
                c = {"B": B0 + 6 * HD + (h // 2) * HD, "D": D0 + 6 * HD + (h // 2) * HD,
                     "C": C0 + g * 12 * HD + 8 * HD + h * HD}[b]
                return z[:, kt, c:c + HD]

            def feed_forward(ff, slots, pos0, loads0, body, block0, rhs, out_of, tiles, more=None):
                def arrived(j):
                    pe.wait_ge(slots[(pos0 + j) % RING], (loads0[j] + 1 + body) * 16)

                def gate_up(j):
                    wait_from(pe, ff.hidden_ready, block0 + j - 3)
                    if j % 2 == 0:
                        arrived(3 * (j // 2))
                        arrived(3 * (j // 2) + 1)
                    n = rhs.shape[2]
                    for i in range(2):
                        w = slot_of(pos0 + 3 * (j // 2) + i).rearrange("p (k c) -> p k c", k=NK)
                        for k in range(NK):
                            m = mm(ps[:, j, i * SEQ:i * SEQ + n], w[:, k, (j % 2) * P:(j % 2 + 1) * P],
                                   rhs[:, k, :], start=(k == 0), stop=(k == NK - 1))
                    m.then_inc(ff.gu_ready, 1)

                def down(j, first=False, last=False):
                    pe.wait_ge(ff.hidden_ready, block0 + j + 1)
                    if j in (0, 2):
                        arrived(3 * (j // 2) + 2)
                    jj = j % 4
                    w = slot_of(pos0 + 3 * (jj // 2) + 2).rearrange("p (k c) -> p k c", k=2)
                    for t in range(tiles):
                        for half in range(2):
                            m = mm(out_of(t)[:, half, :], hidden[:, jj, t * P:(t + 1) * P],
                                   w[:, jj % 2, half * 512:(half + 1) * 512], start=first, stop=last)
                    m.then_inc(ff.down_done, 1)

                if more == "end":
                    down(-1, last=True)
                    return
                gate_up(0)
                if more is not None:
                    down(-1)
                gate_up(1)
                down(0, first=more is None)
                gate_up(2)
                down(1)
                gate_up(3)
                down(2)

            def dispatch(ps_, layer=1):
                def use(*name):
                    n = ps_.ex0 + DISPATCH[name]
                    if n >= EXCHANGE:
                        pe.wait_ge(ps_.ex_done, n - EXCHANGE + 1)
                    return ps[:, n % EXCHANGE, :]

                pe.wait_ge(ps_.picked, 1)
                bank = use("gcol")
                for e in range(8):
                    for t in range(NT):
                        m = mm(bank[:, e:e + 1], pick[:, t, e, :], weight[:, t, e:e + 1], start=(t == 0), stop=(t == NT - 1))
                m.then_inc(ps_.ex_ready, 1)
                for i in range(4):
                    bank = use("spread", i)
                    for j in range(2):
                        for t in range(NT):
                            m = nc.tensor.transpose(bank[:, j * SEQ + t * P:j * SEQ + (t + 1) * P], pick[:, t, 2 * i + j, :], ident)
                    m.then_inc(ps_.ex_ready, 1)
                for e in range(8):
                    for b in range(2):
                        bank = use("gather", e, b)
                        for i in range(4):
                            c = (4 * b + i) * P
                            for t in range(NT):
                                m = mm(bank[:, i * P:(i + 1) * P], xn[:, t, c:c + P], pick[:, t, e, :],
                                       start=(t == 0), stop=(t == NT - 1))
                        m.then_inc(ps_.ex_ready, 1)
                pe.wait_ge(ps_.ex_done, ps_.ex0 + len(DISPATCH))

            def experts(ps_):
                n, ff = FF_BODIES[1], ps_.ff
                with pe.Fori(0, N_EXPERTS) as e:
                    pe.wait_ge(ps_.cur_x_ready, e + 1)
                    y = lambda t: acc(0)
                    a = (ff, ps_.slots, ps_.pos0, ps_.loads0)
                    before = e * N_MOE_BLOCKS + ff.before
                    feed_forward(*a, e * n, before, cur_x, y, 1)
                    with pe.Fori(1, n) as c:
                        feed_forward(*a, e * n + c, before + c * FF_BLOCKS, cur_x, y, 1, more="go on")
                    feed_forward(*a, e * n + n, before + N_MOE_BLOCKS, cur_x, y, 1, more="end")
                    pe.wait_ge(ps_.ys_act, e + 1)
                    pe.wait_ge(ps_.ys_dve, e + 1)
                    pe.wait_ge(ps_.cur_s_ready, e + 1)
                    for t in (1, 0):
                        for half in range(2):
                            m = mm(acc(t)[:, half, :], cur_spread[:, t * P:(t + 1) * P],
                                   ys[:, half * 512:(half + 1) * 512], start=True, stop=True)
                        m.then_inc(ps_.back, 1)
                    pe.wait_ge(ps_.added, e * NT + NT)

            pe.wait_ge(const_in_s, 16)
            for layer in range(DEPTH):
                for t in range(NT):
                    pe.wait_ge(xn_done, 2 * NT * layer + t + 1)
                    turn_tile(layer, "pre", xn, t)
                emptied(layer, "pre", NT - 1, 1)
                for s in MIXER:
                    if s[0] == "z":
                        c, w = s[1]
                        pos = WHERE[(layer, "z", c, w)]
                        bank = bank_for(layer, "z", c)
                        loaded(pe, pos)
                        wv = slot_of(pos).rearrange("p (k c) -> p k c", k=NK)
                        for t in range(NT):
                            for k in range(NK):
                                m = mm(bank[:, t * SEQ:t * SEQ + w], hT[:, k, t * P:(t + 1) * P], wv[:, k, 0:w],
                                       start=(k == 0), stop=(k == NK - 1))
                        m.then_inc(ex_ready, 1)
                    elif s[0] == "swap":
                        swap(layer, s[1])
                    elif s[0] == "project_a":
                        emptied(layer, "swap", "An", 1)
                        pe.wait_ge(params_in, PARAMS(layer))
                        for t in range(NT):
                            bank = bank_for(layer, "qa", t)
                            for k in range(2):
                                m = mm(bank[:, 0:384], lowT[:, k, t * P:(t + 1) * P], w_uq[:, k, :], start=(k == 0), stop=(k == 1))
                            m.then_inc(ex_ready, 1)
                            bank = bank_for(layer, "kva", t)
                            mm(bank, lowT[:, 2, t * P:(t + 1) * P], w_ukv[:, :], start=True, stop=True).then_inc(ex_ready, 1)
                    elif s[0] == "score":
                        _, j, b, h = s
                        if h == 0:
                            emptied(layer, "swap", {"A": "Ak", "B": "Bk", "C": "C2k", "D": "Dk"}[b], 1 if b == "A" else 0)
                        for g in range(NSETS[b]):
                            n = SETS * layer + SET0[j] + g
                            if n >= 2:
                                pe.wait_ge(score_read, n - 1)
                            q, k = score_operands(b, h, g)
                            bank = ps[:, 4 + n % 2, :]
                            for t in range(NT):
                                m = mm(bank[:, t * SEQ:(t + 1) * SEQ], q[:, t * P:(t + 1) * P], k, start=True, stop=True)
                            m.then_inc(scored, 1)
                    elif s[0] == "turn":
                        _, j, b, h = s
                        pe.wait_ge(prob_done, len(JOBS) * layer + j + 1)
                        for g in range(NSETS[b]):
                            bank = bank_for(layer, "turn", j, g)
                            for kt in range(NT):
                                for t in range(NT):
                                    m = nc.tensor.transpose(bank[:, kt * SEQ + t * P:kt * SEQ + (t + 1) * P],
                                                            probs[:, j % 2, t, g, kt * P:(kt + 1) * P], ident)
                            m.then_inc(ex_ready, 1)
                    elif s[0] == "pv":
                        _, j, b, h = s
                        if h % 2 == 0:
                            pair = (len(JOBS) * layer + j) // 2
                            wait_from(pe, o_done, pair)
                        for g in range(NSETS[b]):
                            emptied(layer, "turn", j, g)
                            n = SETS * layer + SET0[j] + g
                            for kt in range(NT):
                                m = mm(O_BANK[(h % 2) * HD:(h % 2 + 1) * HD, :], values(b, h, g, kt), pT[:, n % NPT, kt, :],
                                       start=(g == 0 and kt == 0), stop=(g == NSETS[b] - 1 and kt == NT - 1))
                            m.then_inc(pv_done, 1)
                    elif s[0] == "fill":
                        u = s[1]
                        order, c = divmod(u, 8)
                        n = BRANCH_ID[BRANCH_ORDER[order]]
                        wait_from(pe, unit_done, UNITS * layer + u - 1)
                        bank = ps[:, 6 + u % 2, :]
                        pos = WHERE[(layer, "gate", n, c // 2)]
                        loaded(pe, pos)
                        wg = slot_of(pos).rearrange("p (k c) -> p k c", k=NK)
                        for k in range(NK):
                            mm(bank[:, 0:SEQ], wg[:, k, (c % 2) * P:(c % 2 + 1) * P], hT[:, k, :],
                               start=(k == 0), stop=(k == NK - 1))
                        pos = WHERE[(layer, "branch", n)]
                        loaded(pe, pos)
                        pe.wait_ge(o_done, len(JOBS) // 2 * layer + 2 * (order + 1))
                        wb = slot_of(pos).rearrange("p (k c) -> p k c", k=2)
                        for k in range(2):
                            m = mm(bank[:, SEQ:2 * SEQ], wb[:, k, c * P:(c + 1) * P], oT[:, 2 * n + k, :],
                                   start=(k == 0), stop=(k == 1))
                        m.then_inc(unit_ready, 1)
                pe.wait_ge(unit_done, UNITS * (layer + 1))
                for t in range(NT):
                    for i in range(4):
                        pos = WHERE[(layer, "out", i)]
                        loaded(pe, pos)
                        wo = slot_of(pos).rearrange("p (k c) -> p k c", k=2)
                        for k in range(2):
                            for half in range(2):
                                m = mm(acc(t)[:, half, :], mergedT[:, 2 * i + k, t * P:(t + 1) * P],
                                       wo[:, k, half * 512:(half + 1) * 512], start=(i == 0 and k == 0), stop=(i == 3 and k == 1))
                    m.then_inc(mix_done, 1)
                for t in range(NT):
                    pe.wait_ge(xn_done, 2 * NT * layer + NT + t + 1)
                    turn_tile(layer, "fpre", xn, t)
                emptied(layer, "fpre", NT - 1, 1)
                if layer % 2 == 0:
                    a = (ffn, slot_in, LOOPS[0], [(LOOPS[0] + j) // RING for j in range(RING)])
                    feed_forward(*a, 0, 0, hT, acc, NT)
                    with pe.Fori(1, FF_BODIES[0]) as c:
                        feed_forward(*a, c, c * FF_BLOCKS, hT, acc, NT, more="go on")
                    feed_forward(*a, FF_BODIES[0], N_FFN_BLOCKS, hT, acc, NT, more="end")
                else:
                    pe.wait_ge(params_in, PARAMS(layer))
                    bank = bank_for(layer, "logits")
                    for t in range(NT):
                        for k in range(NK):
                            m = mm(bank[:, t * 8:t * 8 + 8], hT[:, k, t * P:(t + 1) * P], rtr_w[:, k, :],
                                   start=(k == 0), stop=(k == NK - 1))
                    m.then_inc(ex_ready, 1)
                    pe.wait_ge(routed, 1)
                    bank = bank_for(layer, "rank")
                    mm(bank[:, 0:8], upper, chosen[:, 0, :], start=True, stop=True)
                    mm(bank[:, 8:16], ones, chosen[:, 0, :], start=True, stop=False)
                    mm(bank[:, 8:16], upper, chosen[:, 1, :], start=False, stop=True)
                    mm(bank[:, 16:24], ones, chosen[:, 0, :], start=True, stop=False)
                    mm(bank[:, 16:24], ones, chosen[:, 1, :], start=False, stop=True).then_inc(ex_ready, 1)
                    dispatch(main_pass)
                    experts(main_pass)
                    pe.wait_ge(overflow_ready, 1)
                    more = pe.value_load(overflow[0:1, 0:1], min_val=0, max_val=1)
                    with pe.If(more > 0):
                        pe.sem_inc(over.gu_ready, 4)
                        pe.sem_inc(over.down_done, 4)
                        dispatch(over_pass)
                        experts(over_pass)
                pe.wait_ge(p_loaded, 16 * (layer + 1))
                for t in range(NT):
                    pe.wait_ge(x_done, X_COUNT(layer, 1, t))
                    turn_tile(layer, "xt", x, t)
                bank = bank_for(layer, "pt")
                for k in range(2):
                    for t in range(NT):
                        m = nc.tensor.transpose(bank[:, k * SEQ + t * P:k * SEQ + (t + 1) * P], p_sb[:, t, k * P:(k + 1) * P], ident)
                m.then_inc(ex_ready, 1)
                emptied(layer, "pt")
                for t in range(NT):
                    pos = WHERE[(layer, "proj")]
                    loaded(pe, pos)
                    wp = slot_of(pos).rearrange("p (k c) -> p k c", k=2)
                    for k in range(2):
                        for half in range(2):
                            mm(ps[:, 2 * t + half, :], pleT[:, k, t * P:(t + 1) * P], wp[:, k, half * 512:(half + 1) * 512],
                               start=(k == 0), stop=(k == 1))
                    for i in range(4):
                        pos = WHERE[(layer, "ple", i)]
                        loaded(pe, pos)
                        wg = slot_of(pos).rearrange("p (k c) -> p k c", k=2)
                        for k in range(2):
                            for half in range(2):
                                m = mm(acc(t)[:, half, :], hT[:, 2 * i + k, t * P:(t + 1) * P],
                                       wg[:, k, half * 512:(half + 1) * 512], start=(i == 0 and k == 0), stop=(i == 3 and k == 1))
                    m.then_inc(ple_done, 1)

        @block.scalar
        def _(act):
            copy, activation = nc.scalar.copy, nc.scalar.activation

            def taken(layer, *name):
                n = USE[(layer,) + name]
                act.wait_ge(ex_ready, n + 1)
                return ps[:, n % EXCHANGE, :]

            def square(n, src, rubbish):
                wait_from(act, sq_done, n)
                activation(rubbish, src, ACT.Square, accum_out=sumsq[:, n:n + 1]).then_inc(sq_done, 1)

            def turned_tile(layer, kind, t):
                for b in range(2):
                    bank = taken(layer, kind, t, b)
                    copy(hT[:, 4 * b:4 * b + 4, t * P:(t + 1) * P], bank.rearrange("p (i s) -> p i s", i=4)).then_inc(ex_done, 1)

            def swapped(layer, item):
                if item in ("Aq", "Ak"):
                    for u in range(2):
                        bank = taken(layer, "swap", item, u)
                        dst = qaT if item == "Aq" else kaT
                        copy(dst[0:A_QK, 2 * u:2 * u + 2, :], bank[0:A_QK, :].rearrange("p (h s) -> p h s", h=2)).then_inc(ex_done, 1)
                elif item == "An":
                    for u, (a, n) in enumerate(((0, 2), (2, 1))):
                        bank = taken(layer, "swap", item, u)
                        copy(lowT[:, a:a + n, :], bank[:, 0:n * SEQ].rearrange("p (h s) -> p h s", h=n)).then_inc(ex_done, 1)
                elif item[-1] == "q":
                    a = 0 if item[0] in "BD" else 2 + 2 * int(item[1])
                    bank = taken(layer, "swap", item, 0)
                    copy(qT[:, a:a + 2, :], bank.rearrange("p (h s) -> p h s", h=2)).then_inc(ex_done, 1)
                else:
                    bank = taken(layer, "swap", item, 0)
                    if layer == 0:
                        act.wait_ge(kz_zero, 1)
                    for half in range(2):
                        r = slice(half * HD, (half + 1) * HD)
                        if item[0] in "BD":
                            ins = copy(kz[r, half, :], bank[r, 0:SEQ])
                        else:
                            a = 2 + 4 * int(item[1]) + half
                            ins = copy(kz[r, a:a + 3:2, :], bank[r, :].rearrange("p (h s) -> p h s", h=2))
                    ins.then_inc(ex_done, 1)

            def silus(ff, block0, tokens):
                for j in range(FF_BLOCKS):
                    act.wait_ge(ff.gu_ready, block0 + j + 1)
                    wait_from(act, ff.hidden_ready, block0 + j - 3)
                    activation(silu[:, j, 0:tokens], ps[:, j, SEQ:SEQ + tokens], ACT.Silu).then_inc(ff.silu_ready, 1)

            def dispatched(ps_):
                def bank(*name):
                    n = ps_.ex0 + DISPATCH[name]
                    act.wait_ge(ps_.ex_ready, n + 1)
                    return ps[:, n % EXCHANGE, :]

                copy(gcol, bank("gcol")[:, 0:8]).then_inc(ps_.ex_done, 1)
                for i in range(4):
                    copy(spread[:, 2 * i:2 * i + 2, :], bank("spread", i).rearrange("p (e s) -> p e s", e=2)).then_inc(ps_.ex_done, 1)
                for e in range(8):
                    for b in range(2):
                        copy(xg[:, e, b * 512:(b + 1) * 512], bank("gather", e, b)).then_inc(ps_.ex_done, 1)

            def expert_silus(ps_):
                n, ff = FF_BODIES[1], ps_.ff
                with act.Fori(0, N_EXPERTS) as e:
                    with act.Fori(0, n) as c:
                        silus(ff, (e * n + c) * FF_BLOCKS + ff.before, CAP)
                    act.wait_ge(ff.down_done, (e + 1) * N_MOE_BLOCKS + ff.before)
                    act.wait_ge(ps_.cur_s_ready, e + 1)
                    activation(ys[:, 0:512], acc(0)[:, 0, :], ACT.Copy, scale=cur_g).then_inc(ps_.ys_act, 1)

            act.wait_ge(x_in_s, 16)
            for layer in range(DEPTH):
                s0 = STATS * layer
                for t in range(NT):
                    if layer:
                        act.wait_ge(x_done, X_COUNT(layer - 1, 2, t))
                    square(s0 + ST_PRE + t, x[:, t, :], post_tmp[:, 0, :])
                for t in range(NT):
                    turned_tile(layer, "pre", t)
                for s in MIXER:
                    if s[0] == "z":
                        c, w = s[1]
                        bank = taken(layer, "z", c)
                        copy(z[:, :, c:c + w], bank.rearrange("p (t s) -> p t s", t=NT)[:, :, 0:w]).then_inc(ex_done, 1)
                    elif s[0] == "norm_a":
                        act.wait_ge(ex_done, USE[(layer, "z", A0 + 256)] + 1)
                        for i, (a, width) in enumerate(((0, A_Q_RANK), (A_Q_RANK, A_KV_RANK))):
                            for t in range(NT):
                                square(s0 + ST_A + NT * i + t, z[:, t, a:a + width], egate[:, 0, 0:width])
                    elif s[0] == "swap":
                        swapped(layer, s[1])
                    elif s[0] == "project_a":
                        for t in range(NT):
                            bank = taken(layer, "qa", t)
                            if t == 0:
                                act.wait_ge(ex_ready, USE[(layer, "kva", 0)] + 1)
                            copy(qa_sb[:, t, :], bank[:, 0:384]).then_inc(ex_done, 1)
                            bank = taken(layer, "kva", t)
                            copy(kva[:, t, :], bank).then_inc(ex_done, 1)
                    elif s[0] == "score":
                        _, j, b, h = s
                        n, i = len(JOBS) * layer + j, j % 2
                        scale = (A_QK if b == "A" else HD) ** -0.5
                        act.wait_ge(bias_done, n + 1)
                        for t in range(NT):
                            e = probs[:, i, t, 0:NSETS[b], :]
                            ins = activation(e, e, ACT.Exp, bias=bias[:, i, t:t + 1], scale=scale, accum_out=total[:, i, t:t + 1])
                        if b == "D":
                            ins = activation(sunk[:, i, :], bias[:, i, :], ACT.Exp, bias=sink[:, h:h + 1])
                        ins.then_inc(exp_done, 1)
                    elif s[0] == "turn":
                        _, j, b, h = s
                        for g in range(NSETS[b]):
                            bank = taken(layer, "turn", j, g)
                            n = SETS * layer + SET0[j] + g
                            wait_from(act, pv_done, n - NPT + 1)
                            copy(pT[:, n % NPT, :, :], bank.rearrange("p (k s) -> p k s", k=NT)).then_inc(ex_done, 1)
                    elif s[0] == "pv" and s[3] % 2:
                        _, j, b, h = s
                        act.wait_ge(pv_done, SETS * layer + SET0[j + 1])
                        copy(oT[:, 2 * BRANCH_ID[b] + h // 2, :], O_BANK).then_inc(o_done, 1)
                    elif s[0] == "fill":
                        u = s[1]
                        act.wait_ge(unit_ready, UNITS * layer + u + 1)
                        wait_from(act, unit_done, UNITS * layer + u - 1)
                        activation(egate[:, u % 2, :], ps[:, 6 + u % 2, 0:SEQ], ACT.Exp, scale=-1.0).then_inc(egate_done, 1)
                for t in range(NT):
                    act.wait_ge(mix_done, NT * layer + t + 1)
                    square(s0 + ST_POST + t, acc(t).rearrange("p b c -> p (b c)"), junk)
                for t in range(NT):
                    act.wait_ge(x_done, X_COUNT(layer, 0, t))
                    square(s0 + ST_FPRE + t, x[:, t, :], junk)
                for t in range(NT):
                    turned_tile(layer, "fpre", t)
                if layer % 2 == 0:
                    silus(ffn, 0, SEQ)
                    with act.Fori(1, FF_BODIES[0]) as c:
                        silus(ffn, c * FF_BLOCKS, SEQ)
                    act.wait_ge(ffn.down_done, N_FFN_BLOCKS)
                    for t in range(NT):
                        square(s0 + ST_FPOST + t, acc(t).rearrange("p b c -> p (b c)"), junk)
                else:
                    bank = taken(layer, "logits")
                    copy(lg, bank[:, 0:NT * 8].rearrange("p (t e) -> p t e", t=NT)).then_inc(ex_done, 1)
                    act.wait_ge(route_exp_in, 1)
                    activation(rt[:, 3, :], rt[:, 2, :], ACT.Exp).then_inc(route_exp, 1)
                    bank = taken(layer, "rank")
                    copy(rank, bank[:, 0:24].rearrange("p (t e) -> p t e", t=3)).then_inc(ex_done, 1)
                    dispatched(main_pass)
                    expert_silus(main_pass)
                    act.wait_ge(overflow_ready, 1)
                    more = act.value_load(overflow[0:1, 0:1], min_val=0, max_val=1)
                    with act.If(more > 0):
                        act.sem_inc(over.silu_ready, 4)
                        dispatched(over_pass)
                        expert_silus(over_pass)
                    act.wait_ge(moe_done, 1)
                    for t in range(NT):
                        square(s0 + ST_FPOST + t, fsum[:, t, :], junk)
                for t in range(NT):
                    turned_tile(layer, "xt", t)
                bank = taken(layer, "pt")
                copy(pleT, bank.rearrange("p (k s) -> p k s", k=2)).then_inc(ex_done, 1)
                for t in range(NT):
                    act.wait_ge(ple_done, NT * layer + t + 1)
                    activation(xn[:, t, :], acc(t).rearrange("p b c -> p (b c)"), ACT.Exp, scale=-1.0).then_inc(ple_exp, 1)
                for t in range(NT):
                    act.wait_ge(ple_prod, NT * layer + t + 1)
                    square(s0 + ST_PLE + t, xn[:, t, :], post_tmp[:, t, :])

        @block.vector
        def _(dve):
            step = Count(dve_step)
            v = nc.vector

            def link(ins, s=None):
                s = s or step
                s.up(ins)
                s.wait(dve)

            def normed(layer, which, g, st):
                n = 5 * layer + g
                dve.wait_ge(gain_in[n % 2], 16 * (n // 2 + 1))
                for t in range(NT):
                    k = STATS * layer + st + t
                    dve.wait_ge(rstd_done, k + 1)
                    v.scalar_tensor_tensor(out=xn[:, t, :], in0=x[:, t, :], scalar=rstd[:, k:k + 1], in1=gain[:, n % 2, :],
                                           op0=ALU.mult, op1=ALU.mult).then_inc(xn_done, 1)

            def residual(layer, g, st, src, tmp):
                n = 5 * layer + g
                dve.wait_ge(gain_in[n % 2], 16 * (n // 2 + 1))
                for t in range(NT):
                    k = STATS * layer + st + t
                    dve.wait_ge(rstd_done, k + 1)
                    link(v.scalar_tensor_tensor(out=tmp(t), in0=src(t), scalar=rstd[:, k:k + 1], in1=gain[:, n % 2, :],
                                                op0=ALU.mult, op1=ALU.mult))
                    v.tensor_tensor(x[:, t, :], x[:, t, :], tmp(t), ALU.add).then_inc(x_done, 1)

            def rotate(src, dst, table, t, heads, groups):
                width = src.shape[2]
                half = width // groups // 2
                n = heads * width
                cos, sin = tab[table][:, 0, t, :], tab[table][:, 1, t, :]
                a = rot[:, 0, 0:n].rearrange("p (h d) -> p h d", h=heads)
                b = rot[:, 1, 0:n].rearrange("p (h d) -> p h d", h=heads)
                link(v.tensor_tensor(a, src, cos.unsqueeze(1).broadcast_to([P, heads, width]), ALU.mult))
                for g in range(groups):
                    for i in range(2):
                        to = slice((2 * g + i) * half, (2 * g + i + 1) * half)
                        of = slice((2 * g + 1 - i) * half, (2 * g + 2 - i) * half)
                        link(v.tensor_tensor(b[:, :, to], src[:, :, of], sin[:, to].unsqueeze(1).broadcast_to([P, heads, half]), ALU.mult))
                if dst is None:
                    return a, b
                return v.tensor_tensor(dst, a, b, ALU.add)

            def stage(layer, item):
                i = STAGED.index(item)
                n = len(STAGED) * layer + i
                if n >= 2:
                    l0, last = divmod(n - 2, len(STAGED))
                    name = STAGED[last]
                    dve.wait_ge(ex_ready, USE[(l0, "swap", name, 1 if name[0] == "A" else 0)] + 1)
                wait_from(dve, staged_done, n)
                return staged[:, n % 2]

            def rope(layer, item):
                r = stage(layer, item)
                b = item[0]
                if b == "A":
                    for t in range(NT):
                        rv = r[:, t, :].rearrange("p (h d) -> p h d", h=A_HEADS)
                        if item == "Aq":
                            if t == 0:
                                dve.wait_ge(ex_done, USE[(layer, "kva", NT - 1)] + 1)
                            src = qa_sb[:, t, :].rearrange("p (h d) -> p h d", h=A_HEADS)
                            link(rotate(src[:, :, A_NOPE:A_QK], rv[:, :, A_NOPE:A_QK], "a", t, A_HEADS, 1))
                            last = v.tensor_copy(rv[:, :, 0:A_NOPE], src[:, :, 0:A_NOPE])
                        else:
                            src = z[:, t, A_Q_RANK + A_KV_RANK:B0].unsqueeze(1)
                            one, two = rotate(src, None, "a", t, 1, 1)
                            link(v.tensor_tensor(rv[:, :, A_NOPE:A_QK], one.broadcast_to([P, A_HEADS, A_ROPE]),
                                                 two.broadcast_to([P, A_HEADS, A_ROPE]), ALU.add))
                            last = v.tensor_copy(rv[:, :, 0:A_NOPE],
                                                 kva[:, t, :].rearrange("p (h d) -> p h d", h=A_HEADS)[:, :, 0:A_NOPE])
                        if t == 0:
                            link(last)
                    last.then_inc(staged_done, 1)
                    return
                heads = 4 if item[-1] == "q" or b == "C" else 2
                if b == "C":
                    col = C0 + int(item[1]) * 12 * HD + (4 * HD if item[2] == "k" else 0)
                    dve.wait_ge(ex_done, USE[(layer, "z", col)] + 1)
                else:
                    col = (B0 if b == "B" else D0) + (4 * HD if item[1] == "k" else 0)
                    if b == "D":
                        dve.wait_ge(ex_done, USE[(layer, "z", D0 + 256)] + 1)
                for t in range(NT):
                    src = z[:, t, col:col + heads * HD].rearrange("p (h d) -> p h d", h=heads)
                    one, two = rotate(src, None, "axial" if b == "B" else "full", t, heads, 2 if b == "B" else 1)
                    dst = r[:, t, 0:heads * HD]
                    if b in "BD" and heads == 4:
                        dst = dst.rearrange("p (b x d) -> p x b d", b=2, x=2)
                        one = one.rearrange("p (x b) d -> p x b d", x=2)
                        two = two.rearrange("p (x b) d -> p x b d", x=2)
                    else:
                        dst = dst.rearrange("p (h d) -> p h d", h=heads)
                    last = v.tensor_tensor(dst, one, two, ALU.add)
                    if t == 0:
                        link(last)
                last.then_inc(staged_done, 1)

            def softmax(layer, j, b, h):
                i, n = j % 2, len(JOBS) * layer + j
                scale = (A_QK if b == "A" else HD) ** -0.5
                if n >= 2:
                    l0, jj = divmod(n - 2, len(JOBS))
                    dve.wait_ge(ex_ready, USE[(l0, "turn", jj, NSETS[JOBS[jj][0]] - 1)] + 1)
                for g in range(NSETS[b]):
                    k = SETS * layer + SET0[j] + g
                    dve.wait_ge(scored, k + 1)
                    for t in range(NT):
                        s = ps[:, 4 + k % 2, t * SEQ:(t + 1) * SEQ]
                        e, m = probs[:, i, t, g, :], peak[:, i, t, g:g + 1]
                        if b in "AB":
                            ins = v.tensor_scalar(e, s, 1.0, None, ALU.mult, ALU.max, accum_out=m)
                        else:
                            ins = v.tensor_tensor_reduce(out=e, in0=s, in1=mask[:, g if b == "C" else 3, t, :], scale=1.0,
                                                         scalar=-3.0e38, op0=ALU.add, op1=ALU.max, accum_out=m)
                    ins.then_inc(score_read, 1)
                dve.wait_ge(score_read, SETS * layer + SET0[j + 1])
                src = peak[:, i, :, 0]
                if b == "C":
                    link(v.tensor_reduce(top[:, i, :], peak[:, i, :, :], AX.X, ALU.max))
                    src = top[:, i, :]
                if b == "D":
                    link(v.tensor_scalar(top[:, i, :], src, scale, sink[:, h:h + 1], ALU.mult, ALU.max))
                    v.tensor_scalar(bias[:, i, :], top[:, i, :], -1.0, None, ALU.mult).then_inc(bias_done, 1)
                else:
                    v.tensor_scalar(bias[:, i, :], src, -scale, None, ALU.mult).then_inc(bias_done, 1)
                dve.wait_ge(exp_done, n + 1)
                if b == "D":
                    link(v.tensor_tensor(total[:, i, :], total[:, i, :], sunk[:, i, :], ALU.add))
                link(v.reciprocal(inv[:, i, :], total[:, i, :]))
                for t in range(NT):
                    e = probs[:, i, t, 0:NSETS[b], :]
                    ins = v.tensor_scalar(e, e, inv[:, i, t:t + 1], None, ALU.mult)
                ins.then_inc(prob_done, 1)

            def hiddens(ff, block0, tokens):
                for j in range(FF_BLOCKS):
                    dve.wait_ge(ff.silu_ready, block0 + j + 1)
                    wait_from(dve, ff.down_done, block0 + j - 3)
                    v.tensor_tensor(hidden[:, j, 0:tokens], silu[:, j, 0:tokens], ps[:, j, 0:tokens], ALU.mult)\
                        .then_inc(ff.hidden_ready, 1)

            def route():
                bc = lambda a: a.unsqueeze(2).broadcast_to([P, NT, 8])
                r = lambda n: rt[:, n, :]
                dve.wait_ge(ex_done, USE[(1, "logits")] + 1)
                link(v.tensor_tensor(lg, lg, rtr_b[:, :, :], ALU.add))
                for n, onehot in enumerate((first, second)):
                    link(v.tensor_reduce(r(n), lg, AX.X, ALU.max))
                    link(v.tensor_tensor(eq, lg, bc(r(n)), ALU.is_equal))
                    link(v.tensor_scalar(eq, eq, -100.0, 100.0, ALU.mult, ALU.add))
                    link(v.tensor_tensor(idx, eq, iota8, ALU.add))
                    link(v.tensor_reduce(r(4), idx, AX.X, ALU.min))
                    link(v.tensor_tensor(onehot, idx, bc(r(4)), ALU.is_equal))
                    if n == 0:
                        link(v.scalar_tensor_tensor(out=lg, in0=onehot, scalar=-3.0e38, in1=lg, op0=ALU.mult, op1=ALU.add))
                v.tensor_tensor(r(2), r(1), r(0), ALU.subtract).then_inc(route_exp_in, 1)
                dve.wait_ge(route_exp, 1)
                link(v.tensor_scalar(r(5), r(3), 1.0, None, ALU.add))
                link(v.reciprocal(r(6), r(5)))
                link(v.tensor_tensor(r(7), r(3), r(6), ALU.mult))
                link(v.tensor_tensor(weight, first, bc(r(6)), ALU.mult))
                link(v.tensor_tensor(eq, second, bc(r(7)), ALU.mult))
                link(v.tensor_tensor(weight, weight, eq, ALU.add))
                v.tensor_tensor(chosen, first, second, ALU.add).then_inc(routed, 1)
                dve.wait_ge(ex_done, USE[(1, "rank")] + 1)
                link(v.tensor_scalar(overflow_f, rank[:, 2, :], float(CAP), None, ALU.is_gt))
                link(v.tensor_reduce(r(0)[:, 0:1], overflow_f, AX.X, ALU.max))
                v.tensor_copy(overflow[:, :], r(0)[:, 0:1]).then_inc(overflow_ready, 1)

            def picks(ps_):
                for t in range(NT):
                    for e in range(8):
                        ins = v.tensor_scalar(pick[:, t, e, :], iota, rank[:, t, e:e + 1], chosen[:, t, e:e + 1], ALU.is_equal, ALU.mult)
                ins.then_inc(ps_.picked, 1)

            def expert_hiddens(ps_):
                n, ff = FF_BODIES[1], ps_.ff
                flat = cur_x.rearrange("p k n -> p (k n)")
                dve.wait_ge(ps_.ex_done, ps_.ex0 + len(DISPATCH))
                v.tensor_copy(flat, xg[:, 0, :]).then_inc(ps_.cur_x_ready, 1)
                with dve.Fori(0, N_EXPERTS) as e:
                    v.tensor_copy(cur_spread, spread[:, e, :])
                    v.tensor_copy(cur_g, gcol[:, bass.ds(e, 1)]).then_inc(ps_.cur_s_ready, 1)
                    with dve.Fori(0, n) as c:
                        hiddens(ff, (e * n + c) * FF_BLOCKS + ff.before, CAP)
                    dve.wait_ge(ff.gu_ready, (e + 1) * N_MOE_BLOCKS + ff.before)
                    dve.wait_ge(ps_.cur_x_ready, e + 1)
                    v.tensor_copy(flat, xg[:, (e + 1) % N_EXPERTS, :]).then_inc(ps_.cur_x_ready, 1)
                    dve.wait_ge(ff.down_done, (e + 1) * N_MOE_BLOCKS + ff.before)
                    dve.wait_ge(ps_.cur_s_ready, e + 1)
                    v.tensor_scalar(ys[:, 512:1024], acc(0)[:, 1, :], cur_g, None, ALU.mult).then_inc(ps_.ys_dve, 1)
                    for i, t in enumerate((1, 0)):
                        dve.wait_ge(ps_.back, e * NT + i + 1)
                        v.tensor_tensor(fsum[:, t, :], fsum[:, t, :], acc(t).rearrange("p b c -> p (b c)"), ALU.add)\
                            .then_inc(ps_.added, 1)
                    dve.wait_ge(ps_.added, e * NT + NT)

            dve.wait_ge(x_in_s, 16)
            dve.wait_ge(const_in_s, 16)
            for layer in range(DEPTH):
                normed(layer, "pre", 0, ST_PRE)
                for s in MIXER:
                    if s[0] == "norm_b":
                        dve.wait_ge(ex_done, USE[(layer, "z", B0 + 256)] + 1)
                        dve.wait_ge(params_in, PARAMS(layer))
                        for t in range(NT):
                            q = z[:, t, B0:B0 + 6 * HD]
                            link(v.tensor_tensor(rot[:, 0, :], q, q, ALU.mult))
                            ins = v.tensor_reduce(sumsq_b[:, t, :], rot[:, 0, :].rearrange("p (h d) -> p h d", h=6), AX.X, ALU.add)
                            if t == 0:
                                link(ins)
                        ins.then_inc(sqb_done, 1)
                        dve.wait_ge(rstdb_done, layer + 1)
                        for t in range(NT):
                            q = z[:, t, B0:B0 + 6 * HD].rearrange("p (h d) -> p h d", h=6)
                            link(v.tensor_tensor(q, q, rstd_b[:, t, :].unsqueeze(2).broadcast_to([P, 6, HD]), ALU.mult))
                            link(v.tensor_tensor(q, q, gain_b[:, :, :], ALU.mult))
                    elif s[0] == "norm_a":
                        r = stage(layer, "An")
                        for t in range(NT):
                            for i, (a, w) in enumerate(((0, A_Q_RANK), (A_Q_RANK, A_KV_RANK))):
                                k = STATS * layer + ST_A + NT * i + t
                                dve.wait_ge(rstd_done, STATS * layer + ST_A + 2 * NT)
                                ins = v.scalar_tensor_tensor(out=r[:, t, a:a + w], in0=z[:, t, a:a + w], scalar=rstd[:, k:k + 1],
                                                             in1=gain_a[:, a:a + w], op0=ALU.mult, op1=ALU.mult)
                        ins.then_inc(staged_done, 1)
                    elif s[0] == "rope":
                        rope(layer, s[1])
                    elif s[0] == "score":
                        softmax(layer, *s[1:])
                    elif s[0] == "fill":
                        u = s[1]
                        n, c = UNITS * layer + u, u % 8
                        e = egate[:, u % 2, :]
                        dve.wait_ge(egate_done, n + 1)
                        link(v.tensor_scalar(e, e, 1.0, None, ALU.add))
                        link(v.reciprocal(e, e))
                        up = ps[:, 6 + u % 2, SEQ:2 * SEQ]
                        if u < 8:
                            v.tensor_tensor(mergedT[:, c, :], up, e, ALU.mult).then_inc(unit_done, 1)
                        else:
                            link(v.tensor_tensor(e, up, e, ALU.mult))
                            v.tensor_tensor(mergedT[:, c, :], mergedT[:, c, :], e, ALU.add).then_inc(unit_done, 1)
                flat = lambda t: acc(t).rearrange("p b c -> p (b c)")
                residual(layer, 1, ST_POST, flat, lambda t: post_tmp[:, t, :])
                normed(layer, "fpre", 2, ST_FPRE)
                if layer % 2 == 0:
                    dve.wait_ge(x_done, X_COUNT(layer, 0, NT - 1))
                    hiddens(ffn, 0, SEQ)
                    with dve.Fori(1, FF_BODIES[0]) as c:
                        hiddens(ffn, c * FF_BLOCKS, SEQ)
                    residual(layer, 3, ST_FPOST, flat, lambda t: post_tmp[:, t, :])
                else:
                    link(v.memset(fsum, 0.0))
                    route()
                    dve.wait_ge(overflow_ready, 1)
                    picks(main_pass)
                    expert_hiddens(main_pass)
                    more = dve.value_load(overflow[0:1, 0:1], min_val=0, max_val=1)
                    with dve.If(more > 0):
                        dve.sem_inc(over.hidden_ready, 4)
                        v.tensor_scalar(rank, rank, float(-CAP), None, ALU.add).then_inc(over_ranked, 1)
                        dve.wait_ge(over_ranked, 1)
                        picks(over_pass)
                        expert_hiddens(over_pass)
                    v.memset(overflow_f, 0.0).then_inc(moe_done, 1)
                    residual(layer, 3, ST_FPOST, lambda t: fsum[:, t, :], lambda t: xn[:, t, :])
                for t in range(NT):
                    n = NT * layer + t
                    dve.wait_ge(ple_exp, n + 1)
                    e = xn[:, t, :]
                    link(v.tensor_scalar(e, e, 1.0, None, ALU.add))
                    link(v.reciprocal(e, e))
                    v.tensor_tensor(e, e, ps[:, 2 * t:2 * t + 2, :].rearrange("p b c -> p (b c)"), ALU.mult).then_inc(ple_prod, 1)
                residual(layer, 4, ST_PLE, lambda t: xn[:, t, :], lambda t: post_tmp[:, t, :])


_INS = ["x", "p", "w_in", "a_qa_g", "a_kva_g", "a_w_uq", "a_w_ukv", "b_q_g", "b_k_g", "d_sink", "w_branch", "w_out",
        "mix_pre_g", "mix_post_g", "ffn_pre_g", "ffn_post_g", "ffn_w_gate", "ffn_w_up", "ffn_w_down",
        "router_w", "router_b", "moe_w_gate", "moe_w_up", "moe_w_down", "ple_w_proj", "ple_w_gate", "ple_post_g"]


def kernel(**inputs):
    import concourse.bacc as bacc
    from concourse.bass_utils import run_bass_kernel_spmd as run

    nc = bacc.Bacc("TRN2", target_bir_lowering=False, num_devices=1)
    arrays, args = {}, []
    for name in _INS:
        a = np.ascontiguousarray(inputs[name])
        arrays[f"in_{name}_dram"] = a
        args.append(nc.dram_tensor(f"in_{name}_dram", a.shape, mybir.dt.from_np(a.dtype), kind="ExternalInput").ap())
    arrays["in_const_dram"] = constants()
    args.append(nc.dram_tensor("in_const_dram", (P, CONST_W), F32, kind="ExternalInput").ap())
    args.append(nc.dram_tensor("out_0_dram", (1, SEQ, D_MODEL), F32, kind="ExternalOutput").ap())
    trunk(nc, args)
    r = run(nc, [arrays], core_ids=[0])
    return r.results[0]["out_0_dram"]
```

```python
from contextlib import ExitStack

import numpy as np

import concourse.bass as bass
from concourse import mybir

ALU = mybir.AluOpType
ACT = mybir.ActivationFunctionType
AX = mybir.AxisListType
F32 = mybir.dt.float32
F32R = mybir.dt.float32r
I32 = mybir.dt.int32

P = 128
D_MODEL, SEQ, DEPTH = 1024, 256, 2
NT = SEQ // P
NK = D_MODEL // P
HD = 64
GRID_W, ROPE_THETA = 64, 10000.0
EPS, MASKED = 1e-6, -1e30
A_Q_RANK, A_KV_RANK, A_ROPE, A_NOPE, A_HEADS = 256, 128, 32, 64, 4
A_QK = A_NOPE + A_ROPE
PATTERNS = ((128, 1), (512, 4), (2048, 16))
D_HALF_WINDOW = 128
A0 = 0
B0 = A_Q_RANK + A_KV_RANK + A_ROPE
C0 = B0 + 8 * HD
D0 = C0 + len(PATTERNS) * 12 * HD
GATE0 = D0 + 8 * HD
D_FF, MOE_FF, N_EXPERTS = 4096, 3584, 8
CAP = P
PLE_DIM = 256

RING = 6
SLOT = 2048
WORK = 26176
CW = SLOT // NK

CONST_FIELDS = (("ident", P), ("upper", P), ("ones", P), ("iota", P), ("iota8", NT * 8),
                ("mask", 4 * NT * SEQ), ("full", 2 * NT * HD), ("axial", 2 * NT * HD), ("rope_a", 2 * NT * A_ROPE))
CONST_AT, _n = {}, 0
for _name, _w in CONST_FIELDS:
    CONST_AT[_name] = _n
    _n += _w
CONST_W = _n


def constants():
    c = np.zeros((P, CONST_W), np.float32)

    def put(name, a):
        c[:, CONST_AT[name]:CONST_AT[name] + a.reshape(P, -1).shape[1]] = a.reshape(P, -1)

    p = np.arange(P)
    put("ident", np.eye(P, dtype=np.float32))
    put("upper", (p[:, None] < p[None, :]).astype(np.float32))
    put("ones", np.ones((P, P), np.float32))
    put("iota", np.broadcast_to(p.astype(np.float32), (P, P)))
    put("iota8", np.broadcast_to(np.tile(np.arange(8, dtype=np.float32), NT), (P, NT * 8)))
    q = (np.arange(NT)[None, :] * P + p[:, None])[:, :, None]
    k = np.arange(SEQ)[None, None, :]
    masks = []
    for window, dil in PATTERNS:
        masks.append((q % dil == k % dil) & (np.abs(q - k) <= window // 2))
    masks.append(np.abs(q - k) <= D_HALF_WINDOW)
    put("mask", np.stack([np.where(m, 0.0, MASKED) for m in masks], 1).astype(np.float32))

    def table(pos, dim):
        half = dim // 2
        inv = np.power(np.float32(ROPE_THETA), -np.arange(half, dtype=np.float32) / np.float32(half))
        ang = pos.astype(np.float32)[..., None] * inv.astype(np.float32)
        cos, sin = np.cos(ang.astype(np.float64)), np.sin(ang.astype(np.float64))
        return np.concatenate([cos, cos], -1), np.concatenate([-sin, sin], -1)

    pos = np.arange(NT)[None, :] * P + p[:, None]
    put("full", np.stack(table(pos, HD), 1).astype(np.float32))
    row, col = table(pos // GRID_W, HD // 2), table(pos % GRID_W, HD // 2)
    put("axial", np.stack([np.concatenate([row[i], col[i]], -1) for i in range(2)], 1).astype(np.float32))
    put("rope_a", np.stack(table(pos, A_ROPE), 1).astype(np.float32))
    return c


BRANCH_ORDER = "BADC"
BRANCH_ID = {"A": 0, "B": 1, "C": 2, "D": 3}
Z_SLOTS = {"B": [(B0, 256), (B0 + 256, 256)], "A": [(A0, 256), (A0 + 256, 160)],
           "D": [(D0, 256), (D0 + 256, 256)], "C": [(C0 + 256 * i, 256) for i in range(9)]}


def mixer_steps():
    zc = [("z", s) for s in Z_SLOTS["C"]]
    steps = [("z", s) for b in "BA" for s in Z_SLOTS[b]] + [("norm_b",), ("rope", "Bq"), ("rope", "Bk")]
    steps += [("z", s) for s in Z_SLOTS["D"]] + zc[0:2] + [("swap", "Bq"), ("swap", "Bk"), ("norm_a",), zc[2], ("swap", "An")]
    fillers = {("B", 0): [zc[3], ("project_a",), zc[4]], ("B", 1): zc[5:7], ("B", 2): zc[7:8], ("B", 3): zc[8:9]}
    staged = {("B", 1): "Aq", ("B", 2): "Ak", ("B", 3): "C0q", ("A", 0): "Dq", ("A", 1): "Dk", ("A", 2): "C0k",
              ("A", 3): "C1q", ("D", 0): "C1k", ("D", 1): "C2q", ("D", 2): "C2k"}
    heads = [(b, h) for b in BRANCH_ORDER for h in range(4)]
    fill = 0
    steps += [("score", 0) + heads[0]]
    for j, (b, h) in enumerate(heads):
        item = staged.get((b, h))
        if item:
            steps += [("rope", item)]
        if b == "B":
            steps += fillers[(b, h)]
        else:
            steps += [("fill", fill), ("fill", fill + 1)]
            fill += 2
        steps += [("turn", j, b, h)]
        last_of_branch = h == 3
        if not last_of_branch:
            steps += [("score", j + 1) + heads[j + 1]]
        steps += [("pv", j, b, h)]
        if item:
            steps += [("swap", item)]
        if last_of_branch and j + 1 < len(heads):
            steps += [("score", j + 1) + heads[j + 1]]
    steps += [("fill", u) for u in range(fill, 32)]
    return steps


MIXER = mixer_steps()
ROPES = [s[1] for s in MIXER if s[0] == "rope"]
NSETS = {"A": 1, "B": 1, "C": 3, "D": 1}
JOBS = [(s[2], s[3]) for s in MIXER if s[0] == "score"]
SET0 = [sum(NSETS[b] for b, _ in JOBS[:j]) for j in range(len(JOBS) + 1)]
SETS = SET0[-1]
UNITS = 32
STAGED = [s[1] for s in MIXER if s[0] == "rope" or s == ("swap", "An")]


def statistics():
    order = [(0, "pre", t) for t in range(NT)]
    for layer in range(DEPTH):
        order += [(layer, kind, t) for kind in ("low_q", "low_kv") for t in range(NT)]
        order += [(layer, kind, t) for t in range(NT) for kind in ("post", "fpre")]
        order += [(layer, "fpost", t) for t in range(NT)]
        for t in range(NT):
            order += [(layer, "ple", t)] + ([(layer + 1, "pre", t)] if layer + 1 < DEPTH else [])
    return {k: n for n, k in enumerate(order)}


STAT = statistics()


def exchange_uses():
    uses = []

    def add(layer, *name):
        uses.append((layer,) + name)

    for layer in range(DEPTH):
        for t in range(NT):
            for b in range(2):
                add(layer, "pre", t, b)
        for s in MIXER:
            if s[0] == "z":
                add(layer, "z", s[1][0])
            elif s[0] == "swap":
                for i in range(2 if s[1] in ("Aq", "Ak", "An") else 1):
                    add(layer, "swap", s[1], i)
            elif s[0] == "project_a":
                for t in range(NT):
                    add(layer, "qa", t)
                    add(layer, "kva", t)
            elif s[0] == "turn":
                for g in range(NSETS[s[2]]):
                    add(layer, "turn", s[1], g)
        for t in range(NT):
            for b in range(2):
                add(layer, "fpre", t, b)
        if layer % 2:
            add(layer, "logits")
            add(layer, "rank")
            for u in dispatch_uses():
                add(layer, *u)
        add(layer, "pt")
        for t in range(NT):
            for half in range(2):
                add(layer, "proj", t, half)
        for t in range(NT):
            for b in range(2):
                add(layer, "xt", t, b)
    return {u: n for n, u in enumerate(uses)}


def dispatch_uses():
    return [("gcol",)] + [("spread", i) for i in range(4)] + [("gather", e, b) for e in range(8) for b in range(2)]


USE = exchange_uses()
DISPATCH = {u: n for n, u in enumerate(dispatch_uses())}
EXCHANGE = 3


class Count:

    def __init__(self, sem, at=0):
        self.sem, self.at = sem, at

    def up(self, ins):
        ins.then_inc(self.sem, 1)
        self.at = self.at + 1

    def wait(self, eng):
        eng.wait_ge(self.sem, self.at)


def X_COUNT(layer, which, t):
    return NT * (3 * layer + which) + t + 1


def PARAMS(layer):
    return 16 * (11 * (layer + 1) + 3)


def wait_from(eng, sem, value):
    if not isinstance(value, int) or value > 0:
        eng.wait_ge(sem, value)


class FeedForward:

    def __init__(self, sems, before, chunks_before):
        self.gu_ready, self.silu_ready, self.hidden_ready, self.down_done, self.step, self.down_hi, self.down_split = sems
        self.before, self.chunks_before = before, chunks_before


def ring_plan():
    plan, at, loops = {}, 0, {}
    for layer in range(DEPTH):
        z = [s[1] for s in MIXER if s[0] == "z"]
        seen = 0
        for s in MIXER:
            if s[0] == "z":
                plan[at] = (layer, "z") + s[1]
                at += 1
            if s[0] == "fill" and s[1] % 8 == 0:
                b = BRANCH_ID[BRANCH_ORDER[s[1] // 8]]
                for i in range(4):
                    plan[at] = (layer, "gate", b, i)
                    at += 1
                plan[at] = (layer, "branch", b)
                at += 1
        for i in range(4):
            plan[at] = (layer, "out", i)
            at += 1
        loops[layer] = at
        at += (D_FF if layer % 2 == 0 else N_EXPERTS * MOE_FF) // CW * 3
        plan[at] = (layer, "proj")
        at += 1
        for i in range(4):
            plan[at] = (layer, "ple", i)
            at += 1
    return plan, loops, at


PLAN, LOOPS, _ = ring_plan()
WHERE = {v: k for k, v in PLAN.items()}
FF_BODIES = {0: D_FF // (2 * CW), 1: MOE_FF // (2 * CW)}
FF_BLOCKS = 2 * CW // P
N_FFN_BLOCKS = D_FF // P
N_MOE_BLOCKS = MOE_FF // P


def trunk(nc, args):
    (x_in, p_in, w_in, a_qa_g, a_kva_g, a_w_uq, a_w_ukv, b_q_g, b_k_g, d_sink, w_branch, w_out,
     mix_pre_g, mix_post_g, ffn_pre_g, ffn_post_g, ffn_w_gate, ffn_w_up, ffn_w_down,
     router_w, router_b, moe_w_gate, moe_w_up, moe_w_down, ple_w_proj, ple_w_gate, ple_post_g,
     const_in, out) = args
    ctx = ExitStack()
    with ctx:
        place = [-(-nc.sbuf_base // 64) * 64]

        def sb(name, shape, dt=F32):
            size = 4
            for n in shape[1:]:
                size *= n
            at = place[0]
            place[0] += -(-size // 64) * 64
            return nc.alloc_sbuf_tensor_at(name, shape, dt, offset=at)

        def sem(name):
            return ctx.enter_context(nc.semaphore(name))

        ring_at = place[0]
        ring = sb("ring", [P, RING, SLOT])
        ring_lo = nc.alloc_sbuf_tensor_at("ring_lo", [P, RING, SLOT], F32R, offset=ring_at)
        x = sb("x", [P, NT, D_MODEL])
        xn = sb("xn", [P, NT, D_MODEL])
        hT = sb("hT", [P, NK, SEQ])
        work_at = place[0]
        work = sb("work", [P, WORK])

        def rounded(name, at, shape):
            return nc.alloc_sbuf_tensor_at(name, shape, F32R, offset=work_at + 4 * at)

        cn = sb("cn", [P, CONST_W])
        gain = sb("gain", [P, 2, D_MODEL])
        gain_a = sb("gain_a", [P, 384])
        gain_b = sb("gain_b", [P, 6, HD])
        sink = sb("sink", [P, 4])
        w_uq = sb("w_uq", [P, 2, 384])
        w_ukv = sb("w_ukv", [P, 512])
        rtr_w = sb("rtr_w", [P, NK, 8])
        rtr_b = sb("rtr_b", [P, NT, 8])
        sumsq = sb("sumsq", [P, len(STAT)])
        var = sb("var", [P, len(STAT)])
        rstd = sb("rstd", [P, len(STAT)])
        sumsq_b = sb("sumsq_b", [P, NT, 6])
        var_b = sb("var_b", [P, NT, 6])
        rstd_b = sb("rstd_b", [P, NT, 6])
        minus_half = sb("minus_half", [P, NT * 6])
        peak = sb("peak", [P, 2, NT, 3])
        top = sb("top", [P, 2, NT])
        bias = sb("bias", [P, 2, NT])
        total = sb("total", [P, 2, NT])
        sunk = sb("sunk", [P, 2, NT])
        inv = sb("inv", [P, 2, NT])
        egate = sb("egate", [P, 2, SEQ])

        def carve(start=0):
            at = [start]

            def take(n):
                at[0] += n
                assert at[0] <= WORK
                return work[:, at[0] - n:at[0]]
            return take

        take = carve()
        z = take(NT * GATE0).rearrange("p (t c) -> p t c", t=NT)
        qT = take(8 * SEQ).rearrange("p (b s) -> p b s", b=8)
        qaT = take(4 * SEQ).rearrange("p (b s) -> p b s", b=4)
        kaT = take(4 * SEQ).rearrange("p (b s) -> p b s", b=4)
        probs = take(2 * NT * 3 * SEQ).rearrange("p (j t g s) -> p j t g s", j=2, t=NT, g=3)
        NPT = 3
        pT = take(NPT * 2 * SEQ).rearrange("p (n k s) -> p n k s", n=NPT, k=NT)
        kva = take(NT * 512).rearrange("p (t c) -> p t c", t=NT)
        lowT = take(3 * SEQ).rearrange("p (b s) -> p b s", b=3)
        oT = take(NK * SEQ)
        post_tmp = oT.rearrange("p (t d) -> p t d", t=NT)
        oT = oT.rearrange("p (b s) -> p b s", b=NK)
        kz = take(14 * SEQ).rearrange("p (b s) -> p b s", b=14)
        staged = take(2 * NT * 384).rearrange("p (n t c) -> p n t c", n=2, t=NT)
        rot = take(2 * 384).rearrange("p (n c) -> p n c", n=2)
        qa_sb = xn[:, :, 0:384]
        mergedT = xn[:, :, :].rearrange("p t (b s) -> p (t b) s", s=SEQ)

        up_gate_hi_w = rounded("up_gate_hi_w", 0, [P, 4, SLOT])
        xg = work[:, 0:8192].rearrange("p (e m) -> p e m", e=N_EXPERTS)
        proj = work[:, 0:2048].rearrange("p (t d) -> p t d", t=NT)
        junk = work[:, 4096:4096 + D_MODEL]
        down_hi_w = rounded("down_hi_w", 8192, [P, 2, SLOT])
        down_lo_w = rounded("down_lo_w", 12288, [P, 2, SLOT])
        hidden_hi = rounded("hidden_hi", 16384, [P, 4, SEQ])
        hidden_lo = rounded("hidden_lo", 17408, [P, 4, SEQ])
        take = carve(18432)
        hidden = take(2 * SEQ).rearrange("p (n s) -> p n s", n=2)
        silu = take(4 * SEQ).rearrange("p (n s) -> p n s", n=4)
        cur_spread = take(SEQ)
        small_at = 18432 + 7 * SEQ
        hT_hi = rounded("hT_hi", 20992, [P, NK, SEQ])
        hT_lo = rounded("hT_lo", 23040, [P, NK, SEQ])
        take = carve(20992)
        pick = take(NT * 8 * CAP)
        cur_x, ys = pick[:, 0:D_MODEL].rearrange("p (k n) -> p k n", k=NK), pick[:, D_MODEL:]
        pick = pick.rearrange("p (t e n) -> p t e n", t=NT, e=8)
        spread = take(8 * SEQ).rearrange("p (e s) -> p e s", e=8)
        p_sb = take(NT * PLE_DIM).rearrange("p (t c) -> p t c", t=NT)
        pleT = take(2 * SEQ).rearrange("p (k s) -> p k s", k=2)
        fsum = hT[:, :, :].rearrange("p k s -> p (k s)").rearrange("p (t d) -> p t d", t=NT)
        take = carve(small_at)
        lg = take(NT * 8).rearrange("p (t e) -> p t e", t=NT)
        eq = take(NT * 8).rearrange("p (t e) -> p t e", t=NT)
        idx = take(NT * 8).rearrange("p (t e) -> p t e", t=NT)
        first = take(NT * 8).rearrange("p (t e) -> p t e", t=NT)
        second = take(NT * 8).rearrange("p (t e) -> p t e", t=NT)
        chosen = take(NT * 8).rearrange("p (t e) -> p t e", t=NT)
        weight = take(NT * 8).rearrange("p (t e) -> p t e", t=NT)
        rank = take(3 * 8).rearrange("p (t e) -> p t e", t=3)
        gcol = take(8)
        cur_g = take(1)
        rt = take(NT * 8).rearrange("p (n t) -> p n t", t=NT)
        overflow_f = take(8)
        overflow = sb("overflow", [P, 1], I32)

        ps = ctx.enter_context(nc.psum_tensor("ps", [P, 8, 512], F32))
        O_BANK = ps[:, 3, 0:SEQ]

        def acc(t):
            return ps[:, 4 + 2 * t:6 + 2 * t, :]

        def const(name, n):
            return cn[:, CONST_AT[name]:CONST_AT[name] + n]

        ident, upper, ones = const("ident", P), const("upper", P), const("ones", P)
        iota = const("iota", P)
        iota8 = const("iota8", NT * 8).rearrange("p (t e) -> p t e", t=NT)
        mask = const("mask", 4 * NT * SEQ).rearrange("p (m t s) -> p m t s", m=4, t=NT)
        tab = {"full": const("full", 2 * NT * HD).rearrange("p (f t d) -> p f t d", f=2, t=NT),
               "axial": const("axial", 2 * NT * HD).rearrange("p (f t d) -> p f t d", f=2, t=NT),
               "a": const("rope_a", 2 * NT * A_ROPE).rearrange("p (f t d) -> p f t d", f=2, t=NT)}

        const_in_s, x_in_s = sem("const_loaded"), sem("x_loaded")
        slot_in = [sem(f"slot{i}_loaded") for i in range(RING)]
        gain_in = [sem(f"gain{i}_loaded") for i in range(2)]
        params_in, p_loaded = sem("params_loaded"), sem("p_loaded")
        kz_zero = sem("kz_zeroed")
        ex_ready, ex_done = sem("exchange_ready"), sem("exchange_emptied")
        sq_done, rstd_done = sem("sumsq_done"), sem("rstd_done")
        sqb_done, rstdb_done = sem("sumsq_b_done"), sem("rstd_b_done")
        xn_done, x_done = sem("normed_ready"), sem("residual_ready")
        staged_done = sem("staged_ready")
        qa_read = sem("a_projections_read")
        scored, score_read = sem("scores_ready"), sem("scores_read")
        bias_done, exp_done, prob_done = sem("bias_ready"), sem("exp_ready"), sem("probs_ready")
        pv_done, o_done = sem("pv_done"), sem("o_emptied")
        unit_ready, egate_done, unit_done = sem("unit_ready"), sem("gate_exp_ready"), sem("unit_merged")
        mix_done = sem("mix_ready")
        ple_done, ple_exp, ple_prod = sem("ple_ready"), sem("ple_gate_exp_ready"), sem("ple_product_ready")
        route_exp_in, route_exp, routed = sem("route_difference_ready"), sem("route_exp_ready"), sem("routed")
        overflow_ready, moe_done = sem("overflow_known"), sem("moe_done")
        dve_step, act_step, pool_step = sem("vector_step"), sem("scalar_step"), sem("pool_step")
        stored = sem("stored")

        FF_SEMS = ("gate_up_ready", "silu_ready", "hidden_ready", "down_done", "hidden_step", "down_hi_ready", "down_split")
        ffn = FeedForward([sem(f"ff_{n}") for n in FF_SEMS], 0, 0)
        up_gate_hi, up_gate_split = sem("up_gate_hi_ready"), sem("up_gate_split")
        hT_split = sem("hT_split")
        moe = FeedForward([ffn.gu_ready, ffn.silu_ready, ffn.hidden_ready, ffn.down_done, ffn.step, ffn.down_hi, ffn.down_split],
                          N_FFN_BLOCKS, D_FF // CW)

        class Pass:

            def __init__(self, tag, ff, ex, ex0, slots, pos0, loads0):
                self.ff, self.ex_ready, self.ex_done, self.ex0 = ff, ex[0], ex[1], ex0
                self.slots, self.pos0, self.loads0 = slots, pos0, loads0
                self.picked = sem(f"{tag}_pick_ready")
                self.cur_x_ready, self.cur_s_ready = sem(f"{tag}_tokens_ready"), sem(f"{tag}_spread_ready")
                self.ys_act, self.ys_dve = sem(f"{tag}_y_low_ready"), sem(f"{tag}_y_high_ready")
                self.back, self.added = sem(f"{tag}_scatter_ready"), sem(f"{tag}_scatter_added")

        main_pass = Pass("moe", moe, (ex_ready, ex_done), USE[(1, "gcol")], slot_in, LOOPS[1],
                         [(LOOPS[1] + j) // RING for j in range(RING)])
        over = FeedForward([sem(f"over_{n}") for n in FF_SEMS], 4, 2)
        over_pass = Pass("over", over, (sem("over_exchange_ready"), sem("over_exchange_emptied")), 0,
                         [sem(f"over_slot{i}_loaded") for i in range(RING)], LOOPS[1], [0] * RING)
        over_ranked = sem("over_ranks_ready")

        def slot_of(pos):
            return ring[:, pos % RING, :]

        def loaded(eng, pos):
            eng.wait_ge(slot_in[pos % RING], 16 * (pos // RING + 1))

        def released(pos):
            what = PLAN[pos]
            layer, kind = what[0], what[1]
            if kind == "z":
                return ex_ready, USE[(layer, "z", what[2])] + 1
            if kind == "gate":
                order = BRANCH_ORDER.index("ABCD"[what[2]])
                return unit_ready, UNITS * layer + 8 * order + 2 * what[3] + 2
            if kind == "branch":
                return unit_ready, UNITS * layer + 8 * BRANCH_ORDER.index("ABCD"[what[2]]) + 8
            if kind == "out":
                return mix_done, NT * (layer + 1)
            if kind == "proj":
                return ex_ready, USE[(layer, "proj", NT - 1, 1)] + 1
            return ple_done, NT * (layer + 1)

        def blocks_before(layer):
            return 0 if layer == 0 else N_FFN_BLOCKS

        def blocks_after(layer):
            return N_FFN_BLOCKS if layer == 0 else N_FFN_BLOCKS + N_EXPERTS * N_MOE_BLOCKS

        block = ctx.enter_context(nc.Block())

        @block.sync
        def _(sp):
            w_in_v = [w_in[l].rearrange("(k p) c -> p k c", p=P) for l in range(DEPTH)]

            def load(pos):
                layer, kind, *r = PLAN[pos]
                dst, wide = slot_of(pos), None
                if kind == "z":
                    c, w = r
                    dst = dst.rearrange("p (k c) -> p k c", k=NK)[:, :, 0:w]
                    src = w_in_v[layer][:, :, c:c + w]
                elif kind == "gate":
                    c = GATE0 + r[0] * D_MODEL + r[1] * CW
                    dst = dst.rearrange("p (k c) -> p k c", k=NK)
                    src = w_in_v[layer][:, :, c:c + CW]
                else:
                    dst = dst.rearrange("p (k c) -> p k c", k=2)
                    if kind == "branch":
                        src = w_branch[layer, r[0]].rearrange("(k p) c -> p k c", p=P)
                    elif kind == "out":
                        src = w_out[layer].rearrange("(i k p) c -> i p k c", p=P, k=2)[r[0]]
                    elif kind == "proj":
                        src = ple_w_proj[layer].rearrange("(k p) c -> p k c", p=P)
                    else:
                        src = ple_w_gate[layer].rearrange("(i k p) c -> i p k c", p=P, k=2)[r[0]]
                prior = pos - RING
                if prior >= 0:
                    if prior in PLAN:
                        sp.wait_ge(*released(prior))
                    else:
                        looped = 0 if prior < LOOPS[1] else 1
                        sp.wait_ge(ffn.gu_ready, blocks_after(looped))
                        sp.wait_ge(ffn.down_split, blocks_after(looped) // 2)
                sp.dma_start(dst, src).then_inc(slot_in[pos % RING], 16)

            def ff_loads(views, chunk, pos0, slots, ff, block0, chunk0, prior=None):
                for i in range(2):
                    for j in range(3):
                        pos = pos0 + 3 * i + j
                        if prior is not None:
                            if prior + 3 * i + j >= 0:
                                sp.wait_ge(*released(prior + 3 * i + j))
                        elif j < 2:
                            sp.wait_ge(ff.gu_ready, block0 - FF_BLOCKS + 2 * (i + 1))
                        else:
                            sp.wait_ge(ff.down_split, chunk0 - 2 + i + 1)
                        dst = ring[:, pos % RING, :].rearrange("p (k c) -> p k c", k=NK if j < 2 else 2)
                        sp.dma_start(dst, views[j][chunk + i]).then_inc(slots[pos % RING], 16)

            def up_gate_view(w):
                return w.rearrange("(k p) (c f) -> c p k f", p=P, f=CW)

            def moe_view(w):
                return w.rearrange("e (k p) (c f) -> e c p k f", p=P, f=CW)

            def expert_views(e):
                return [moe_view(moe_w_up[0])[e], moe_view(moe_w_gate[0])[e],
                        moe_w_down[0].rearrange("e (c k p) d -> e c p k d", p=P, k=2)[e]]

            sp.dma_start(cn[:, :], const_in).then_inc(const_in_s, 16)
            sp.dma_start(x[:, :, :], x_in[0].rearrange("(t p) d -> p t d", p=P)).then_inc(x_in_s, 16)
            n = FF_BODIES[1]
            for layer in range(DEPTH):
                start = 0 if layer == 0 else WHERE[(0, "ple", 3)] + 1
                for pos in range(start, LOOPS[layer]):
                    load(pos)
                pos0 = LOOPS[layer]
                if layer == 0:
                    views = [up_gate_view(ffn_w_up[0]), up_gate_view(ffn_w_gate[0]),
                             ffn_w_down[0].rearrange("(c k p) d -> c p k d", p=P, k=2)]
                    ff_loads(views, 0, pos0, slot_in, ffn, 0, 0, prior=pos0 - RING)
                    with sp.Fori(1, FF_BODIES[0]) as c:
                        ff_loads(views, 2 * c, pos0, slot_in, ffn, FF_BLOCKS * c, 2 * c)
                else:
                    before = moe.before
                    ff_loads(expert_views(0), 0, pos0, slot_in, moe, before, moe.chunks_before, prior=pos0 - RING)
                    with sp.Fori(1, n) as c:
                        ff_loads(expert_views(0), 2 * c, pos0, slot_in, moe, FF_BLOCKS * c + before, 2 * c + moe.chunks_before)
                    with sp.Fori(1, N_EXPERTS) as e:
                        with sp.Fori(0, n) as c:
                            ff_loads(expert_views(e), 2 * c, pos0, slot_in, moe, (e * n + c) * FF_BLOCKS + before,
                                     (e * n + c) * 2 + moe.chunks_before)
                    sp.wait_ge(overflow_ready, 1)
                    more = sp.value_load(overflow[0:1, 0:1], min_val=0, max_val=1)
                    with sp.If(more > 0):
                        sp.wait_ge(ffn.gu_ready, blocks_after(1))
                        sp.wait_ge(ffn.down_done, blocks_after(1))
                        with sp.Fori(0, N_EXPERTS) as e:
                            with sp.Fori(0, n) as c:
                                ff_loads(expert_views(e), 2 * c, over_pass.pos0, over_pass.slots, over,
                                         (e * n + c) * FF_BLOCKS + over.before, (e * n + c) * 2 + over.chunks_before)
                        total_blocks = over.before + N_EXPERTS * N_MOE_BLOCKS
                        sp.wait_ge(over.gu_ready, total_blocks)
                        sp.wait_ge(over.down_done, total_blocks)
                for pos in range(WHERE[(layer, "proj")], WHERE[(layer, "ple", 3)] + 1):
                    load(pos)
            out_v = out[0].rearrange("(t p) d -> p t d", p=P)
            for t in range(NT):
                sp.wait_ge(x_done, X_COUNT(DEPTH - 1, 2, t))
                sp.dma_start(out_v[:, t, :], x[:, t, :]).then_inc(stored, 16)
            sp.wait_ge(stored, 16 * NT)

        @block.gpsimd
        def _(pool):
            step = Count(pool_step)
            gains = [g for l in range(DEPTH) for g in (mix_pre_g[l], mix_post_g[l], ffn_pre_g[l], ffn_post_g[l], ple_post_g[l])]

            def load_gain(n):
                if n >= len(gains):
                    return
                if n >= 2:
                    last_layer, last = divmod(n - 2, 5)
                    if last in (0, 2):
                        pool.wait_ge(xn_done, 2 * NT * last_layer + NT * (last // 2) + NT)
                    else:
                        pool.wait_ge(x_done, X_COUNT(last_layer, {1: 0, 3: 1, 4: 2}[last], NT - 1))
                pool.dma_start(gain[:, n % 2, :], gains[n].partition_broadcast(P)).then_inc(gain_in[n % 2], 16)

            def load_params(layer):
                if layer:
                    pool.wait_ge(staged_done, len(STAGED) * layer)
                    pool.wait_ge(ex_done, USE[(layer - 1, "kva", NT - 1)] + 1)
                    pool.wait_ge(prob_done, len(JOBS) * layer)
                    pool.wait_ge(exp_done, len(JOBS) * layer)
                pool.dma_start(gain_a[:, 0:256], a_qa_g[layer].partition_broadcast(P)).then_inc(params_in, 16)
                pool.dma_start(gain_a[:, 256:384], a_kva_g[layer].partition_broadcast(P)).then_inc(params_in, 16)
                for h in range(6):
                    g = b_q_g if h < 4 else b_k_g
                    pool.dma_start(gain_b[:, h, :], g[layer].partition_broadcast(P)).then_inc(params_in, 16)
                pool.dma_start(sink[:, :], d_sink[layer].partition_broadcast(P)).then_inc(params_in, 16)
                pool.dma_start(w_uq[:, :, :], a_w_uq[layer].rearrange("(k p) c -> p k c", p=P)).then_inc(params_in, 16)
                pool.dma_start(w_ukv[:, :], a_w_ukv[layer]).then_inc(params_in, 16)

            def stat(layer, kind, t, width=D_MODEL):
                n = STAT[(layer, kind, t)]
                pool.wait_ge(sq_done, n + 1)
                step.up(nc.gpsimd.tensor_scalar(var[:, n:n + 1], sumsq[:, n:n + 1], 1.0 / width, EPS, ALU.mult, ALU.add))
                step.wait(pool)
                nc.gpsimd.tensor_tensor(rstd[:, n:n + 1], var[:, n:n + 1], minus_half[:, 0:1], ALU.pow).then_inc(rstd_done, 1)

            load_gain(0)
            load_gain(1)
            load_params(0)
            nc.gpsimd.memset(minus_half[:, :], -0.5).then_inc(pool_step, 1)
            step.at += 1
            for t in range(NT):
                pool.dma_start(rtr_b[:, t, :], router_b[0].partition_broadcast(P)).then_inc(params_in, 16)
            pool.dma_start(rtr_w[:, :, :], router_w[0].rearrange("(k p) e -> p k e", p=P)).then_inc(params_in, 16)
            for layer in range(DEPTH):
                if layer == 0:
                    for t in range(NT):
                        stat(layer, "pre", t)
                else:
                    pool.wait_ge(x_done, X_COUNT(layer - 1, 2, NT - 1))
                nc.gpsimd.memset(kz, 0.0).then_inc(kz_zero, 1)
                step.wait(pool)
                load_gain(5 * layer + 2)
                for s in MIXER:
                    if s[0] == "norm_b":
                        pool.wait_ge(sqb_done, layer + 1)
                        fl = lambda a: a[:, :, :].rearrange("p t h -> p (t h)")
                        step.up(nc.gpsimd.tensor_scalar(fl(var_b), fl(sumsq_b), 1.0 / HD, EPS, ALU.mult, ALU.add))
                        step.wait(pool)
                        nc.gpsimd.tensor_tensor(fl(rstd_b), fl(var_b), minus_half[:, :], ALU.pow).then_inc(rstdb_done, 1)
                    if s[0] == "norm_a":
                        for kind, width in (("low_q", A_Q_RANK), ("low_kv", A_KV_RANK)):
                            for t in range(NT):
                                stat(layer, kind, t, width)
                for t in range(NT):
                    stat(layer, "post", t)
                    stat(layer, "fpre", t)
                load_gain(5 * layer + 3)
                if layer + 1 < DEPTH:
                    load_params(layer + 1)
                load_gain(5 * layer + 4)
                pool.wait_ge(mix_done, NT * (layer + 1))
                pool.wait_ge(x_done, X_COUNT(layer, 0, NT - 1))
                pool.dma_start(p_sb, p_in[layer, 0].rearrange("(t p) c -> p t c", p=P)).then_inc(p_loaded, 16)
                for t in range(NT):
                    stat(layer, "fpost", t)
                load_gain(5 * layer + 5)
                for t in range(NT):
                    stat(layer, "ple", t)
                    if layer + 1 < DEPTH:
                        stat(layer + 1, "pre", t)
                load_gain(5 * layer + 6)

        @block.tensor
        def _(pe):
            mm = nc.tensor.matmul

            def bank_for(layer, *name):
                n = USE[(layer,) + name]
                if n >= EXCHANGE:
                    pe.wait_ge(ex_done, n - EXCHANGE + 1)
                return ps[:, n % EXCHANGE, :]

            def emptied(layer, *name):
                pe.wait_ge(ex_done, USE[(layer,) + name] + 1)

            def turn_tile(layer, kind, src, t):
                for b in range(2):
                    bank = bank_for(layer, kind, t, b)
                    for i in range(4):
                        c = (4 * b + i) * P
                        m = nc.tensor.transpose(bank[:, i * P:(i + 1) * P], src[:, t, c:c + P], ident)
                    m.then_inc(ex_ready, 1)

            def swap(layer, item):
                pe.wait_ge(staged_done, len(STAGED) * layer + STAGED.index(item) + 1)
                r = staged[:, (len(STAGED) * layer + STAGED.index(item)) % 2]
                if item in ("Aq", "Ak"):
                    for u in range(2):
                        bank = bank_for(layer, "swap", item, u)
                        for h in range(2):
                            for t in range(NT):
                                c = (2 * u + h) * A_QK
                                m = nc.tensor.transpose(bank[0:A_QK, h * SEQ + t * P:h * SEQ + (t + 1) * P],
                                                        r[:, t, c:c + A_QK], ident)
                        m.then_inc(ex_ready, 1)
                    return
                if item == "An":
                    groups = [[0, 1], [2]]
                else:
                    groups = [[0]] if item in ("Bk", "Dk") else [[0, 1]]
                for u, g in enumerate(groups):
                    bank = bank_for(layer, "swap", item, u)
                    for i, b in enumerate(g):
                        for t in range(NT):
                            m = nc.tensor.transpose(bank[:, i * SEQ + t * P:i * SEQ + (t + 1) * P],
                                                    r[:, t, b * P:(b + 1) * P], ident)
                    m.then_inc(ex_ready, 1)

            def score_operands(b, h, g):
                if b == "A":
                    return qaT[0:A_QK, h, :], kaT[0:A_QK, h, :]
                if b in "BD":
                    return qT[:, h % 2, :], kz[:, h // 2, :]
                return qT[:, 2 + 2 * g + h // 2, :], kz[:, 2 + 4 * g + h, :]

            def values(b, h, g, kt):
                if b == "A":
                    return kva[:, kt, h * P + A_NOPE:(h + 1) * P]
                c = {"B": B0 + 6 * HD + (h // 2) * HD, "D": D0 + 6 * HD + (h // 2) * HD,
                     "C": C0 + g * 12 * HD + 8 * HD + h * HD}[b]
                return z[:, kt, c:c + HD]

            def feed_forward(ff, slots, pos0, loads0, body, block0, rhs, out_of, tiles, more=None):
                split = type(rhs) is tuple
                chunk0 = body * 2 + ff.chunks_before

                def gate_up(j):
                    wait_from(pe, ff.hidden_ready, block0 + j - 3)
                    if j % 2 == 0:
                        if split:
                            pe.wait_ge(up_gate_split, chunk0 * 2 + j + 2)
                        else:
                            for i in range(2):
                                pe.wait_ge(slots[(pos0 + 3 * (j // 2) + i) % RING], (loads0[3 * (j // 2) + i] + 1 + body) * 16)
                    cols = slice((j % 2) * P, (j % 2 + 1) * P)
                    for i in range(2):
                        slot = (pos0 + 3 * (j // 2) + i) % RING
                        if split:
                            hi = up_gate_hi_w[:, 2 * (j // 2) + i, :].rearrange("p (k c) -> p k c", k=NK)
                            lo = ring_lo[:, slot, :].rearrange("p (k c) -> p k c", k=NK)
                            pairs = ((hi, rhs[0]), (hi, rhs[1]), (lo, rhs[0]))
                        else:
                            pairs = ((ring[:, slot, :].rearrange("p (k c) -> p k c", k=NK), rhs),)
                        out = ps[:, j, i * SEQ:i * SEQ + pairs[0][1].shape[2]]
                        for k in range(NK):
                            for w, xs in pairs:
                                m = mm(out, w[:, k, cols], xs[:, k, :], start=(k == 0 and w is pairs[0][0] and xs is pairs[0][1]),
                                       stop=(k == NK - 1 and w is pairs[-1][0] and xs is pairs[-1][1]))
                    m.then_inc(ff.gu_ready, 1)

                def down(j, first=False, last=False):
                    pe.wait_ge(ff.hidden_ready, block0 + j + 1)
                    if j in (0, 2):
                        pe.wait_ge(ff.down_split, chunk0 + j // 2 + 1)
                    jj = j % 4
                    hi, lo = [w[:, jj // 2, :].rearrange("p (k c) -> p k c", k=2) for w in (down_hi_w, down_lo_w)]
                    for t in range(tiles):
                        for n, (a, w) in enumerate(((hidden_hi, hi), (hidden_hi, lo), (hidden_lo, hi))):
                            for half in range(2):
                                m = mm(out_of(t)[:, half, :], a[:, jj, t * P:(t + 1) * P],
                                       w[:, jj % 2, half * 512:(half + 1) * 512], start=first and n == 0, stop=last and n == 2)
                    m.then_inc(ff.down_done, 1)

                if more == "end":
                    down(-1, last=True)
                    return
                gate_up(0)
                if more is not None:
                    down(-1)
                gate_up(1)
                down(0, first=more is None)
                gate_up(2)
                down(1)
                gate_up(3)
                down(2)

            def dispatch(ps_, layer=1):
                def use(*name):
                    n = ps_.ex0 + DISPATCH[name]
                    if n >= EXCHANGE:
                        pe.wait_ge(ps_.ex_done, n - EXCHANGE + 1)
                    return ps[:, n % EXCHANGE, :]

                pe.wait_ge(ps_.picked, 1)
                bank = use("gcol")
                for e in range(8):
                    for t in range(NT):
                        m = mm(bank[:, e:e + 1], pick[:, t, e, :], weight[:, t, e:e + 1], start=(t == 0), stop=(t == NT - 1))
                m.then_inc(ps_.ex_ready, 1)
                for i in range(4):
                    bank = use("spread", i)
                    for j in range(2):
                        for t in range(NT):
                            m = nc.tensor.transpose(bank[:, j * SEQ + t * P:j * SEQ + (t + 1) * P], pick[:, t, 2 * i + j, :], ident)
                    m.then_inc(ps_.ex_ready, 1)
                for e in range(8):
                    for b in range(2):
                        bank = use("gather", e, b)
                        for i in range(4):
                            c = (4 * b + i) * P
                            for t in range(NT):
                                m = mm(bank[:, i * P:(i + 1) * P], xn[:, t, c:c + P], pick[:, t, e, :],
                                       start=(t == 0), stop=(t == NT - 1))
                        m.then_inc(ps_.ex_ready, 1)
                pe.wait_ge(ps_.ex_done, ps_.ex0 + len(DISPATCH))

            def experts(ps_):
                n, ff = FF_BODIES[1], ps_.ff
                with pe.Fori(0, N_EXPERTS) as e:
                    pe.wait_ge(ps_.cur_x_ready, e + 1)
                    y = lambda t: acc(0)
                    a = (ff, ps_.slots, ps_.pos0, ps_.loads0)
                    before = e * N_MOE_BLOCKS + ff.before
                    feed_forward(*a, e * n, before, cur_x, y, 1)
                    with pe.Fori(1, n) as c:
                        feed_forward(*a, e * n + c, before + c * FF_BLOCKS, cur_x, y, 1, more="go on")
                    feed_forward(*a, e * n + n, before + N_MOE_BLOCKS, cur_x, y, 1, more="end")
                    pe.wait_ge(ps_.ys_act, e + 1)
                    pe.wait_ge(ps_.ys_dve, e + 1)
                    pe.wait_ge(ps_.cur_s_ready, e + 1)
                    for t in (1, 0):
                        for half in range(2):
                            m = mm(acc(t)[:, half, :], cur_spread[:, t * P:(t + 1) * P],
                                   ys[:, half * 512:(half + 1) * 512], start=True, stop=True)
                        m.then_inc(ps_.back, 1)
                    pe.wait_ge(ps_.added, e * NT + NT)

            pe.wait_ge(const_in_s, 16)
            for layer in range(DEPTH):
                for t in range(NT):
                    pe.wait_ge(xn_done, 2 * NT * layer + t + 1)
                    turn_tile(layer, "pre", xn, t)
                emptied(layer, "pre", NT - 1, 1)
                for s in MIXER:
                    if s[0] == "z":
                        c, w = s[1]
                        pos = WHERE[(layer, "z", c, w)]
                        bank = bank_for(layer, "z", c)
                        loaded(pe, pos)
                        wv = slot_of(pos).rearrange("p (k c) -> p k c", k=NK)
                        for t in range(NT):
                            for k in range(NK):
                                m = mm(bank[:, t * SEQ:t * SEQ + w], hT[:, k, t * P:(t + 1) * P], wv[:, k, 0:w],
                                       start=(k == 0), stop=(k == NK - 1))
                        m.then_inc(ex_ready, 1)
                    elif s[0] == "swap":
                        swap(layer, s[1])
                    elif s[0] == "project_a":
                        emptied(layer, "swap", "An", 1)
                        pe.wait_ge(params_in, PARAMS(layer))
                        for t in range(NT):
                            bank = bank_for(layer, "qa", t)
                            for k in range(2):
                                m = mm(bank[:, 0:384], lowT[:, k, t * P:(t + 1) * P], w_uq[:, k, :], start=(k == 0), stop=(k == 1))
                            m.then_inc(ex_ready, 1)
                            bank = bank_for(layer, "kva", t)
                            mm(bank, lowT[:, 2, t * P:(t + 1) * P], w_ukv[:, :], start=True, stop=True).then_inc(ex_ready, 1)
                    elif s[0] == "score":
                        _, j, b, h = s
                        if h == 0:
                            emptied(layer, "swap", {"A": "Ak", "B": "Bk", "C": "C2k", "D": "Dk"}[b], 1 if b == "A" else 0)
                        for g in range(NSETS[b]):
                            n = SETS * layer + SET0[j] + g
                            if n >= 2:
                                pe.wait_ge(score_read, n - 1)
                            q, k = score_operands(b, h, g)
                            bank = ps[:, 4 + n % 2, :]
                            for t in range(NT):
                                m = mm(bank[:, t * SEQ:(t + 1) * SEQ], q[:, t * P:(t + 1) * P], k, start=True, stop=True)
                            m.then_inc(scored, 1)
                    elif s[0] == "turn":
                        _, j, b, h = s
                        pe.wait_ge(prob_done, len(JOBS) * layer + j + 1)
                        for g in range(NSETS[b]):
                            bank = bank_for(layer, "turn", j, g)
                            for kt in range(NT):
                                for t in range(NT):
                                    m = nc.tensor.transpose(bank[:, kt * SEQ + t * P:kt * SEQ + (t + 1) * P],
                                                            probs[:, j % 2, t, g, kt * P:(kt + 1) * P], ident)
                            m.then_inc(ex_ready, 1)
                    elif s[0] == "pv":
                        _, j, b, h = s
                        if h % 2 == 0:
                            pair = (len(JOBS) * layer + j) // 2
                            wait_from(pe, o_done, pair)
                        for g in range(NSETS[b]):
                            emptied(layer, "turn", j, g)
                            n = SETS * layer + SET0[j] + g
                            for kt in range(NT):
                                m = mm(O_BANK[(h % 2) * HD:(h % 2 + 1) * HD, :], values(b, h, g, kt), pT[:, n % NPT, kt, :],
                                       start=(g == 0 and kt == 0), stop=(g == NSETS[b] - 1 and kt == NT - 1))
                            m.then_inc(pv_done, 1)
                    elif s[0] == "fill":
                        u = s[1]
                        order, c = divmod(u, 8)
                        n = BRANCH_ID[BRANCH_ORDER[order]]
                        wait_from(pe, unit_done, UNITS * layer + u - 1)
                        bank = ps[:, 6 + u % 2, :]
                        pos = WHERE[(layer, "gate", n, c // 2)]
                        loaded(pe, pos)
                        wg = slot_of(pos).rearrange("p (k c) -> p k c", k=NK)
                        for k in range(NK):
                            mm(bank[:, 0:SEQ], wg[:, k, (c % 2) * P:(c % 2 + 1) * P], hT[:, k, :],
                               start=(k == 0), stop=(k == NK - 1))
                        pos = WHERE[(layer, "branch", n)]
                        loaded(pe, pos)
                        pe.wait_ge(o_done, len(JOBS) // 2 * layer + 2 * (order + 1))
                        wb = slot_of(pos).rearrange("p (k c) -> p k c", k=2)
                        for k in range(2):
                            m = mm(bank[:, SEQ:2 * SEQ], wb[:, k, c * P:(c + 1) * P], oT[:, 2 * n + k, :],
                                   start=(k == 0), stop=(k == 1))
                        m.then_inc(unit_ready, 1)
                pe.wait_ge(unit_done, UNITS * (layer + 1))
                for t in range(NT):
                    for i in range(4):
                        pos = WHERE[(layer, "out", i)]
                        loaded(pe, pos)
                        wo = slot_of(pos).rearrange("p (k c) -> p k c", k=2)
                        for k in range(2):
                            for half in range(2):
                                m = mm(acc(t)[:, half, :], mergedT[:, 2 * i + k, t * P:(t + 1) * P],
                                       wo[:, k, half * 512:(half + 1) * 512], start=(i == 0 and k == 0), stop=(i == 3 and k == 1))
                    m.then_inc(mix_done, 1)
                for t in range(NT):
                    pe.wait_ge(xn_done, 2 * NT * layer + NT + t + 1)
                    turn_tile(layer, "fpre", xn, t)
                emptied(layer, "fpre", NT - 1, 1)
                if layer % 2 == 0:
                    a = (ffn, slot_in, LOOPS[0], [(LOOPS[0] + j) // RING for j in range(RING)])
                    pe.wait_ge(hT_split, NT)
                    feed_forward(*a, 0, 0, (hT_hi, hT_lo), acc, NT)
                    with pe.Fori(1, FF_BODIES[0]) as c:
                        feed_forward(*a, c, c * FF_BLOCKS, (hT_hi, hT_lo), acc, NT, more="go on")
                    feed_forward(*a, FF_BODIES[0], N_FFN_BLOCKS, (hT_hi, hT_lo), acc, NT, more="end")
                else:
                    pe.wait_ge(params_in, PARAMS(layer))
                    bank = bank_for(layer, "logits")
                    for t in range(NT):
                        for k in range(NK):
                            m = mm(bank[:, t * 8:t * 8 + 8], hT[:, k, t * P:(t + 1) * P], rtr_w[:, k, :],
                                   start=(k == 0), stop=(k == NK - 1))
                    m.then_inc(ex_ready, 1)
                    pe.wait_ge(routed, 1)
                    bank = bank_for(layer, "rank")
                    mm(bank[:, 0:8], upper, chosen[:, 0, :], start=True, stop=True)
                    mm(bank[:, 8:16], ones, chosen[:, 0, :], start=True, stop=False)
                    mm(bank[:, 8:16], upper, chosen[:, 1, :], start=False, stop=True)
                    mm(bank[:, 16:24], ones, chosen[:, 0, :], start=True, stop=False)
                    mm(bank[:, 16:24], ones, chosen[:, 1, :], start=False, stop=True).then_inc(ex_ready, 1)
                    dispatch(main_pass)
                    experts(main_pass)
                    pe.wait_ge(overflow_ready, 1)
                    more = pe.value_load(overflow[0:1, 0:1], min_val=0, max_val=1)
                    with pe.If(more > 0):
                        pe.sem_inc(over.gu_ready, 4)
                        pe.sem_inc(over.down_done, 4)
                        dispatch(over_pass)
                        experts(over_pass)
                pe.wait_ge(p_loaded, 16 * (layer + 1))
                bank = bank_for(layer, "pt")
                for k in range(2):
                    for t in range(NT):
                        m = nc.tensor.transpose(bank[:, k * SEQ + t * P:k * SEQ + (t + 1) * P], p_sb[:, t, k * P:(k + 1) * P], ident)
                m.then_inc(ex_ready, 1)
                emptied(layer, "pt")
                pos = WHERE[(layer, "proj")]
                loaded(pe, pos)
                wp = slot_of(pos).rearrange("p (k c) -> p k c", k=2)
                for t in range(NT):
                    for half in range(2):
                        bank = bank_for(layer, "proj", t, half)
                        for k in range(2):
                            m = mm(bank, pleT[:, k, t * P:(t + 1) * P], wp[:, k, half * 512:(half + 1) * 512],
                                   start=(k == 0), stop=(k == 1))
                        m.then_inc(ex_ready, 1)
                for t in range(NT):
                    pe.wait_ge(x_done, X_COUNT(layer, 1, NT - 1 if layer % 2 else t))
                    turn_tile(layer, "xt", x, t)
                emptied(layer, "xt", NT - 1, 1)
                pe.wait_ge(x_done, X_COUNT(layer, 1, NT - 1))
                for t in range(NT):
                    for i in range(4):
                        pos = WHERE[(layer, "ple", i)]
                        loaded(pe, pos)
                        wg = slot_of(pos).rearrange("p (k c) -> p k c", k=2)
                        for k in range(2):
                            for half in range(2):
                                m = mm(acc(t)[:, half, :], hT[:, 2 * i + k, t * P:(t + 1) * P],
                                       wg[:, k, half * 512:(half + 1) * 512], start=(i == 0 and k == 0), stop=(i == 3 and k == 1))
                    m.then_inc(ple_done, 1)

        @block.scalar
        def _(act):
            copy, activation = nc.scalar.copy, nc.scalar.activation

            def taken(layer, *name):
                n = USE[(layer,) + name]
                act.wait_ge(ex_ready, n + 1)
                return ps[:, n % EXCHANGE, :]

            def square(which, src, rubbish):
                n = STAT[which]
                wait_from(act, sq_done, n)
                activation(rubbish, src, ACT.Square, accum_out=sumsq[:, n:n + 1]).then_inc(sq_done, 1)

            def turned_tile(layer, kind, t):
                for b in range(2):
                    bank = taken(layer, kind, t, b).rearrange("p (i s) -> p i s", i=4)
                    ins = copy(hT[:, 4 * b:4 * b + 4, t * P:(t + 1) * P], bank)
                    if kind == "fpre" and layer % 2 == 0:
                        ins = copy(hT_hi[:, 4 * b:4 * b + 4, t * P:(t + 1) * P], bank)
                    ins.then_inc(ex_done, 1)

            def swapped(layer, item):
                if item in ("Aq", "Ak"):
                    for u in range(2):
                        bank = taken(layer, "swap", item, u)
                        dst = qaT if item == "Aq" else kaT
                        copy(dst[0:A_QK, 2 * u:2 * u + 2, :], bank[0:A_QK, :].rearrange("p (h s) -> p h s", h=2)).then_inc(ex_done, 1)
                elif item == "An":
                    for u, (a, n) in enumerate(((0, 2), (2, 1))):
                        bank = taken(layer, "swap", item, u)
                        copy(lowT[:, a:a + n, :], bank[:, 0:n * SEQ].rearrange("p (h s) -> p h s", h=n)).then_inc(ex_done, 1)
                elif item[-1] == "q":
                    a = 0 if item[0] in "BD" else 2 + 2 * int(item[1])
                    bank = taken(layer, "swap", item, 0)
                    copy(qT[:, a:a + 2, :], bank.rearrange("p (h s) -> p h s", h=2)).then_inc(ex_done, 1)
                else:
                    bank = taken(layer, "swap", item, 0)
                    act.wait_ge(kz_zero, layer + 1)
                    for half in range(2):
                        r = slice(half * HD, (half + 1) * HD)
                        if item[0] in "BD":
                            ins = copy(kz[r, half, :], bank[r, 0:SEQ])
                        else:
                            a = 2 + 4 * int(item[1]) + half
                            ins = copy(kz[r, a:a + 3:2, :], bank[r, :].rearrange("p (h s) -> p h s", h=2))
                    ins.then_inc(ex_done, 1)

            def up_gate_his(pos0, i, body, chunk0):
                for n in range(2):
                    pos = pos0 + 3 * i + n
                    act.wait_ge(slot_in[pos % RING], (pos // RING + 1 + body) * 16)
                    copy(up_gate_hi_w[:, 2 * i + n, :], ring[:, pos % RING, :]).then_inc(up_gate_hi, 1)

            def silus(ff, slots, pos0, loads0, body, block0, tokens, around=None):
                for j in range(FF_BLOCKS):
                    if j % 2 == 0:
                        pos = pos0 + 3 * (j // 2) + 2
                        act.wait_ge(slots[pos % RING], (loads0[3 * (j // 2) + 2] + 1 + body) * 16)
                        wait_from(act, ff.down_done, block0 + j - 2)
                        copy(down_hi_w[:, j // 2, :], ring[:, pos % RING, :]).then_inc(ff.down_hi, 1)
                    act.wait_ge(ff.gu_ready, block0 + j + 1)
                    wait_from(act, ff.hidden_ready, block0 + j - 3)
                    activation(silu[:, j, 0:tokens], ps[:, j, SEQ:SEQ + tokens], ACT.Silu).then_inc(ff.silu_ready, 1)
                    if around:
                        around(j)

            def dispatched(ps_):
                def bank(*name):
                    n = ps_.ex0 + DISPATCH[name]
                    act.wait_ge(ps_.ex_ready, n + 1)
                    return ps[:, n % EXCHANGE, :]

                copy(gcol, bank("gcol")[:, 0:8]).then_inc(ps_.ex_done, 1)
                for i in range(4):
                    copy(spread[:, 2 * i:2 * i + 2, :], bank("spread", i).rearrange("p (e s) -> p e s", e=2)).then_inc(ps_.ex_done, 1)
                for e in range(8):
                    for b in range(2):
                        copy(xg[:, e, b * 512:(b + 1) * 512], bank("gather", e, b)).then_inc(ps_.ex_done, 1)

            def expert_silus(ps_):
                n, ff = FF_BODIES[1], ps_.ff
                with act.Fori(0, N_EXPERTS) as e:
                    with act.Fori(0, n) as c:
                        silus(ff, ps_.slots, ps_.pos0, ps_.loads0, e * n + c, (e * n + c) * FF_BLOCKS + ff.before, CAP)
                    act.wait_ge(ff.down_done, (e + 1) * N_MOE_BLOCKS + ff.before)
                    act.wait_ge(ps_.cur_s_ready, e + 1)
                    activation(ys[:, 0:512], acc(0)[:, 0, :], ACT.Copy, scale=cur_g).then_inc(ps_.ys_act, 1)

            act.wait_ge(x_in_s, 16)
            for layer in range(DEPTH):
                if layer == 0:
                    for t in range(NT):
                        square((layer, "pre", t), x[:, t, :], junk)
                for t in range(NT):
                    turned_tile(layer, "pre", t)
                for s in MIXER:
                    if s[0] == "z":
                        c, w = s[1]
                        bank = taken(layer, "z", c)
                        copy(z[:, :, c:c + w], bank.rearrange("p (t s) -> p t s", t=NT)[:, :, 0:w]).then_inc(ex_done, 1)
                    elif s[0] == "norm_a":
                        act.wait_ge(ex_done, USE[(layer, "z", A0 + 256)] + 1)
                        for kind, a, width in (("low_q", 0, A_Q_RANK), ("low_kv", A_Q_RANK, A_KV_RANK)):
                            for t in range(NT):
                                square((layer, kind, t), z[:, t, a:a + width], egate[:, 0, 0:width])
                    elif s[0] == "swap":
                        swapped(layer, s[1])
                    elif s[0] == "project_a":
                        for t in range(NT):
                            bank = taken(layer, "qa", t)
                            if t == 0:
                                act.wait_ge(ex_ready, USE[(layer, "kva", 0)] + 1)
                            copy(qa_sb[:, t, :], bank[:, 0:384]).then_inc(ex_done, 1)
                            bank = taken(layer, "kva", t)
                            copy(kva[:, t, :], bank).then_inc(ex_done, 1)
                    elif s[0] == "score":
                        _, j, b, h = s
                        n, i = len(JOBS) * layer + j, j % 2
                        scale = (A_QK if b == "A" else HD) ** -0.5
                        act.wait_ge(bias_done, n + 1)
                        for t in range(NT):
                            e = probs[:, i, t, 0:NSETS[b], :]
                            ins = activation(e, e, ACT.Exp, bias=bias[:, i, t:t + 1], scale=scale, accum_out=total[:, i, t:t + 1])
                        if b == "D":
                            ins = activation(sunk[:, i, :], bias[:, i, :], ACT.Exp, bias=sink[:, h:h + 1])
                        ins.then_inc(exp_done, 1)
                    elif s[0] == "turn":
                        _, j, b, h = s
                        for g in range(NSETS[b]):
                            bank = taken(layer, "turn", j, g)
                            n = SETS * layer + SET0[j] + g
                            wait_from(act, pv_done, n - NPT + 1)
                            copy(pT[:, n % NPT, :, :], bank.rearrange("p (k s) -> p k s", k=NT)).then_inc(ex_done, 1)
                    elif s[0] == "pv" and s[3] % 2:
                        _, j, b, h = s
                        act.wait_ge(pv_done, SETS * layer + SET0[j + 1])
                        copy(oT[:, 2 * BRANCH_ID[b] + h // 2, :], O_BANK).then_inc(o_done, 1)
                    elif s[0] == "fill":
                        u = s[1]
                        act.wait_ge(unit_ready, UNITS * layer + u + 1)
                        wait_from(act, unit_done, UNITS * layer + u - 1)
                        activation(egate[:, u % 2, :], ps[:, 6 + u % 2, 0:SEQ], ACT.Exp, scale=-1.0).then_inc(egate_done, 1)
                for t in range(NT):
                    act.wait_ge(mix_done, NT * layer + t + 1)
                    square((layer, "post", t), acc(t).rearrange("p b c -> p (b c)"), junk)
                    act.wait_ge(x_done, X_COUNT(layer, 0, t))
                    square((layer, "fpre", t), x[:, t, :], junk)
                for t in range(NT):
                    turned_tile(layer, "fpre", t)
                if layer % 2 == 0:
                    n, pos0 = FF_BODIES[0], LOOPS[0]
                    loads0 = [(pos0 + j) // RING for j in range(RING)]

                    def dense(c, last=False):
                        def around(j):
                            if j == 0:
                                up_gate_his(pos0, 1, c, 2 * c)
                            if j == 2 and not last:
                                up_gate_his(pos0, 0, c + 1, 2 * c + 2)
                        silus(ffn, slot_in, pos0, loads0, c, c * FF_BLOCKS, SEQ, around)

                    up_gate_his(pos0, 0, 0, 0)
                    dense(0)
                    with act.Fori(1, n - 1) as c:
                        dense(c)
                    dense(n - 1, last=True)
                    act.wait_ge(ffn.down_done, N_FFN_BLOCKS)
                    for t in range(NT):
                        square((layer, "fpost", t), acc(t).rearrange("p b c -> p (b c)"), junk)
                else:
                    bank = taken(layer, "logits")
                    copy(lg, bank[:, 0:NT * 8].rearrange("p (t e) -> p t e", t=NT)).then_inc(ex_done, 1)
                    act.wait_ge(route_exp_in, 1)
                    activation(rt[:, 3, :], rt[:, 2, :], ACT.Exp).then_inc(route_exp, 1)
                    bank = taken(layer, "rank")
                    copy(rank, bank[:, 0:24].rearrange("p (t e) -> p t e", t=3)).then_inc(ex_done, 1)
                    dispatched(main_pass)
                    expert_silus(main_pass)
                    act.wait_ge(overflow_ready, 1)
                    more = act.value_load(overflow[0:1, 0:1], min_val=0, max_val=1)
                    with act.If(more > 0):
                        act.sem_inc(over.silu_ready, 4)
                        act.sem_inc(over.down_hi, 2)
                        dispatched(over_pass)
                        expert_silus(over_pass)
                    act.wait_ge(moe_done, 1)
                    for t in range(NT):
                        square((layer, "fpost", t), fsum[:, t, :], junk)
                bank = taken(layer, "pt")
                copy(pleT, bank.rearrange("p (k s) -> p k s", k=2)).then_inc(ex_done, 1)
                for t in range(NT):
                    for half in range(2):
                        bank = taken(layer, "proj", t, half)
                        copy(proj[:, t, half * 512:(half + 1) * 512], bank).then_inc(ex_done, 1)
                for t in range(NT):
                    turned_tile(layer, "xt", t)
                for t in range(NT):
                    act.wait_ge(ple_done, NT * layer + t + 1)
                    activation(xn[:, t, :], acc(t).rearrange("p b c -> p (b c)"), ACT.Exp, scale=-1.0).then_inc(ple_exp, 1)
                    act.wait_ge(ple_prod, NT * layer + t + 1)
                    square((layer, "ple", t), xn[:, t, :], junk)
                    if layer + 1 < DEPTH:
                        act.wait_ge(x_done, X_COUNT(layer, 2, t))
                        square((layer + 1, "pre", t), x[:, t, :], junk)

        @block.vector
        def _(dve):
            step = Count(dve_step)
            v = nc.vector

            def link(ins, s=None):
                s = s or step
                s.up(ins)
                s.wait(dve)

            def normed(layer, kind, g, t):
                n, k = 5 * layer + g, STAT[(layer, kind, t)]
                dve.wait_ge(gain_in[n % 2], 16 * (n // 2 + 1))
                dve.wait_ge(rstd_done, k + 1)
                v.scalar_tensor_tensor(out=xn[:, t, :], in0=x[:, t, :], scalar=rstd[:, k:k + 1], in1=gain[:, n % 2, :],
                                       op0=ALU.mult, op1=ALU.mult).then_inc(xn_done, 1)

            def residual(layer, kind, g, t, src, tmp):
                n, k = 5 * layer + g, STAT[(layer, kind, t)]
                dve.wait_ge(gain_in[n % 2], 16 * (n // 2 + 1))
                dve.wait_ge(rstd_done, k + 1)
                link(v.scalar_tensor_tensor(out=tmp, in0=src, scalar=rstd[:, k:k + 1], in1=gain[:, n % 2, :],
                                            op0=ALU.mult, op1=ALU.mult))
                v.tensor_tensor(x[:, t, :], x[:, t, :], tmp, ALU.add).then_inc(x_done, 1)

            def rotate(src, dst, table, t, heads, groups):
                width = src.shape[2]
                half = width // groups // 2
                n = heads * width
                cos, sin = tab[table][:, 0, t, :], tab[table][:, 1, t, :]
                a = rot[:, 0, 0:n].rearrange("p (h d) -> p h d", h=heads)
                b = rot[:, 1, 0:n].rearrange("p (h d) -> p h d", h=heads)
                link(v.tensor_tensor(a, src, cos.unsqueeze(1).broadcast_to([P, heads, width]), ALU.mult))
                for g in range(groups):
                    for i in range(2):
                        to = slice((2 * g + i) * half, (2 * g + i + 1) * half)
                        of = slice((2 * g + 1 - i) * half, (2 * g + 2 - i) * half)
                        link(v.tensor_tensor(b[:, :, to], src[:, :, of], sin[:, to].unsqueeze(1).broadcast_to([P, heads, half]), ALU.mult))
                if dst is None:
                    return a, b
                return v.tensor_tensor(dst, a, b, ALU.add)

            def stage(layer, item):
                i = STAGED.index(item)
                n = len(STAGED) * layer + i
                if n >= 2:
                    l0, last = divmod(n - 2, len(STAGED))
                    name = STAGED[last]
                    dve.wait_ge(ex_ready, USE[(l0, "swap", name, 1 if name[0] == "A" else 0)] + 1)
                wait_from(dve, staged_done, n)
                return staged[:, n % 2]

            def rope(layer, item):
                r = stage(layer, item)
                b = item[0]
                if b == "A":
                    for t in range(NT):
                        rv = r[:, t, :].rearrange("p (h d) -> p h d", h=A_HEADS)
                        if item == "Aq":
                            if t == 0:
                                dve.wait_ge(ex_done, USE[(layer, "kva", NT - 1)] + 1)
                            src = qa_sb[:, t, :].rearrange("p (h d) -> p h d", h=A_HEADS)
                            link(rotate(src[:, :, A_NOPE:A_QK], rv[:, :, A_NOPE:A_QK], "a", t, A_HEADS, 1))
                            last = v.tensor_copy(rv[:, :, 0:A_NOPE], src[:, :, 0:A_NOPE])
                        else:
                            src = z[:, t, A_Q_RANK + A_KV_RANK:B0].unsqueeze(1)
                            one, two = rotate(src, None, "a", t, 1, 1)
                            link(v.tensor_tensor(rv[:, :, A_NOPE:A_QK], one.broadcast_to([P, A_HEADS, A_ROPE]),
                                                 two.broadcast_to([P, A_HEADS, A_ROPE]), ALU.add))
                            last = v.tensor_copy(rv[:, :, 0:A_NOPE],
                                                 kva[:, t, :].rearrange("p (h d) -> p h d", h=A_HEADS)[:, :, 0:A_NOPE])
                        if t == 0:
                            link(last)
                    last.then_inc(staged_done, 1)
                    return
                heads = 4 if item[-1] == "q" or b == "C" else 2
                if b == "C":
                    col = C0 + int(item[1]) * 12 * HD + (4 * HD if item[2] == "k" else 0)
                    dve.wait_ge(ex_done, USE[(layer, "z", col)] + 1)
                else:
                    col = (B0 if b == "B" else D0) + (4 * HD if item[1] == "k" else 0)
                    if b == "D":
                        dve.wait_ge(ex_done, USE[(layer, "z", D0 + 256)] + 1)
                for t in range(NT):
                    src = z[:, t, col:col + heads * HD].rearrange("p (h d) -> p h d", h=heads)
                    one, two = rotate(src, None, "axial" if b == "B" else "full", t, heads, 2 if b == "B" else 1)
                    dst = r[:, t, 0:heads * HD]
                    if b in "BD" and heads == 4:
                        dst = dst.rearrange("p (b x d) -> p x b d", b=2, x=2)
                        one = one.rearrange("p (x b) d -> p x b d", x=2)
                        two = two.rearrange("p (x b) d -> p x b d", x=2)
                    else:
                        dst = dst.rearrange("p (h d) -> p h d", h=heads)
                    last = v.tensor_tensor(dst, one, two, ALU.add)
                    if t == 0:
                        link(last)
                last.then_inc(staged_done, 1)

            def softmax(layer, j, b, h):
                i, n = j % 2, len(JOBS) * layer + j
                scale = (A_QK if b == "A" else HD) ** -0.5
                if n >= 2:
                    l0, jj = divmod(n - 2, len(JOBS))
                    dve.wait_ge(ex_ready, USE[(l0, "turn", jj, NSETS[JOBS[jj][0]] - 1)] + 1)
                for g in range(NSETS[b]):
                    k = SETS * layer + SET0[j] + g
                    dve.wait_ge(scored, k + 1)
                    for t in range(NT):
                        s = ps[:, 4 + k % 2, t * SEQ:(t + 1) * SEQ]
                        e, m = probs[:, i, t, g, :], peak[:, i, t, g:g + 1]
                        if b in "AB":
                            ins = v.tensor_scalar(e, s, 1.0, None, ALU.mult, ALU.max, accum_out=m)
                        else:
                            ins = v.tensor_tensor_reduce(out=e, in0=s, in1=mask[:, g if b == "C" else 3, t, :], scale=1.0,
                                                         scalar=-3.0e38, op0=ALU.add, op1=ALU.max, accum_out=m)
                    ins.then_inc(score_read, 1)
                dve.wait_ge(score_read, SETS * layer + SET0[j + 1])
                src = peak[:, i, :, 0]
                if b == "C":
                    link(v.tensor_reduce(top[:, i, :], peak[:, i, :, :], AX.X, ALU.max))
                    src = top[:, i, :]
                if b == "D":
                    link(v.tensor_scalar(top[:, i, :], src, scale, sink[:, h:h + 1], ALU.mult, ALU.max))
                    v.tensor_scalar(bias[:, i, :], top[:, i, :], -1.0, None, ALU.mult).then_inc(bias_done, 1)
                else:
                    v.tensor_scalar(bias[:, i, :], src, -scale, None, ALU.mult).then_inc(bias_done, 1)
                dve.wait_ge(exp_done, n + 1)
                if b == "D":
                    link(v.tensor_tensor(total[:, i, :], total[:, i, :], sunk[:, i, :], ALU.add))
                link(v.reciprocal(inv[:, i, :], total[:, i, :]))
                for t in range(NT):
                    e = probs[:, i, t, 0:NSETS[b], :]
                    ins = v.tensor_scalar(e, e, inv[:, i, t:t + 1], None, ALU.mult)
                ins.then_inc(prob_done, 1)

            def up_gate_los(pos0, i, body):
                for n in range(2):
                    pos = pos0 + 3 * i + n
                    dve.wait_ge(up_gate_hi, 4 * body + 2 * i + n + 1)
                    v.tensor_tensor(ring_lo[:, pos % RING, :], ring[:, pos % RING, :], up_gate_hi_w[:, 2 * i + n, :], ALU.subtract)\
                        .then_inc(up_gate_split, 1)

            def hiddens(ff, pos0, body, block0, tokens, around=None):
                for j in range(FF_BLOCKS):
                    if j % 2 == 0:
                        pos = pos0 + 3 * (j // 2) + 2
                        dve.wait_ge(ff.down_hi, body * 2 + (ff.chunks_before + j // 2 + 1))
                        wait_from(dve, ff.down_done, block0 + j - 2)
                        v.tensor_tensor(down_lo_w[:, j // 2, :], ring[:, pos % RING, :], down_hi_w[:, j // 2, :], ALU.subtract)\
                            .then_inc(ff.down_split, 1)
                    h, hi, lo = hidden[:, j % 2, 0:tokens], hidden_hi[:, j, 0:tokens], hidden_lo[:, j, 0:tokens]
                    dve.wait_ge(ff.silu_ready, block0 + j + 1)
                    wait_from(dve, ff.down_done, block0 + j - 3)
                    wait_from(dve, ff.hidden_ready, block0 + j)
                    v.tensor_tensor(h, silu[:, j, 0:tokens], ps[:, j, 0:tokens], ALU.mult).then_inc(ff.step, 1)
                    steps = block0 * 2 + 2 * j
                    dve.wait_ge(ff.step, steps + 1)
                    v.tensor_copy(hi, h).then_inc(ff.step, 1)
                    dve.wait_ge(ff.step, steps + 2)
                    v.tensor_tensor(lo, h, hi, ALU.subtract).then_inc(ff.hidden_ready, 1)
                    if around:
                        around(j)

            def route():
                bc = lambda a: a.unsqueeze(2).broadcast_to([P, NT, 8])
                r = lambda n: rt[:, n, :]
                dve.wait_ge(ex_done, USE[(1, "logits")] + 1)
                link(v.tensor_tensor(lg, lg, rtr_b[:, :, :], ALU.add))
                for n, onehot in enumerate((first, second)):
                    link(v.tensor_reduce(r(n), lg, AX.X, ALU.max))
                    link(v.tensor_tensor(eq, lg, bc(r(n)), ALU.is_equal))
                    link(v.tensor_scalar(eq, eq, -100.0, 100.0, ALU.mult, ALU.add))
                    link(v.tensor_tensor(idx, eq, iota8, ALU.add))
                    link(v.tensor_reduce(r(4), idx, AX.X, ALU.min))
                    link(v.tensor_tensor(onehot, idx, bc(r(4)), ALU.is_equal))
                    if n == 0:
                        link(v.scalar_tensor_tensor(out=lg, in0=onehot, scalar=-3.0e38, in1=lg, op0=ALU.mult, op1=ALU.add))
                v.tensor_tensor(r(2), r(1), r(0), ALU.subtract).then_inc(route_exp_in, 1)
                dve.wait_ge(route_exp, 1)
                link(v.tensor_scalar(r(5), r(3), 1.0, None, ALU.add))
                link(v.reciprocal(r(6), r(5)))
                link(v.tensor_tensor(r(7), r(3), r(6), ALU.mult))
                link(v.tensor_tensor(weight, first, bc(r(6)), ALU.mult))
                link(v.tensor_tensor(eq, second, bc(r(7)), ALU.mult))
                link(v.tensor_tensor(weight, weight, eq, ALU.add))
                v.tensor_tensor(chosen, first, second, ALU.add).then_inc(routed, 1)
                dve.wait_ge(ex_done, USE[(1, "rank")] + 1)
                link(v.tensor_scalar(overflow_f, rank[:, 2, :], float(CAP), None, ALU.is_gt))
                link(v.tensor_reduce(r(0)[:, 0:1], overflow_f, AX.X, ALU.max))
                v.tensor_copy(overflow[:, :], r(0)[:, 0:1]).then_inc(overflow_ready, 1)

            def picks(ps_):
                for t in range(NT):
                    for e in range(8):
                        ins = v.tensor_scalar(pick[:, t, e, :], iota, rank[:, t, e:e + 1], chosen[:, t, e:e + 1], ALU.is_equal, ALU.mult)
                ins.then_inc(ps_.picked, 1)

            def expert_hiddens(ps_):
                n, ff = FF_BODIES[1], ps_.ff
                flat = cur_x.rearrange("p k n -> p (k n)")
                dve.wait_ge(ps_.ex_done, ps_.ex0 + len(DISPATCH))
                v.tensor_copy(flat, xg[:, 0, :]).then_inc(ps_.cur_x_ready, 1)
                with dve.Fori(0, N_EXPERTS) as e:
                    v.tensor_copy(cur_spread, spread[:, e, :])
                    v.tensor_copy(cur_g, gcol[:, bass.ds(e, 1)]).then_inc(ps_.cur_s_ready, 1)
                    with dve.Fori(0, n) as c:
                        hiddens(ff, ps_.pos0, e * n + c, (e * n + c) * FF_BLOCKS + ff.before, CAP)
                    dve.wait_ge(ff.gu_ready, (e + 1) * N_MOE_BLOCKS + ff.before)
                    dve.wait_ge(ps_.cur_x_ready, e + 1)
                    v.tensor_copy(flat, xg[:, (e + 1) % N_EXPERTS, :]).then_inc(ps_.cur_x_ready, 1)
                    dve.wait_ge(ff.down_done, (e + 1) * N_MOE_BLOCKS + ff.before)
                    dve.wait_ge(ps_.cur_s_ready, e + 1)
                    v.tensor_scalar(ys[:, 512:1024], acc(0)[:, 1, :], cur_g, None, ALU.mult).then_inc(ps_.ys_dve, 1)
                    for i, t in enumerate((1, 0)):
                        dve.wait_ge(ps_.back, e * NT + i + 1)
                        v.tensor_tensor(fsum[:, t, :], fsum[:, t, :], acc(t).rearrange("p b c -> p (b c)"), ALU.add)\
                            .then_inc(ps_.added, 1)
                    dve.wait_ge(ps_.added, e * NT + NT)

            dve.wait_ge(x_in_s, 16)
            dve.wait_ge(const_in_s, 16)
            for layer in range(DEPTH):
                if layer == 0:
                    for t in range(NT):
                        normed(layer, "pre", 0, t)
                for s in MIXER:
                    if s[0] == "norm_b":
                        dve.wait_ge(ex_done, USE[(layer, "z", B0 + 256)] + 1)
                        dve.wait_ge(params_in, PARAMS(layer))
                        for t in range(NT):
                            q = z[:, t, B0:B0 + 6 * HD]
                            link(v.tensor_tensor(rot[:, 0, :], q, q, ALU.mult))
                            ins = v.tensor_reduce(sumsq_b[:, t, :], rot[:, 0, :].rearrange("p (h d) -> p h d", h=6), AX.X, ALU.add)
                            if t == 0:
                                link(ins)
                        ins.then_inc(sqb_done, 1)
                        dve.wait_ge(rstdb_done, layer + 1)
                        for t in range(NT):
                            q = z[:, t, B0:B0 + 6 * HD].rearrange("p (h d) -> p h d", h=6)
                            link(v.tensor_tensor(q, q, rstd_b[:, t, :].unsqueeze(2).broadcast_to([P, 6, HD]), ALU.mult))
                            link(v.tensor_tensor(q, q, gain_b[:, :, :], ALU.mult))
                    elif s[0] == "norm_a":
                        r = stage(layer, "An")
                        for t in range(NT):
                            for kind, a, w in (("low_q", 0, A_Q_RANK), ("low_kv", A_Q_RANK, A_KV_RANK)):
                                k = STAT[(layer, kind, t)]
                                dve.wait_ge(rstd_done, STAT[(layer, "low_kv", NT - 1)] + 1)
                                ins = v.scalar_tensor_tensor(out=r[:, t, a:a + w], in0=z[:, t, a:a + w], scalar=rstd[:, k:k + 1],
                                                             in1=gain_a[:, a:a + w], op0=ALU.mult, op1=ALU.mult)
                        ins.then_inc(staged_done, 1)
                    elif s[0] == "rope":
                        rope(layer, s[1])
                    elif s[0] == "score":
                        softmax(layer, *s[1:])
                    elif s[0] == "fill":
                        u = s[1]
                        n, c = UNITS * layer + u, u % 8
                        e = egate[:, u % 2, :]
                        dve.wait_ge(egate_done, n + 1)
                        link(v.tensor_scalar(e, e, 1.0, None, ALU.add))
                        link(v.reciprocal(e, e))
                        up = ps[:, 6 + u % 2, SEQ:2 * SEQ]
                        if u < 8:
                            v.tensor_tensor(mergedT[:, c, :], up, e, ALU.mult).then_inc(unit_done, 1)
                        else:
                            link(v.tensor_tensor(e, up, e, ALU.mult))
                            v.tensor_tensor(mergedT[:, c, :], mergedT[:, c, :], e, ALU.add).then_inc(unit_done, 1)
                flat = lambda t: acc(t).rearrange("p b c -> p (b c)")
                for t in range(NT):
                    residual(layer, "post", 1, t, flat(t), post_tmp[:, t, :])
                    dve.wait_ge(mix_done, NT * (layer + 1))
                    normed(layer, "fpre", 2, t)
                if layer % 2 == 0:
                    for t in range(NT):
                        dve.wait_ge(ex_done, USE[(layer, "fpre", t, 1)] + 1)
                        cols = slice(t * P, (t + 1) * P)
                        v.tensor_tensor(hT_lo[:, :, cols], hT[:, :, cols], hT_hi[:, :, cols], ALU.subtract).then_inc(hT_split, 1)
                    n, pos0 = FF_BODIES[0], LOOPS[0]

                    def dense(c, last=False):
                        def around(j):
                            if j == 0:
                                up_gate_los(pos0, 1, c)
                            if j == 2 and not last:
                                up_gate_los(pos0, 0, c + 1)
                        hiddens(ffn, pos0, c, c * FF_BLOCKS, SEQ, around)

                    up_gate_los(pos0, 0, 0)
                    dense(0)
                    with dve.Fori(1, n - 1) as c:
                        dense(c)
                    dense(n - 1, last=True)
                    for t in range(NT):
                        residual(layer, "fpost", 3, t, flat(t), post_tmp[:, t, :])
                else:
                    route()
                    link(v.memset(fsum, 0.0))
                    dve.wait_ge(overflow_ready, 1)
                    picks(main_pass)
                    expert_hiddens(main_pass)
                    more = dve.value_load(overflow[0:1, 0:1], min_val=0, max_val=1)
                    with dve.If(more > 0):
                        dve.sem_inc(over.hidden_ready, 4)
                        dve.sem_inc(over.step, 8)
                        dve.sem_inc(over.down_split, 2)
                        v.tensor_scalar(rank, rank, float(-CAP), None, ALU.add).then_inc(over_ranked, 1)
                        dve.wait_ge(over_ranked, 1)
                        picks(over_pass)
                        expert_hiddens(over_pass)
                    v.memset(overflow_f, 0.0).then_inc(moe_done, 1)
                    for t in range(NT):
                        residual(layer, "fpost", 3, t, fsum[:, t, :], xn[:, t, :])
                for t in range(NT):
                    n = NT * layer + t
                    dve.wait_ge(ple_exp, n + 1)
                    e = xn[:, t, :]
                    link(v.tensor_scalar(e, e, 1.0, None, ALU.add))
                    link(v.reciprocal(e, e))
                    v.tensor_tensor(e, e, proj[:, t, :], ALU.mult).then_inc(ple_prod, 1)
                    residual(layer, "ple", 4, t, e, post_tmp[:, t, :])
                    if layer + 1 < DEPTH:
                        normed(layer + 1, "pre", 0, t)


_INS = ["x", "p", "w_in", "a_qa_g", "a_kva_g", "a_w_uq", "a_w_ukv", "b_q_g", "b_k_g", "d_sink", "w_branch", "w_out",
        "mix_pre_g", "mix_post_g", "ffn_pre_g", "ffn_post_g", "ffn_w_gate", "ffn_w_up", "ffn_w_down",
        "router_w", "router_b", "moe_w_gate", "moe_w_up", "moe_w_down", "ple_w_proj", "ple_w_gate", "ple_post_g"]


def kernel(**inputs):
    import concourse.bacc as bacc
    from concourse.bass_utils import run_bass_kernel_spmd as run

    nc = bacc.Bacc("TRN2", target_bir_lowering=False, num_devices=1)
    arrays, args = {}, []
    for name in _INS:
        a = np.ascontiguousarray(inputs[name])
        arrays[f"in_{name}_dram"] = a
        args.append(nc.dram_tensor(f"in_{name}_dram", a.shape, mybir.dt.from_np(a.dtype), kind="ExternalInput").ap())
    arrays["in_const_dram"] = constants()
    args.append(nc.dram_tensor("in_const_dram", (P, CONST_W), F32, kind="ExternalInput").ap())
    args.append(nc.dram_tensor("out_0_dram", (1, SEQ, D_MODEL), F32, kind="ExternalOutput").ap())
    trunk(nc, args)
    r = run(nc, [arrays], core_ids=[0])
    return r.results[0]["out_0_dram"]
```

```python
from contextlib import ExitStack

import numpy as np

import concourse.bass as bass
from concourse import mybir

ALU = mybir.AluOpType
ACT = mybir.ActivationFunctionType
AX = mybir.AxisListType
F32 = mybir.dt.float32
F32R = mybir.dt.float32r
I32 = mybir.dt.int32

P = 128
D_MODEL, SEQ, DEPTH = 1024, 256, 2
NT = SEQ // P
NK = D_MODEL // P
HD = 64
GRID_W, ROPE_THETA = 64, 10000.0
EPS, MASKED = 1e-6, -1e30
A_Q_RANK, A_KV_RANK, A_ROPE, A_NOPE, A_HEADS = 256, 128, 32, 64, 4
A_QK = A_NOPE + A_ROPE
PATTERNS = ((128, 1), (512, 4), (2048, 16))
D_HALF_WINDOW = 128
A0 = 0
B0 = A_Q_RANK + A_KV_RANK + A_ROPE
C0 = B0 + 8 * HD
D0 = C0 + len(PATTERNS) * 12 * HD
GATE0 = D0 + 8 * HD
D_FF, MOE_FF, N_EXPERTS = 4096, 3584, 8
CAP = P
PLE_DIM = 256

RING = 6
SLOT = 2048
WORK = 26176
CW = SLOT // NK
ECW = 2 * CW

CONST_FIELDS = (("ident", P), ("upper", P), ("ones", P), ("iota", P), ("iota8", NT * 8),
                ("mask", 4 * NT * SEQ), ("full", 2 * NT * HD), ("axial", 2 * NT * HD), ("rope_a", 2 * NT * A_ROPE))
CONST_AT, _n = {}, 0
for _name, _w in CONST_FIELDS:
    CONST_AT[_name] = _n
    _n += _w
CONST_W = _n


def constants():
    c = np.zeros((P, CONST_W), np.float32)

    def put(name, a):
        c[:, CONST_AT[name]:CONST_AT[name] + a.reshape(P, -1).shape[1]] = a.reshape(P, -1)

    p = np.arange(P)
    put("ident", np.eye(P, dtype=np.float32))
    put("upper", (p[:, None] < p[None, :]).astype(np.float32))
    put("ones", np.ones((P, P), np.float32))
    put("iota", np.broadcast_to(p.astype(np.float32), (P, P)))
    put("iota8", np.broadcast_to(np.tile(np.arange(8, dtype=np.float32), NT), (P, NT * 8)))
    q = (np.arange(NT)[None, :] * P + p[:, None])[:, :, None]
    k = np.arange(SEQ)[None, None, :]
    masks = []
    for window, dil in PATTERNS:
        masks.append((q % dil == k % dil) & (np.abs(q - k) <= window // 2))
    masks.append(np.abs(q - k) <= D_HALF_WINDOW)
    put("mask", np.stack([np.where(m, 0.0, MASKED) for m in masks], 1).astype(np.float32))

    def table(pos, dim):
        half = dim // 2
        inv = np.power(np.float32(ROPE_THETA), -np.arange(half, dtype=np.float32) / np.float32(half))
        ang = pos.astype(np.float32)[..., None] * inv.astype(np.float32)
        cos, sin = np.cos(ang.astype(np.float64)), np.sin(ang.astype(np.float64))
        return np.concatenate([cos, cos], -1), np.concatenate([-sin, sin], -1)

    pos = np.arange(NT)[None, :] * P + p[:, None]
    put("full", np.stack(table(pos, HD), 1).astype(np.float32))
    row, col = table(pos // GRID_W, HD // 2), table(pos % GRID_W, HD // 2)
    put("axial", np.stack([np.concatenate([row[i], col[i]], -1) for i in range(2)], 1).astype(np.float32))
    put("rope_a", np.stack(table(pos, A_ROPE), 1).astype(np.float32))
    return c


BRANCH_ORDER = "BADC"
BRANCH_ID = {"A": 0, "B": 1, "C": 2, "D": 3}
WIDE_Z = [(B0, 512), (A0, B0 - A0), (D0, 512), (C0, 512)]
NARROW_Z = [(c, 256) for c in range(C0 + 512, D0, 256)]


def mixer_steps():
    zn = [("z", s) for s in NARROW_Z]
    steps = [("z", s) for s in WIDE_Z] + [("norm_b",), ("rope", "Bq"), ("rope", "Bk"), zn[0]]
    steps += [("swap", "Bq"), ("swap", "Bk"), ("norm_a",), zn[1], ("swap", "An")]
    fillers = {("B", 0): [zn[2], ("project_a",), zn[3]], ("B", 1): zn[4:5], ("B", 2): zn[5:6], ("B", 3): zn[6:7]}
    staged = {("B", 1): "Aq", ("B", 2): "Ak", ("B", 3): "C0q", ("A", 0): "Dq", ("A", 1): "Dk", ("A", 2): "C0k",
              ("A", 3): "C1q", ("D", 0): "C1k", ("D", 1): "C2q", ("D", 2): "C2k"}
    heads = [(b, h) for b in BRANCH_ORDER for h in range(4)]
    fill = 0
    steps += [("score", 0) + heads[0]]
    for j, (b, h) in enumerate(heads):
        item = staged.get((b, h))
        if item:
            steps += [("rope", item)]
        if b == "B":
            steps += fillers[(b, h)]
        else:
            steps += [("fill", fill), ("fill", fill + 1)]
            fill += 2
        steps += [("turn", j, b, h)]
        last_of_branch = h == 3
        if not last_of_branch:
            steps += [("score", j + 1) + heads[j + 1]]
        steps += [("pv", j, b, h)]
        if item:
            steps += [("swap", item)]
        if last_of_branch and j + 1 < len(heads):
            steps += [("score", j + 1) + heads[j + 1]]
    steps += [("fill", u) for u in range(fill, 32)]
    return steps


MIXER = mixer_steps()
NSETS = {"A": 1, "B": 1, "C": 3, "D": 1}
JOBS = [(s[2], s[3]) for s in MIXER if s[0] == "score"]
SET0 = [sum(NSETS[b] for b, _ in JOBS[:j]) for j in range(len(JOBS) + 1)]
SETS = SET0[-1]
UNITS = 32
OUT_SPLITS = (25, 27, 29)
STAGED = [s[1] for s in MIXER if s[0] == "rope" or s == ("swap", "An")]


def statistics():
    order = [(0, "pre", t) for t in range(NT)]
    for layer in range(DEPTH):
        order += [(layer, kind, t) for kind in ("low_q", "low_kv") for t in range(NT)]
        order += [(layer, kind, t) for t in range(NT) for kind in ("post", "fpre")]
        order += [(layer, "fpost", t) for t in range(NT)]
        for t in range(NT):
            order += [(layer, "ple", t)] + ([(layer + 1, "pre", t)] if layer + 1 < DEPTH else [])
    return {k: n for n, k in enumerate(order)}


STAT = statistics()


def exchange_uses():
    uses = []

    def add(layer, *name):
        uses.append((layer,) + name)

    for layer in range(DEPTH):
        for s in MIXER:
            if s[0] == "z":
                for t in range(NT if s[1] in WIDE_Z else 1):
                    add(layer, "z", s[1][0], t)
            elif s[0] == "swap":
                for i in range(2 if s[1] in ("Aq", "Ak", "An") else 1):
                    add(layer, "swap", s[1], i)
            elif s[0] == "project_a":
                for t in range(NT):
                    add(layer, "qa", t)
                    add(layer, "kva", t)
            elif s[0] == "turn":
                for g in range(NSETS[s[2]]):
                    add(layer, "turn", s[1], g)
        if layer % 2:
            for t in range(NT):
                for b in range(2):
                    add(layer, "fpre", t, b)
                add(layer, "logits", t)
            add(layer, "rank")
        add(layer, "pt")
        for t in range(NT):
            for half in range(2):
                add(layer, "proj", t, half)
    return {u: n for n, u in enumerate(uses)}


def z_block(column):
    return [c for c, w in WIDE_Z + NARROW_Z if c <= column < c + w][0]


USE = exchange_uses()
Z_DONE = {(u[0], u[2]): n for u, n in USE.items() if u[1] == "z"}
SPLIT_TILES = [(layer, kind, t) for layer in range(DEPTH) for kind in ["pre"] + (["fpre"] if layer % 2 == 0 else []) + ["xt"] for t in range(NT)]
EXCHANGE = 3


class Count:

    def __init__(self, sem, at=0):
        self.sem, self.at = sem, at

    def up(self, ins):
        ins.then_inc(self.sem, 1)
        self.at = self.at + 1

    def wait(self, eng):
        eng.wait_ge(self.sem, self.at)


def X_COUNT(layer, which, t):
    return NT * (3 * layer + which) + t + 1


def PARAMS(layer):
    return 16 * (11 * (layer + 1) + 3)


def wait_from(eng, sem, value):
    if not isinstance(value, int) or value > 0:
        eng.wait_ge(sem, value)


class FeedForward:

    def __init__(self, sem):
        self.gu_ready, self.silu_ready = sem("ff_gate_up_ready"), sem("ff_silu_ready")
        self.hidden_step, self.hidden_ready = sem("ff_hidden_step"), sem("ff_hidden_ready")
        self.up_gate_hi, self.up_gate_split = sem("ff_up_gate_hi_ready"), sem("ff_up_gate_split")
        self.down_hi, self.down_split = sem("ff_down_hi_ready"), sem("ff_down_split")
        self.down_done = sem("ff_down_done")


class ExpertPass:

    def __init__(self, sem, tag, slots, loads0):
        self.slots, self.loads0 = slots, loads0
        self.up_gate_hi, self.up_gate_split = sem(f"{tag}_up_gate_hi_ready"), sem(f"{tag}_up_gate_split")
        self.up_gate_used = sem(f"{tag}_up_gate_used")
        self.down_hi, self.down_split = sem(f"{tag}_down_hi_ready"), sem(f"{tag}_down_split")
        self.up_copied, self.silu_ready = sem(f"{tag}_up_copied"), sem(f"{tag}_silu_ready")
        self.hidden_ready, self.turned = sem(f"{tag}_hidden_ready"), sem(f"{tag}_hidden_turned")
        self.turned_hi, self.turned_split = sem(f"{tag}_turned_hi_ready"), sem(f"{tag}_turned_split")
        self.down_done = sem(f"{tag}_down_done")
        self.columns, self.picked = sem(f"{tag}_routing_columns_ready"), sem(f"{tag}_pick_ready")
        self.gathered = sem(f"{tag}_tokens_gathered")
        self.tokens_hi, self.tokens_split = sem(f"{tag}_tokens_hi_ready"), sem(f"{tag}_tokens_split")
        self.spread_turned, self.spread_ready = sem(f"{tag}_spread_turned"), sem(f"{tag}_spread_ready")
        self.y_hi_done, self.y_split = sem(f"{tag}_y_hi_ready"), sem(f"{tag}_y_split")
        self.back, self.added = sem(f"{tag}_scatter_ready"), sem(f"{tag}_scatter_added")


def for_chunks(engine, chunk):
    def expert(e):
        chunk(e * E_CHUNKS, e, 0)
        chunk(e * E_CHUNKS + 1, e, 1)
        chunk(e * E_CHUNKS + 2, e, 2)
        with engine.Fori(3, E_CHUNKS - 1) as c:
            chunk(e * E_CHUNKS + c, e, "mid")
        chunk(e * E_CHUNKS + (E_CHUNKS - 1), e, "last")

    expert(0)
    with engine.Fori(1, N_EXPERTS) as e:
        expert(e)


def ring_plan():
    plan, at, loops = {}, 0, {}
    for layer in range(DEPTH):
        for s in MIXER:
            if s[0] == "z":
                for half in range(2 if s[1] in WIDE_Z else 1):
                    plan[at] = (layer, "z") + s[1] + (half,)
                    at += 1
            if s[0] == "fill" and s[1] % 8 == 0:
                b = BRANCH_ID[BRANCH_ORDER[s[1] // 8]]
                for i in range(4):
                    plan[at] = (layer, "gate", b, i)
                    at += 1
                plan[at] = (layer, "branch", b)
                at += 1
        for i in range(4):
            plan[at] = (layer, "out", i)
            at += 1
        loops[layer] = at
        at += (D_FF if layer % 2 == 0 else N_EXPERTS * MOE_FF) // CW * 3
        plan[at] = (layer, "proj")
        at += 1
        for i in range(4):
            plan[at] = (layer, "ple", i)
            at += 1
    return plan, loops, at


PLAN, LOOPS, _ = ring_plan()
WHERE = {v: k for k, v in PLAN.items()}
FF_BODIES = D_FF // (2 * CW)
FF_BLOCKS = 2 * CW // P
N_FFN_BLOCKS = D_FF // P
E_CHUNKS = MOE_FF // ECW
E_BLOCKS = ECW // P
ALL_CHUNKS = N_EXPERTS * E_CHUNKS


def trunk(nc, args):
    (x_in, p_in, w_in, a_qa_g, a_kva_g, a_w_uq, a_w_ukv, b_q_g, b_k_g, d_sink, w_branch, w_out,
     mix_pre_g, mix_post_g, ffn_pre_g, ffn_post_g, ffn_w_gate, ffn_w_up, ffn_w_down,
     router_w, router_b, moe_w_gate, moe_w_up, moe_w_down, ple_w_proj, ple_w_gate, ple_post_g,
     const_in, out) = args
    ctx = ExitStack()
    with ctx:
        place = [-(-nc.sbuf_base // 64) * 64]

        def sb(name, shape, dt=F32):
            size = 4
            for n in shape[1:]:
                size *= n
            at = place[0]
            place[0] += -(-size // 64) * 64
            return nc.alloc_sbuf_tensor_at(name, shape, dt, offset=at)

        def sem(name):
            return ctx.enter_context(nc.semaphore(name))

        ring_at = place[0]
        ring = sb("ring", [P, RING, SLOT])
        ring_lo = nc.alloc_sbuf_tensor_at("ring_lo", [P, RING, SLOT], F32R, offset=ring_at)
        x = sb("x", [P, NT, D_MODEL])
        xn = sb("xn", [P, NT, D_MODEL])
        hT = sb("hT", [P, NK, SEQ])
        work_at = place[0]
        work = sb("work", [P, WORK])

        def rounded(name, at, shape):
            return nc.alloc_sbuf_tensor_at(name, shape, F32R, offset=work_at + 4 * at)

        cn = sb("cn", [P, CONST_W])
        gain = sb("gain", [P, 2, D_MODEL])
        gain_a = sb("gain_a", [P, 384])
        gain_b = sb("gain_b", [P, 6, HD])
        sink = sb("sink", [P, 4])
        w_uq = sb("w_uq", [P, 2, 384])
        w_ukv = sb("w_ukv", [P, 512])
        rtr_w = sb("rtr_w", [P, NK, 8])
        rtr_b = sb("rtr_b", [P, NT, 8])
        sumsq = sb("sumsq", [P, len(STAT)])
        var = sb("var", [P, len(STAT)])
        rstd = sb("rstd", [P, len(STAT)])
        sumsq_b = sb("sumsq_b", [P, NT, 6])
        var_b = sb("var_b", [P, NT, 6])
        rstd_b = sb("rstd_b", [P, NT, 6])
        minus_half = sb("minus_half", [P, NT * 6])
        peak = sb("peak", [P, 2, NT, 3])
        top = sb("top", [P, 2, NT])
        bias = sb("bias", [P, 2, NT])
        total = sb("total", [P, 2, NT])
        sunk = sb("sunk", [P, 2, NT])
        inv = sb("inv", [P, 2, NT])
        egate = sb("egate", [P, 2, SEQ])

        def carve(start=0):
            at = [start]

            def take(n):
                at[0] += n
                assert at[0] <= WORK
                return work[:, at[0] - n:at[0]]
            return take

        take = carve()
        z = take(NT * GATE0).rearrange("p (t c) -> p t c", t=NT)
        qT = take(8 * SEQ).rearrange("p (b s) -> p b s", b=8)
        qaT = take(4 * SEQ).rearrange("p (b s) -> p b s", b=4)
        kaT = take(4 * SEQ).rearrange("p (b s) -> p b s", b=4)
        probs = take(2 * NT * 3 * SEQ).rearrange("p (j t g s) -> p j t g s", j=2, t=NT, g=3)
        NPT = 3
        pT = take(NPT * 2 * SEQ).rearrange("p (n k s) -> p n k s", n=NPT, k=NT)
        kva = take(NT * 512).rearrange("p (t c) -> p t c", t=NT)
        lowT = take(3 * SEQ).rearrange("p (b s) -> p b s", b=3)
        oT = take(NK * SEQ)
        post_tmp = oT.rearrange("p (t d) -> p t d", t=NT)
        oT = oT.rearrange("p (b s) -> p b s", b=NK)
        kz = take(14 * SEQ).rearrange("p (b s) -> p b s", b=14)
        staged = take(2 * NT * 384).rearrange("p (n t c) -> p n t c", n=2, t=NT)
        rot = take(2 * 384).rearrange("p (n c) -> p n c", n=2)
        qa_sb = xn[:, :, 0:384]
        mergedT = xn[:, :, :].rearrange("p t (b s) -> p (t b) s", s=SEQ)

        zT_hi = rounded("zT_hi", 11584, [P, NK, SEQ])
        zT_lo = rounded("zT_lo", 13632, [P, NK, SEQ])
        z_hi_w = rounded("z_hi_w", 15936, [P, 2, SLOT])

        up_gate_hi_w = rounded("up_gate_hi_w", 0, [P, 4, SLOT])
        proj = work[:, 0:2048].rearrange("p (t d) -> p t d", t=NT)
        ple_tmp = work[:, 2048:4096].rearrange("p (t d) -> p t d", t=NT)
        weight_hi_w = rounded("weight_hi_w", 5120, [P, 4, SLOT])
        junk = work[:, 4096:4096 + D_MODEL]
        down_hi_w = rounded("down_hi_w", 8192, [P, 2, SLOT])
        down_lo_w = rounded("down_lo_w", 12288, [P, 2, SLOT])
        hidden_hi = rounded("hidden_hi", 16384, [P, 4, SEQ])
        hidden_lo = rounded("hidden_lo", 17408, [P, 4, SEQ])
        take = carve(18432)
        hidden = take(2 * SEQ)
        silu = take(4 * SEQ)
        e_hidden, e_silu, e_up = hidden[:, 0:ECW], silu[:, 0:ECW], silu[:, ECW:2 * ECW]
        hidden = hidden.rearrange("p (n s) -> p n s", n=2)
        silu = silu.rearrange("p (n s) -> p n s", n=4)
        cur_spread = rounded("cur_spread", 18432 + 6 * SEQ, [P, SEQ])
        small_at = 18432 + 7 * SEQ
        hT_hi = rounded("hT_hi", 20992, [P, NK, SEQ])
        hT_lo = rounded("hT_lo", 23040, [P, NK, SEQ])
        tokens_hi = rounded("tokens_hi", 20992, [P, NK, CAP])
        tokens_lo = rounded("tokens_lo", 22016, [P, NK, CAP])
        y_hi = rounded("y_hi", 23040, [P, D_MODEL])
        y_lo = rounded("y_lo", 24064, [P, D_MODEL])
        take = carve(25088)
        p_sb = take(NT * PLE_DIM).rearrange("p (t c) -> p t c", t=NT)
        pleT = take(2 * SEQ).rearrange("p (k s) -> p k s", k=2)
        fsum = hT[:, :, :].rearrange("p k s -> p (k s)").rearrange("p (t d) -> p t d", t=NT)
        take = carve(small_at)
        lg = take(NT * 8).rearrange("p (t e) -> p t e", t=NT)
        eq = take(NT * 8).rearrange("p (t e) -> p t e", t=NT)
        idx = take(NT * 8).rearrange("p (t e) -> p t e", t=NT)
        first = take(NT * 8).rearrange("p (t e) -> p t e", t=NT)
        second = take(NT * 8).rearrange("p (t e) -> p t e", t=NT)
        chosen = take(NT * 8).rearrange("p (t e) -> p t e", t=NT)
        weight = take(NT * 8).rearrange("p (t e) -> p t e", t=NT)
        rank = take(3 * 8).rearrange("p (t e) -> p t e", t=3)
        cur_rank, cur_chosen, cur_weight = take(NT), take(NT), take(NT)
        cur_g = take(1)
        rt = take(NT * 8).rearrange("p (n t) -> p n t", t=NT)
        overflow_f = take(8)
        pick = take(NT * CAP).rearrange("p (t n) -> p t n", t=NT)
        overflow = sb("overflow", [P, 1], I32)

        ps = ctx.enter_context(nc.psum_tensor("ps", [P, 8, 512], F32))
        O_BANK = ps[:, 3, 0:SEQ]

        def acc(t):
            return ps[:, 4 + 2 * t:6 + 2 * t, :]

        UP_BANK, TURN_BANK, GATE_BANK, SPREAD_BANK = (ps[:, b, :] for b in range(4))
        BACK = [ps[:, 2:4, :], ps[:, 6:8, :]]
        GATHER = [ps[:, 6, :], ps[:, 7, :]]

        def const(name, n):
            return cn[:, CONST_AT[name]:CONST_AT[name] + n]

        ident, upper, ones = const("ident", P), const("upper", P), const("ones", P)
        iota = const("iota", P)
        iota8 = const("iota8", NT * 8).rearrange("p (t e) -> p t e", t=NT)
        mask = const("mask", 4 * NT * SEQ).rearrange("p (m t s) -> p m t s", m=4, t=NT)
        tab = {"full": const("full", 2 * NT * HD).rearrange("p (f t d) -> p f t d", f=2, t=NT),
               "axial": const("axial", 2 * NT * HD).rearrange("p (f t d) -> p f t d", f=2, t=NT),
               "a": const("rope_a", 2 * NT * A_ROPE).rearrange("p (f t d) -> p f t d", f=2, t=NT)}

        const_in_s, x_in_s = sem("const_loaded"), [sem(f"x{t}_loaded") for t in range(NT)]
        slot_in = [sem(f"slot{i}_loaded") for i in range(RING)]
        gain_in = [sem(f"gain{i}_loaded") for i in range(2)]
        params_in, p_loaded = sem("params_loaded"), sem("p_loaded")
        kz_zero = sem("kz_zeroed")
        ex_ready, ex_done = sem("exchange_ready"), sem("exchange_emptied")
        sq_done, rstd_done = sem("sumsq_done"), sem("rstd_done")
        sqb_done, rstdb_done = sem("sumsq_b_done"), sem("rstd_b_done")
        xn_done, x_done = sem("normed_ready"), sem("residual_ready")
        staged_done = sem("staged_ready")
        scored, score_read = sem("scores_ready"), sem("scores_read")
        bias_done, exp_done, prob_done = sem("bias_ready"), sem("exp_ready"), sem("probs_ready")
        pv_done, o_done = sem("pv_done"), sem("o_emptied")
        unit_ready, egate_done, unit_done = sem("unit_ready"), sem("gate_exp_ready"), sem("unit_merged")
        mix_done = sem("mix_ready")
        ple_done, ple_gate, ple_prod = sem("ple_ready"), sem("ple_gate_ready"), sem("ple_product_ready")
        route_exp_in, route_exp, routed = sem("route_difference_ready"), sem("route_exp_ready"), sem("routed")
        overflow_ready, moe_done = sem("overflow_known"), sem("moe_done")
        dve_step, pool_step = sem("vector_step"), sem("pool_step")
        stored = sem("stored")

        tile_turned, tile_hi, tile_split = sem("tile_turned"), sem("tile_hi_ready"), sem("tile_split")
        pre_copied = sem("mixer_input_copied")
        z_hi, z_split, z_used = sem("z_weight_hi_ready"), sem("z_weight_split"), sem("z_weight_half_used")
        merged_hi, merged_split = sem("merged_hi_ready"), sem("merged_split")
        weight_hi, weight_split = sem("weight_hi_ready"), sem("weight_split")
        ffn = FeedForward(sem)
        main_pass = ExpertPass(sem, "moe", slot_in, [(LOOPS[1] + j) // RING for j in range(RING)])
        over_pass = ExpertPass(sem, "over", [sem(f"over_slot{i}_loaded") for i in range(RING)], [0] * RING)
        over_ranked = sem("over_ranks_ready")

        def ring_slot(j):
            return (LOOPS[0] + j) % RING

        def expert_slot(j):
            return (LOOPS[1] + j) % RING

        def tile_number(layer, kind, t, b):
            return 2 * SPLIT_TILES.index((layer, kind, t)) + b

        def product_parts(parts, weights):
            return list(enumerate(((parts[0], weights[0]), (parts[0], weights[1]), (parts[1], weights[0]))))

        def weight_number(layer, kind, i):
            return 8 * layer + (4 if kind == "ple" else 0) + i

        def slot_of(pos):
            return ring[:, pos % RING, :]

        def loaded(eng, pos):
            eng.wait_ge(slot_in[pos % RING], 16 * (pos // RING + 1))

        def released(pos):
            what = PLAN[pos]
            layer, kind = what[0], what[1]
            if kind == "z":
                return ex_ready, Z_DONE[(layer, what[2])] + 1
            if kind == "gate":
                order = BRANCH_ORDER.index("ABCD"[what[2]])
                return unit_ready, UNITS * layer + 8 * order + 2 * what[3] + 2
            if kind == "branch":
                return unit_ready, UNITS * layer + 8 * BRANCH_ORDER.index("ABCD"[what[2]]) + 8
            if kind == "out":
                return mix_done, NT * (layer + 1)
            if kind == "proj":
                return ex_ready, USE[(layer, "proj", NT - 1, 1)] + 1
            return ple_done, NT * (layer + 1)

        block = ctx.enter_context(nc.Block())

        @block.sync
        def _(sp):
            w_in_v = [w_in[l].rearrange("(k p) c -> p k c", p=P) for l in range(DEPTH)]

            def load(pos):
                layer, kind, *r = PLAN[pos]
                dst, wide = slot_of(pos), None
                if kind == "z":
                    c, w, half = r
                    if (c, w) in WIDE_Z:
                        dst = dst.rearrange("p (k c) -> p k c", k=4)[:, :, 0:w]
                        src = w_in_v[layer][:, 4 * half:4 * half + 4, c:c + w]
                    else:
                        dst = dst.rearrange("p (k c) -> p k c", k=NK)
                        src = w_in_v[layer][:, :, c:c + w]
                elif kind == "gate":
                    c = GATE0 + r[0] * D_MODEL + r[1] * CW
                    dst = dst.rearrange("p (k c) -> p k c", k=NK)
                    src = w_in_v[layer][:, :, c:c + CW]
                else:
                    dst = dst.rearrange("p (k c) -> p k c", k=2)
                    if kind == "branch":
                        src = w_branch[layer, r[0]].rearrange("(k p) c -> p k c", p=P)
                    elif kind == "out":
                        src = w_out[layer].rearrange("(i k p) c -> i p k c", p=P, k=2)[r[0]]
                    elif kind == "proj":
                        src = ple_w_proj[layer].rearrange("(k p) c -> p k c", p=P)
                    else:
                        src = ple_w_gate[layer].rearrange("(i k p) c -> i p k c", p=P, k=2)[r[0]]
                prior = pos - RING
                if prior >= 0:
                    if prior in PLAN:
                        sp.wait_ge(*released(prior))
                    else:
                        loop_ended(ffn if prior < LOOPS[1] else main_pass)
                sp.dma_start(dst, src).then_inc(slot_in[pos % RING], 16)

            def loop_ended(run):
                if run is ffn:
                    sp.wait_ge(ffn.gu_ready, N_FFN_BLOCKS)
                    sp.wait_ge(ffn.down_split, 2 * FF_BODIES)
                else:
                    sp.wait_ge(run.up_gate_used, 4 * ALL_CHUNKS)
                    sp.wait_ge(run.down_split, 2 * ALL_CHUNKS)

            def ffn_loads(body):
                for i in range(2):
                    for j in range(3):
                        n = 3 * i + j
                        if isinstance(body, int):
                            sp.wait_ge(*released(LOOPS[0] - RING + n))
                        elif j < 2:
                            sp.wait_ge(ffn.gu_ready, (body - 1) * FF_BLOCKS + 2 * (i + 1))
                        else:
                            sp.wait_ge(ffn.down_split, (body - 1) * 2 + i + 1)
                        dst = ring[:, ring_slot(n), :].rearrange("p (k c) -> p k c", k=NK if j < 2 else 2)
                        sp.dma_start(dst, ffn_views[j][2 * body + i]).then_inc(slot_in[ring_slot(n)], 16)

            def expert_load(run, j, b, e, c):
                if isinstance(b, int) and b == 0:
                    if run is main_pass:
                        sp.wait_ge(*released(LOOPS[1] - RING + j))
                elif j < 4:
                    sp.wait_ge(run.up_gate_used, 4 * (b - 1) + j + 1)
                else:
                    sp.wait_ge(run.down_split, 2 * (b - 1) + j - 3)
                dst = ring[:, expert_slot(j), :].rearrange("p (k c) -> p k c", k=4 if j < 4 else 2)
                src = expert_views[j // 2][e][c][j % 2]
                sp.dma_start(dst, src).then_inc(run.slots[expert_slot(j)], 16)

            def all_expert_loads(run):
                def chunk(b, e, c, before):
                    for j in (0, 1):
                        expert_load(run, j, b, e, c)
                    if before:
                        for j in (4, 5):
                            expert_load(run, j, b - 1, *before)
                    for j in (2, 3):
                        expert_load(run, j, b, e, c)

                for j in range(RING):
                    expert_load(run, j, 0, 0, 0)
                chunk(1, 0, 1, None)
                with sp.Fori(2, E_CHUNKS) as c:
                    chunk(c, 0, c, (0, c - 1))
                with sp.Fori(1, N_EXPERTS) as e:
                    chunk(e * E_CHUNKS, e, 0, (e - 1, E_CHUNKS - 1))
                    with sp.Fori(1, E_CHUNKS) as c:
                        chunk(e * E_CHUNKS + c, e, c, (e, c - 1))
                for j in (4, 5):
                    expert_load(run, j, ALL_CHUNKS - 1, N_EXPERTS - 1, E_CHUNKS - 1)

            up_gate_view = lambda w: w.rearrange("(k p) (c f) -> c p k f", p=P, f=CW)
            ffn_views = [up_gate_view(ffn_w_up[0]), up_gate_view(ffn_w_gate[0]),
                         ffn_w_down[0].rearrange("(c k p) d -> c p k d", p=P, k=2)]
            moe_view = lambda w: w.rearrange("e (h k p) (c f) -> e c h p k f", h=2, p=P, f=ECW)
            expert_views = [moe_view(moe_w_up[0]), moe_view(moe_w_gate[0]),
                            moe_w_down[0].rearrange("e (c h k p) d -> e c h p k d", h=2, k=2, p=P)]

            x_v, first = x_in[0].rearrange("(t p) d -> p t d", p=P), CONST_AT["upper"]
            sp.dma_start(x[:, 0, :], x_v[:, 0, :]).then_inc(x_in_s[0], 16)
            sp.dma_start(cn[:, 0:first], const_in[:, 0:first]).then_inc(const_in_s, 16)
            sp.dma_start(x[:, 1, :], x_v[:, 1, :]).then_inc(x_in_s[1], 16)
            for layer in range(DEPTH):
                start = 0 if layer == 0 else WHERE[(0, "ple", 3)] + 1
                for pos in range(start, LOOPS[layer]):
                    load(pos)
                    if pos == 3:
                        sp.dma_start(cn[:, first:], const_in[:, first:]).then_inc(const_in_s, 16)
                if layer % 2 == 0:
                    ffn_loads(0)
                    with sp.Fori(1, FF_BODIES) as body:
                        ffn_loads(body)
                else:
                    all_expert_loads(main_pass)
                    sp.wait_ge(overflow_ready, 1)
                    more = sp.value_load(overflow[0:1, 0:1], min_val=0, max_val=1)
                    with sp.If(more > 0):
                        loop_ended(main_pass)
                        all_expert_loads(over_pass)
                        loop_ended(over_pass)
                for pos in range(WHERE[(layer, "proj")], WHERE[(layer, "ple", 3)] + 1):
                    load(pos)
            out_v = out[0].rearrange("(t p) d -> p t d", p=P)
            for t in range(NT):
                sp.wait_ge(x_done, X_COUNT(DEPTH - 1, 2, t))
                sp.dma_start(out_v[:, t, :], x[:, t, :]).then_inc(stored, 16)
            sp.wait_ge(stored, 16 * NT)

        @block.gpsimd
        def _(pool):
            step = Count(pool_step)
            gains = [g for l in range(DEPTH) for g in (mix_pre_g[l], mix_post_g[l], ffn_pre_g[l], ffn_post_g[l], ple_post_g[l])]

            def load_gain(n):
                if n >= len(gains):
                    return
                if n >= 2:
                    last_layer, last = divmod(n - 2, 5)
                    if last in (0, 2):
                        pool.wait_ge(xn_done, 2 * NT * last_layer + NT * (last // 2) + NT)
                    else:
                        pool.wait_ge(x_done, X_COUNT(last_layer, {1: 0, 3: 1, 4: 2}[last], NT - 1))
                pool.dma_start(gain[:, n % 2, :], gains[n].partition_broadcast(P)).then_inc(gain_in[n % 2], 16)

            def load_params(layer):
                if layer:
                    pool.wait_ge(staged_done, len(STAGED) * layer)
                    pool.wait_ge(ex_done, USE[(layer - 1, "kva", NT - 1)] + 1)
                    pool.wait_ge(prob_done, len(JOBS) * layer)
                    pool.wait_ge(exp_done, len(JOBS) * layer)
                pool.dma_start(gain_a[:, 0:256], a_qa_g[layer].partition_broadcast(P)).then_inc(params_in, 16)
                pool.dma_start(gain_a[:, 256:384], a_kva_g[layer].partition_broadcast(P)).then_inc(params_in, 16)
                for h in range(6):
                    g = b_q_g if h < 4 else b_k_g
                    pool.dma_start(gain_b[:, h, :], g[layer].partition_broadcast(P)).then_inc(params_in, 16)
                pool.dma_start(sink[:, :], d_sink[layer].partition_broadcast(P)).then_inc(params_in, 16)
                pool.dma_start(w_uq[:, :, :], a_w_uq[layer].rearrange("(k p) c -> p k c", p=P)).then_inc(params_in, 16)
                pool.dma_start(w_ukv[:, :], a_w_ukv[layer]).then_inc(params_in, 16)

            def stat(layer, kind, t, width=D_MODEL):
                n = STAT[(layer, kind, t)]
                pool.wait_ge(sq_done, n + 1)
                step.up(nc.gpsimd.tensor_scalar(var[:, n:n + 1], sumsq[:, n:n + 1], 1.0 / width, EPS, ALU.mult, ALU.add))
                step.wait(pool)
                nc.gpsimd.tensor_tensor(rstd[:, n:n + 1], var[:, n:n + 1], minus_half[:, 0:1], ALU.pow).then_inc(rstd_done, 1)

            load_gain(0)
            step.up(nc.gpsimd.memset(minus_half[:, :], -0.5))
            step.wait(pool)
            for t in range(NT):
                stat(0, "pre", t)
            load_gain(1)
            load_params(0)
            for t in range(NT):
                pool.dma_start(rtr_b[:, t, :], router_b[0].partition_broadcast(P)).then_inc(params_in, 16)
            pool.dma_start(rtr_w[:, :, :], router_w[0].rearrange("(k p) e -> p k e", p=P)).then_inc(params_in, 16)
            for layer in range(DEPTH):
                if layer > 0:
                    pool.wait_ge(x_done, X_COUNT(layer - 1, 2, NT - 1))
                nc.gpsimd.memset(kz, 0.0).then_inc(kz_zero, 1)
                step.wait(pool)
                load_gain(5 * layer + 2)
                for s in MIXER:
                    if s[0] == "norm_b":
                        pool.wait_ge(sqb_done, layer + 1)
                        fl = lambda a: a[:, :, :].rearrange("p t h -> p (t h)")
                        step.up(nc.gpsimd.tensor_scalar(fl(var_b), fl(sumsq_b), 1.0 / HD, EPS, ALU.mult, ALU.add))
                        step.wait(pool)
                        nc.gpsimd.tensor_tensor(fl(rstd_b), fl(var_b), minus_half[:, :], ALU.pow).then_inc(rstdb_done, 1)
                    if s[0] == "norm_a":
                        for kind, width in (("low_q", A_Q_RANK), ("low_kv", A_KV_RANK)):
                            for t in range(NT):
                                stat(layer, kind, t, width)
                for t in range(NT):
                    stat(layer, "post", t)
                    stat(layer, "fpre", t)
                load_gain(5 * layer + 3)
                if layer + 1 < DEPTH:
                    load_params(layer + 1)
                load_gain(5 * layer + 4)
                pool.wait_ge(mix_done, NT * (layer + 1))
                pool.wait_ge(x_done, X_COUNT(layer, 0, NT - 1))
                pool.dma_start(p_sb, p_in[layer, 0].rearrange("(t p) c -> p t c", p=P)).then_inc(p_loaded, 16)
                for t in range(NT):
                    stat(layer, "fpost", t)
                load_gain(5 * layer + 5)
                for t in range(NT):
                    stat(layer, "ple", t)
                    if layer + 1 < DEPTH:
                        stat(layer + 1, "pre", t)
                load_gain(5 * layer + 6)

        @block.tensor
        def _(pe):
            mm = nc.tensor.matmul

            def bank_for(layer, *name):
                n = USE[(layer,) + name]
                if n >= EXCHANGE:
                    pe.wait_ge(ex_done, n - EXCHANGE + 1)
                return ps[:, n % EXCHANGE, :]

            def emptied(layer, *name):
                pe.wait_ge(ex_done, USE[(layer,) + name] + 1)

            def turn_tile(layer, kind, src, t):
                for b in range(2):
                    bank = bank_for(layer, kind, t, b)
                    for i in range(4):
                        c = (4 * b + i) * P
                        m = nc.tensor.transpose(bank[:, i * P:(i + 1) * P], src[:, t, c:c + P], ident)
                    m.then_inc(ex_ready, 1)

            def wide_product(layer, bank, i, half, t):
                c, w = WIDE_Z[i]
                pos = WHERE[(layer, "z", c, w, half)]
                pe.wait_ge(z_split, 8 * layer + 2 * i + half + 1)
                hi, lo = [a.rearrange("p (k c) -> p k c", k=4) for a in (z_hi_w[:, half, :], ring_lo[:, pos % RING, :])]
                for k in range(4):
                    for n, (a, b) in product_parts((zT_hi, zT_lo), (hi, lo)):
                        m = mm(bank[:, 0:w], a[:, 4 * half + k, t * P:(t + 1) * P], b[:, k, 0:w],
                               start=(half == k == n == 0), stop=(half == 1 and k == 3 and n == 2))
                return m

            def turn_split_tile(layer, kind, src, t):
                if kind == "pre":
                    pe.wait_ge(xn_done, 2 * NT * layer + t + 1)
                for b in range(2):
                    for i in range(4):
                        c = (4 * b + i) * P
                        m = nc.tensor.transpose(acc(t)[:, b, i * P:(i + 1) * P], src[:, t, c:c + P], ident)
                    m.then_inc(tile_turned, 1)

            def split_product(layer, kind, i, t):
                pos = WHERE[(layer, kind, i)]
                pe.wait_ge(weight_split, weight_number(layer, kind, i) + 1)
                hi, lo = [w.rearrange("p (k c) -> p k c", k=2) for w in (weight_hi_w[:, i, :], ring_lo[:, pos % RING, :])]
                for k in range(2):
                    for n, (a, w) in enumerate(((hT_hi, hi), (hT_hi, lo), (hT_lo, hi))):
                        for half in range(2):
                            m = mm(acc(t)[:, half, :], a[:, 2 * i + k, t * P:(t + 1) * P], w[:, k, half * 512:(half + 1) * 512],
                                   start=(i == k == n == 0), stop=(i == 3 and k == 1 and n == 2))
                return m

            def swap(layer, item):
                pe.wait_ge(staged_done, len(STAGED) * layer + STAGED.index(item) + 1)
                r = staged[:, (len(STAGED) * layer + STAGED.index(item)) % 2]
                if item in ("Aq", "Ak"):
                    for u in range(2):
                        bank = bank_for(layer, "swap", item, u)
                        for h in range(2):
                            for t in range(NT):
                                c = (2 * u + h) * A_QK
                                m = nc.tensor.transpose(bank[0:A_QK, h * SEQ + t * P:h * SEQ + (t + 1) * P],
                                                        r[:, t, c:c + A_QK], ident)
                        m.then_inc(ex_ready, 1)
                    return
                if item == "An":
                    groups = [[0, 1], [2]]
                else:
                    groups = [[0]] if item in ("Bk", "Dk") else [[0, 1]]
                for u, g in enumerate(groups):
                    bank = bank_for(layer, "swap", item, u)
                    for i, b in enumerate(g):
                        for t in range(NT):
                            m = nc.tensor.transpose(bank[:, i * SEQ + t * P:i * SEQ + (t + 1) * P],
                                                    r[:, t, b * P:(b + 1) * P], ident)
                    m.then_inc(ex_ready, 1)

            def score_operands(b, h, g):
                if b == "A":
                    return qaT[0:A_QK, h, :], kaT[0:A_QK, h, :]
                if b in "BD":
                    return qT[:, h % 2, :], kz[:, h // 2, :]
                return qT[:, 2 + 2 * g + h // 2, :], kz[:, 2 + 4 * g + h, :]

            def score(layer, j, b, h, g):
                n = SETS * layer + SET0[j] + g
                if n >= 2:
                    pe.wait_ge(score_read, n - 1)
                q, k = score_operands(b, h, g)
                bank = ps[:, 4 + n % 2, :]
                for t in range(NT):
                    m = mm(bank[:, t * SEQ:(t + 1) * SEQ], q[:, t * P:(t + 1) * P], k, start=True, stop=True)
                m.then_inc(scored, 1)

            def values(b, h, g, kt):
                if b == "A":
                    return kva[:, kt, h * P + A_NOPE:(h + 1) * P]
                c = {"B": B0 + 6 * HD + (h // 2) * HD, "D": D0 + 6 * HD + (h // 2) * HD,
                     "C": C0 + g * 12 * HD + 8 * HD + h * HD}[b]
                return z[:, kt, c:c + HD]

            def feed_forward(body, more=None):
                block0 = body * FF_BLOCKS

                def gate_up(j):
                    wait_from(pe, ffn.hidden_ready, block0 + j - 3)
                    if j % 2 == 0:
                        pe.wait_ge(ffn.up_gate_split, body * 4 + j + 2)
                    cols = slice((j % 2) * P, (j % 2 + 1) * P)
                    for i in range(2):
                        hi = up_gate_hi_w[:, 2 * (j // 2) + i, :].rearrange("p (k c) -> p k c", k=NK)
                        lo = ring_lo[:, ring_slot(3 * (j // 2) + i), :].rearrange("p (k c) -> p k c", k=NK)
                        for k in range(NK):
                            for n, (w, xs) in enumerate(((hi, hT_hi), (hi, hT_lo), (lo, hT_hi))):
                                m = mm(ps[:, j, i * SEQ:(i + 1) * SEQ], w[:, k, cols], xs[:, k, :],
                                       start=(k == 0 and n == 0), stop=(k == NK - 1 and n == 2))
                    m.then_inc(ffn.gu_ready, 1)

                def down(j, first=False, last=False):
                    pe.wait_ge(ffn.hidden_ready, block0 + j + 1)
                    if j in (0, 2):
                        pe.wait_ge(ffn.down_split, 2 * body + j // 2 + 1)
                    jj = j % 4
                    down_product(acc, range(NT), jj, first, last).then_inc(ffn.down_done, 1)

                if more == "end":
                    down(-1, last=True)
                    return
                gate_up(0)
                if more is not None:
                    down(-1)
                gate_up(1)
                down(0, first=more is None)
                gate_up(2)
                down(1)
                gate_up(3)
                down(2)

            def down_product(to, tiles, j, first, last):
                hi, lo = [w[:, j // 2, :].rearrange("p (k c) -> p k c", k=2) for w in (down_hi_w, down_lo_w)]
                for t in tiles:
                    for n, (a, w) in enumerate(((hidden_hi, hi), (hidden_hi, lo), (hidden_lo, hi))):
                        for half in range(2):
                            m = mm(to(t)[:, half, :], a[:, j, t * P:(t + 1) * P],
                                   w[:, j % 2, half * 512:(half + 1) * 512], start=first and n == 0, stop=last and n == 2)
                return m

            def gather(run):
                for half in range(2):
                    for i in range(4):
                        c = (4 * half + i) * P
                        for t in range(NT):
                            m = mm(GATHER[half][:, i * P:(i + 1) * P], xn[:, t, c:c + P], pick[:, t, :],
                                   start=(t == 0), stop=(t == NT - 1))
                    m.then_inc(run.gathered, 1)

            def expert_turn(run, b):
                pe.wait_ge(run.hidden_ready, b + 1)
                wait_from(pe, run.turned_split, b)
                for j in range(E_BLOCKS):
                    m = nc.tensor.transpose(TURN_BANK[:, j * P:(j + 1) * P], e_hidden[:, j * P:(j + 1) * P], ident)
                m.then_inc(run.turned, 1)

            def expert_down(run, b, first=False, last=False):
                pe.wait_ge(run.turned_split, b + 1)
                for j in range(E_BLOCKS):
                    if j % 2 == 0:
                        pe.wait_ge(run.down_split, 2 * b + j // 2 + 1)
                    m = down_product(acc, (0,), j, first and j == 0, last and j == E_BLOCKS - 1)
                    if j % 2:
                        m.then_inc(run.down_done, 1)

            def scatter(run, e):
                pe.wait_ge(run.y_split, e + 1)
                pe.wait_ge(run.spread_ready, e + 1)
                for t in range(NT):
                    for half in range(2):
                        for n, y in enumerate((y_hi, y_lo)):
                            m = mm(BACK[t][:, half, :], cur_spread[:, t * P:(t + 1) * P], y[:, half * 512:(half + 1) * 512],
                                   start=(n == 0), stop=(n == 1))
                    m.then_inc(run.back, 1)

            def expert_chunk(run):
                def chunk(b, e, c):
                    no_chunk_before = isinstance(b, int) and b == 0
                    no_expert_before = isinstance(e, int)

                    def product(bank, j):
                        half = j % 2
                        pe.wait_ge(run.up_gate_split, 4 * b + j + 1)
                        if c == 0 and j < 2:
                            pe.wait_ge(run.tokens_split, 2 * e + half + 1)
                        hi = up_gate_hi_w[:, j, :].rearrange("p (k c) -> p k c", k=4)
                        lo = ring_lo[:, expert_slot(j), :].rearrange("p (k c) -> p k c", k=4)
                        for k in range(4):
                            for n, (xs, w) in enumerate(((tokens_hi, hi), (tokens_hi, lo), (tokens_lo, hi))):
                                m = mm(bank, xs[:, 4 * half + k, :], w[:, k, :], start=(half == k == n == 0),
                                       stop=(half == 1 and k == 3 and n == 2))
                        m.then_inc(run.up_gate_used, 1)

                    wait_from(pe, run.up_copied, b)
                    product(UP_BANK, 0)
                    if not no_chunk_before:
                        expert_turn(run, b - 1)
                    product(UP_BANK, 1)
                    if not no_chunk_before:
                        pe.wait_ge(run.silu_ready, b)
                    if c == 1 and not no_expert_before:
                        scatter(run, e - 1)
                    if c == "last" and no_expert_before:
                        pe.wait_ge(run.picked, e + 2)
                        gather(run)
                    elif c == "last":
                        with pe.If(e < N_EXPERTS - 1):
                            pe.wait_ge(run.picked, e + 2)
                            pe.wait_ge(run.added, 2 * e)
                            gather(run)
                    if not no_chunk_before:
                        expert_down(run, b - 1, first=(c == 1), last=(c == 0))
                    if c == 1:
                        if not no_expert_before:
                            pe.wait_ge(run.spread_ready, e)
                            pe.wait_ge(run.added, 2 * (e - 1) + 1)
                        for t in range(NT):
                            nc.tensor.transpose(SPREAD_BANK[:, t * P:(t + 1) * P], pick[:, t, :], ident)
                        for t in range(NT):
                            m = mm(SPREAD_BANK[:, SEQ:SEQ + 1], pick[:, t, :], cur_weight[:, t:t + 1], start=(t == 0), stop=(t == NT - 1))
                        m.then_inc(run.spread_turned, 1)
                    product(GATE_BANK, 2)
                    product(GATE_BANK, 3)
                return chunk

            def experts(run):
                pe.wait_ge(run.picked, 1)
                gather(run)
                for_chunks(pe, expert_chunk(run))
                last = ALL_CHUNKS - 1
                expert_turn(run, last)
                expert_down(run, last, last=True)
                pe.wait_ge(run.silu_ready, ALL_CHUNKS)
                scatter(run, N_EXPERTS - 1)
                pe.wait_ge(run.added, 2 * N_EXPERTS)

            pe.wait_ge(const_in_s, 16)
            for layer in range(DEPTH):
                turn_split_tile(layer, "pre", xn, 0)
                narrow = False
                for step_number, s in enumerate(MIXER):
                    if s[0] == "z":
                        c, w = s[1]
                        if s[1] in WIDE_Z:
                            i = WIDE_Z.index(s[1])
                            banks = [bank_for(layer, "z", c, t) for t in range(NT)]
                            if i == 0:
                                pe.wait_ge(tile_split, tile_number(layer, "pre", 0, 1) + 1)
                                wide_product(layer, banks[0], i, 0, 0)
                                if layer == 0:
                                    turn_split_tile(layer, "pre", xn, 1)
                                wide_product(layer, banks[0], i, 1, 0).then_inc(ex_ready, 1)
                                if layer > 0:
                                    turn_split_tile(layer, "pre", xn, 1)
                                pe.wait_ge(tile_split, tile_number(layer, "pre", 1, 1) + 1)
                            for half in range(2):
                                for t in (1,) if i == 0 else range(NT):
                                    m = wide_product(layer, banks[t], i, half, t)
                                    if half:
                                        m.then_inc(ex_ready, 1)
                                    elif t == 1:
                                        m.then_inc(z_used, 1)
                        else:
                            if not narrow:
                                pe.wait_ge(pre_copied, 4 * (layer + 1))
                                narrow = True
                            bank = bank_for(layer, "z", c, 0)
                            pos = WHERE[(layer, "z", c, w, 0)]
                            loaded(pe, pos)
                            wv = slot_of(pos).rearrange("p (k c) -> p k c", k=NK)
                            for t in range(NT):
                                for k in range(NK):
                                    m = mm(bank[:, t * SEQ:(t + 1) * SEQ], hT[:, k, t * P:(t + 1) * P], wv[:, k, :],
                                           start=(k == 0), stop=(k == NK - 1))
                            m.then_inc(ex_ready, 1)
                    elif s[0] == "swap":
                        swap(layer, s[1])
                    elif s[0] == "project_a":
                        emptied(layer, "swap", "An", 1)
                        pe.wait_ge(params_in, PARAMS(layer))
                        for t in range(NT):
                            bank = bank_for(layer, "qa", t)
                            for k in range(2):
                                m = mm(bank[:, 0:384], lowT[:, k, t * P:(t + 1) * P], w_uq[:, k, :], start=(k == 0), stop=(k == 1))
                            m.then_inc(ex_ready, 1)
                            bank = bank_for(layer, "kva", t)
                            mm(bank, lowT[:, 2, t * P:(t + 1) * P], w_ukv[:, :], start=True, stop=True).then_inc(ex_ready, 1)
                    elif s[0] == "score":
                        _, j, b, h = s
                        if h == 0:
                            emptied(layer, "swap", {"A": "Ak", "B": "Bk", "C": "C2k", "D": "Dk"}[b], 1 if b == "A" else 0)
                        later = MIXER[step_number + 1][0] == "pv" and NSETS[b] == 3
                        for g in range(2 if later else NSETS[b]):
                            score(layer, j, b, h, g)
                    elif s[0] == "turn":
                        _, j, b, h = s
                        pe.wait_ge(prob_done, len(JOBS) * layer + j + 1)
                        for g in range(NSETS[b]):
                            bank = bank_for(layer, "turn", j, g)
                            for kt in range(NT):
                                for t in range(NT):
                                    m = nc.tensor.transpose(bank[:, kt * SEQ + t * P:kt * SEQ + (t + 1) * P],
                                                            probs[:, j % 2, t, g, kt * P:(kt + 1) * P], ident)
                            m.then_inc(ex_ready, 1)
                    elif s[0] == "pv":
                        _, j, b, h = s
                        if h % 2 == 0:
                            pair = (len(JOBS) * layer + j) // 2
                            wait_from(pe, o_done, pair)
                        for g in range(NSETS[b]):
                            emptied(layer, "turn", j, g)
                            n = SETS * layer + SET0[j] + g
                            for kt in range(NT):
                                m = mm(O_BANK[(h % 2) * HD:(h % 2 + 1) * HD, :], values(b, h, g, kt), pT[:, n % NPT, kt, :],
                                       start=(g == 0 and kt == 0), stop=(g == NSETS[b] - 1 and kt == NT - 1))
                            m.then_inc(pv_done, 1)
                        before = MIXER[step_number - 1]
                        if before[0] == "score" and NSETS[before[2]] == 3:
                            score(layer, *before[1:], 2)
                    elif s[0] == "fill":
                        u = s[1]
                        order, c = divmod(u, 8)
                        n = BRANCH_ID[BRANCH_ORDER[order]]
                        wait_from(pe, unit_done, UNITS * layer + u - 1)
                        bank = ps[:, 6 + u % 2, :]
                        pos = WHERE[(layer, "gate", n, c // 2)]
                        loaded(pe, pos)
                        wg = slot_of(pos).rearrange("p (k c) -> p k c", k=NK)
                        for k in range(NK):
                            mm(bank[:, 0:SEQ], wg[:, k, (c % 2) * P:(c % 2 + 1) * P], hT[:, k, :],
                               start=(k == 0), stop=(k == NK - 1))
                        pos = WHERE[(layer, "branch", n)]
                        loaded(pe, pos)
                        pe.wait_ge(o_done, len(JOBS) // 2 * layer + 2 * (order + 1))
                        wb = slot_of(pos).rearrange("p (k c) -> p k c", k=2)
                        for k in range(2):
                            m = mm(bank[:, SEQ:2 * SEQ], wb[:, k, c * P:(c + 1) * P], oT[:, 2 * n + k, :],
                                   start=(k == 0), stop=(k == 1))
                        m.then_inc(unit_ready, 1)
                for t in range(NT):
                    if t == 1:
                        pe.wait_ge(unit_done, UNITS * (layer + 1))
                    for i in range(4):
                        pe.wait_ge(merged_split, NK * layer + 2 * i + 2)
                        m = split_product(layer, "out", i, t)
                    m.then_inc(mix_done, 1)
                for t in range(NT):
                    pe.wait_ge(xn_done, 2 * NT * layer + NT + t + 1)
                    if layer % 2 == 0:
                        pe.wait_ge(x_done, X_COUNT(layer, 0, t))
                        turn_split_tile(layer, "fpre", xn, t)
                    else:
                        turn_tile(layer, "fpre", xn, t)
                        emptied(layer, "fpre", t, 1)
                        if t == 0:
                            pe.wait_ge(params_in, PARAMS(layer))
                        bank = bank_for(layer, "logits", t)
                        for k in range(NK):
                            m = mm(bank[:, 0:8], hT[:, k, t * P:(t + 1) * P], rtr_w[:, k, :], start=(k == 0), stop=(k == NK - 1))
                        m.then_inc(ex_ready, 1)
                if layer % 2 == 0:
                    pe.wait_ge(tile_split, tile_number(layer, "fpre", NT - 1, 1) + 1)
                    feed_forward(0)
                    with pe.Fori(1, FF_BODIES) as body:
                        feed_forward(body, more="go on")
                    feed_forward(FF_BODIES, more="end")
                else:
                    pe.wait_ge(routed, 1)
                    bank = bank_for(layer, "rank")
                    mm(bank[:, 0:8], upper, chosen[:, 0, :], start=True, stop=True)
                    mm(bank[:, 8:16], ones, chosen[:, 0, :], start=True, stop=False)
                    mm(bank[:, 8:16], upper, chosen[:, 1, :], start=False, stop=True)
                    mm(bank[:, 16:24], ones, chosen[:, 0, :], start=True, stop=False)
                    mm(bank[:, 16:24], ones, chosen[:, 1, :], start=False, stop=True).then_inc(ex_ready, 1)
                    experts(main_pass)
                    pe.wait_ge(overflow_ready, 1)
                    more = pe.value_load(overflow[0:1, 0:1], min_val=0, max_val=1)
                    with pe.If(more > 0):
                        experts(over_pass)
                pe.wait_ge(p_loaded, 16 * (layer + 1))
                bank = bank_for(layer, "pt")
                for k in range(2):
                    for t in range(NT):
                        m = nc.tensor.transpose(bank[:, k * SEQ + t * P:k * SEQ + (t + 1) * P], p_sb[:, t, k * P:(k + 1) * P], ident)
                m.then_inc(ex_ready, 1)
                emptied(layer, "pt")
                pos = WHERE[(layer, "proj")]
                loaded(pe, pos)
                wp = slot_of(pos).rearrange("p (k c) -> p k c", k=2)
                for t in range(NT):
                    for half in range(2):
                        bank = bank_for(layer, "proj", t, half)
                        for k in range(2):
                            m = mm(bank, pleT[:, k, t * P:(t + 1) * P], wp[:, k, half * 512:(half + 1) * 512],
                                   start=(k == 0), stop=(k == 1))
                        m.then_inc(ex_ready, 1)
                for t in range(NT):
                    for i in range(4):
                        if t == 0 and i % 2 == 0:
                            turned = i // 2
                            pe.wait_ge(x_done, X_COUNT(layer, 1, turned))
                            turn_split_tile(layer, "xt", x, turned)
                        if i == 0:
                            pe.wait_ge(tile_split, tile_number(layer, "xt", t, 1) + 1)
                        m = split_product(layer, "ple", i, t)
                    m.then_inc(ple_done, 1)

        @block.scalar
        def _(act):
            copy, activation = nc.scalar.copy, nc.scalar.activation

            def taken(layer, *name):
                n = USE[(layer,) + name]
                act.wait_ge(ex_ready, n + 1)
                return ps[:, n % EXCHANGE, :]

            def square(which, src, rubbish):
                n = STAT[which]
                wait_from(act, sq_done, n)
                activation(rubbish, src, ACT.Square, accum_out=sumsq[:, n:n + 1]).then_inc(sq_done, 1)

            def turned_tile(layer, kind, t):
                for b in range(2):
                    bank = taken(layer, kind, t, b).rearrange("p (i s) -> p i s", i=4)
                    copy(hT[:, 4 * b:4 * b + 4, t * P:(t + 1) * P], bank).then_inc(ex_done, 1)

            def tile_his(layer, kind, t):
                to = zT_hi if kind == "pre" else hT_hi
                for b in range(2):
                    act.wait_ge(tile_turned, tile_number(layer, kind, t, b) + 1)
                    copy(to[:, 4 * b:4 * b + 4, t * P:(t + 1) * P], acc(t)[:, b, :].rearrange("p (i s) -> p i s", i=4))\
                        .then_inc(tile_hi, 1)

            def turned_input(layer, t):
                if layer % 2 == 0:
                    tile_his(layer, "fpre", t)
                else:
                    turned_tile(layer, "fpre", t)

            def merged_his(layer, u):
                act.wait_ge(unit_done, UNITS * layer + u + 1)
                copy(hT_hi[:, u % 8, :], mergedT[:, u % 8, :]).then_inc(merged_hi, 1)

            def z_his(layer, i, half):
                if half == 0:
                    wait_from(act, z_used, 4 * layer + i)
                elif i:
                    act.wait_ge(ex_ready, Z_DONE[(layer, WIDE_Z[i - 1][0])] + 1)
                pos = WHERE[(layer, "z") + WIDE_Z[i] + (half,)]
                loaded(act, pos)
                w = WIDE_Z[i][1]
                wide = lambda a: a.rearrange("p (k c) -> p k c", k=4)[:, :, 0:w]
                copy(wide(z_hi_w[:, half, :]), wide(slot_of(pos))).then_inc(z_hi, 1)

            def weight_his(layer, kind, i):
                pos = WHERE[(layer, kind, i)]
                loaded(act, pos)
                copy(weight_hi_w[:, i, :], slot_of(pos)).then_inc(weight_hi, 1)

            def swapped(layer, item):
                if item in ("Aq", "Ak"):
                    for u in range(2):
                        bank = taken(layer, "swap", item, u)
                        dst = qaT if item == "Aq" else kaT
                        copy(dst[0:A_QK, 2 * u:2 * u + 2, :], bank[0:A_QK, :].rearrange("p (h s) -> p h s", h=2)).then_inc(ex_done, 1)
                elif item == "An":
                    for u, (a, n) in enumerate(((0, 2), (2, 1))):
                        bank = taken(layer, "swap", item, u)
                        copy(lowT[:, a:a + n, :], bank[:, 0:n * SEQ].rearrange("p (h s) -> p h s", h=n)).then_inc(ex_done, 1)
                elif item[-1] == "q":
                    a = 0 if item[0] in "BD" else 2 + 2 * int(item[1])
                    bank = taken(layer, "swap", item, 0)
                    copy(qT[:, a:a + 2, :], bank.rearrange("p (h s) -> p h s", h=2)).then_inc(ex_done, 1)
                else:
                    bank = taken(layer, "swap", item, 0)
                    act.wait_ge(kz_zero, layer + 1)
                    for half in range(2):
                        r = slice(half * HD, (half + 1) * HD)
                        if item[0] in "BD":
                            ins = copy(kz[r, half, :], bank[r, 0:SEQ])
                        else:
                            a = 2 + 4 * int(item[1]) + half
                            ins = copy(kz[r, a:a + 3:2, :], bank[r, :].rearrange("p (h s) -> p h s", h=2))
                    ins.then_inc(ex_done, 1)

            def up_gate_his(i, body):
                for n in range(2):
                    j = 3 * i + n
                    act.wait_ge(slot_in[ring_slot(j)], ((LOOPS[0] + j) // RING + 1 + body) * 16)
                    copy(up_gate_hi_w[:, 2 * i + n, :], ring[:, ring_slot(j), :]).then_inc(ffn.up_gate_hi, 1)

            def silus(body, last=False):
                block0 = body * FF_BLOCKS
                for j in range(FF_BLOCKS):
                    if j % 2 == 0:
                        n = 3 * (j // 2) + 2
                        act.wait_ge(slot_in[ring_slot(n)], ((LOOPS[0] + n) // RING + 1 + body) * 16)
                        wait_from(act, ffn.down_done, block0 + j - 2)
                        copy(down_hi_w[:, j // 2, :], ring[:, ring_slot(n), :]).then_inc(ffn.down_hi, 1)
                    act.wait_ge(ffn.gu_ready, block0 + j + 1)
                    wait_from(act, ffn.hidden_ready, block0 + j - 3)
                    activation(silu[:, j, :], ps[:, j, SEQ:2 * SEQ], ACT.Silu).then_inc(ffn.silu_ready, 1)
                    if j == 0:
                        up_gate_his(1, body)
                    if j == 2 and not last:
                        up_gate_his(0, body + 1)

            def expert_his(run, b, j):
                slot = expert_slot(j)
                act.wait_ge(run.slots[slot], (run.loads0[j] + 1 + b) * 16)
                if j < 4:
                    copy(up_gate_hi_w[:, j, :], ring[:, slot, :]).then_inc(run.up_gate_hi, 1)
                else:
                    wait_from(act, run.down_done, 2 * (b - 1) + j - 3)
                    copy(down_hi_w[:, j - 4, :], ring[:, slot, :]).then_inc(run.down_hi, 1)

            def expert_silu(run, b):
                act.wait_ge(run.up_gate_used, 4 * b + 4)
                wait_from(act, run.hidden_ready, b)
                activation(e_silu, GATE_BANK, ACT.Silu).then_inc(run.silu_ready, 1)

            def turned_his(run, b):
                act.wait_ge(run.turned, b + 1)
                copy(hidden_hi[:, :, 0:CAP], TURN_BANK.rearrange("p (j n) -> p j n", j=E_BLOCKS)).then_inc(run.turned_hi, 1)

            def tokens(run, b, e, half, first):
                if not first:
                    act.wait_ge(run.up_gate_used, 4 * b - 1 + half)
                act.wait_ge(run.gathered, 2 * e + half + 1)
                copy(tokens_hi[:, 4 * half:4 * half + 4, :], GATHER[half].rearrange("p (k n) -> p k n", k=4)).then_inc(run.tokens_hi, 1)

            def routing(run, e, first):
                act.wait_ge(run.spread_turned, e + 1)
                if not first:
                    act.wait_ge(run.y_split, e)
                copy(cur_g, SPREAD_BANK[:, SEQ:SEQ + 1])
                copy(cur_spread[:, :], SPREAD_BANK[:, 0:SEQ]).then_inc(run.spread_ready, 1)

            def y_his(run, e):
                act.wait_ge(run.down_done, 2 * (e + 1) * E_CHUNKS)
                activation(y_hi[:, :], acc(0).rearrange("p b c -> p (b c)"), ACT.Copy, scale=cur_g).then_inc(run.y_hi_done, 1)

            def expert_chunk(run):
                def chunk(b, e, c):
                    no_chunk_before = isinstance(b, int) and b == 0
                    no_expert_before = isinstance(e, int)
                    split_before = no_chunk_before and run is main_pass
                    if not split_before:
                        expert_his(run, b, 0)
                        expert_his(run, b, 1)
                    if c == 0:
                        tokens(run, b, e, 0, no_chunk_before)
                    if c == 1 and not no_expert_before:
                        y_his(run, e - 1)
                    if c == 2:
                        routing(run, e, no_expert_before)
                    if not no_chunk_before:
                        expert_his(run, b - 1, 4)
                        expert_silu(run, b - 1)
                    if c == 0:
                        tokens(run, b, e, 1, no_chunk_before)
                    if not no_chunk_before:
                        expert_his(run, b - 1, 5)
                        turned_his(run, b - 1)
                    if not split_before:
                        expert_his(run, b, 2)
                        expert_his(run, b, 3)
                    act.wait_ge(run.up_gate_used, 4 * b + 2)
                    wait_from(act, run.hidden_ready, b)
                    copy(e_up, UP_BANK).then_inc(run.up_copied, 1)
                return chunk

            def expert_pass(run):
                for_chunks(act, expert_chunk(run))
                last = ALL_CHUNKS - 1
                expert_his(run, last, 4)
                expert_silu(run, last)
                expert_his(run, last, 5)
                turned_his(run, last)
                y_his(run, N_EXPERTS - 1)

            for layer in range(DEPTH):
                if layer == 0:
                    for t in range(NT):
                        act.wait_ge(x_in_s[t], 16)
                        square((layer, "pre", t), x[:, t, :], junk)
                    tile_his(layer, "pre", 0)
                    for half in range(2):
                        z_his(layer, 0, half)
                tile_his(layer, "pre", 1)
                for t in range(NT):
                    for b in range(2):
                        act.wait_ge(tile_split, tile_number(layer, "pre", t, b) + 1)
                        copy(hT[:, 4 * b:4 * b + 4, t * P:(t + 1) * P], acc(t)[:, b, :].rearrange("p (i s) -> p i s", i=4))\
                            .then_inc(pre_copied, 1)
                for s in MIXER:
                    if s[0] == "z":
                        c, w = s[1]
                        if s[1] in WIDE_Z:
                            i = WIDE_Z.index(s[1])
                            for t in range(NT):
                                if i + 1 < len(WIDE_Z):
                                    z_his(layer, i + 1, t)
                                bank = taken(layer, "z", c, t)
                                copy(z[:, t, c:c + w], bank[:, 0:w]).then_inc(ex_done, 1)
                        else:
                            bank = taken(layer, "z", c, 0)
                            copy(z[:, :, c:c + w], bank.rearrange("p (t s) -> p t s", t=NT)).then_inc(ex_done, 1)
                    elif s[0] == "norm_a":
                        act.wait_ge(ex_done, Z_DONE[(layer, A0)] + 1)
                        for kind, a, width in (("low_q", 0, A_Q_RANK), ("low_kv", A_Q_RANK, A_KV_RANK)):
                            for t in range(NT):
                                square((layer, kind, t), z[:, t, a:a + width], egate[:, 0, 0:width])
                    elif s[0] == "swap":
                        swapped(layer, s[1])
                    elif s[0] == "project_a":
                        for t in range(NT):
                            bank = taken(layer, "qa", t)
                            if t == 0:
                                act.wait_ge(ex_ready, USE[(layer, "kva", 0)] + 1)
                            copy(qa_sb[:, t, :], bank[:, 0:384]).then_inc(ex_done, 1)
                            bank = taken(layer, "kva", t)
                            copy(kva[:, t, :], bank).then_inc(ex_done, 1)
                    elif s[0] == "score":
                        _, j, b, h = s
                        n, i = len(JOBS) * layer + j, j % 2
                        scale = (A_QK if b == "A" else HD) ** -0.5
                        act.wait_ge(bias_done, n + 1)
                        for t in range(NT):
                            e = probs[:, i, t, 0:NSETS[b], :]
                            ins = activation(e, e, ACT.Exp, bias=bias[:, i, t:t + 1], scale=scale, accum_out=total[:, i, t:t + 1])
                        if b == "D":
                            ins = activation(sunk[:, i, :], bias[:, i, :], ACT.Exp, bias=sink[:, h:h + 1])
                        ins.then_inc(exp_done, 1)
                    elif s[0] == "turn":
                        _, j, b, h = s
                        for g in range(NSETS[b]):
                            bank = taken(layer, "turn", j, g)
                            n = SETS * layer + SET0[j] + g
                            wait_from(act, pv_done, n - NPT + 1)
                            copy(pT[:, n % NPT, :, :], bank.rearrange("p (k s) -> p k s", k=NT)).then_inc(ex_done, 1)
                    elif s[0] == "pv" and s[3] % 2:
                        _, j, b, h = s
                        act.wait_ge(pv_done, SETS * layer + SET0[j + 1])
                        copy(oT[:, 2 * BRANCH_ID[b] + h // 2, :], O_BANK).then_inc(o_done, 1)
                    elif s[0] == "fill":
                        u = s[1]
                        act.wait_ge(unit_ready, UNITS * layer + u + 1)
                        wait_from(act, unit_done, UNITS * layer + u - 1)
                        activation(egate[:, u % 2, :], ps[:, 6 + u % 2, 0:SEQ], ACT.Exp, scale=-1.0).then_inc(egate_done, 1)
                        if u > UNITS - NK:
                            merged_his(layer, u - 1)
                        if u in OUT_SPLITS:
                            weight_his(layer, "out", OUT_SPLITS.index(u))
                merged_his(layer, UNITS - 1)
                weight_his(layer, "out", 3)
                if layer % 2 == 0:
                    up_gate_his(0, 0)
                else:
                    for j in (0, 1):
                        expert_his(main_pass, 0, j)
                for t in range(NT):
                    act.wait_ge(mix_done, NT * layer + t + 1)
                    square((layer, "post", t), acc(t).rearrange("p b c -> p (b c)"), junk)
                    if t == 1:
                        turned_input(layer, 0)
                    act.wait_ge(x_done, X_COUNT(layer, 0, t))
                    square((layer, "fpre", t), x[:, t, :], junk)
                if layer % 2:
                    copy(lg[:, 0, :], taken(layer, "logits", 0)[:, 0:8]).then_inc(ex_done, 1)
                turned_input(layer, 1)
                if layer % 2:
                    for j in (2, 3):
                        expert_his(main_pass, 0, j)
                if layer % 2 == 0:
                    silus(0)
                    with act.Fori(1, FF_BODIES - 1) as body:
                        silus(body)
                    silus(FF_BODIES - 1, last=True)
                    act.wait_ge(ffn.down_done, N_FFN_BLOCKS)
                    for t in range(NT):
                        square((layer, "fpost", t), acc(t).rearrange("p b c -> p (b c)"), junk)
                else:
                    copy(lg[:, NT - 1, :], taken(layer, "logits", NT - 1)[:, 0:8]).then_inc(ex_done, 1)
                    act.wait_ge(route_exp_in, 1)
                    activation(rt[:, 3, :], rt[:, 2, :], ACT.Exp).then_inc(route_exp, 1)
                    bank = taken(layer, "rank")
                    copy(rank, bank[:, 0:24].rearrange("p (t e) -> p t e", t=3)).then_inc(ex_done, 1)
                    expert_pass(main_pass)
                    act.wait_ge(overflow_ready, 1)
                    more = act.value_load(overflow[0:1, 0:1], min_val=0, max_val=1)
                    with act.If(more > 0):
                        act.wait_ge(main_pass.added, 2 * N_EXPERTS)
                        expert_pass(over_pass)
                    act.wait_ge(moe_done, 1)
                    for t in range(NT):
                        square((layer, "fpost", t), fsum[:, t, :], junk)
                bank = taken(layer, "pt")
                copy(pleT, bank.rearrange("p (k s) -> p k s", k=2)).then_inc(ex_done, 1)
                weight_his(layer, "ple", 0)
                for t in range(NT):
                    for half in range(2):
                        bank = taken(layer, "proj", t, half)
                        copy(proj[:, t, half * 512:(half + 1) * 512], bank).then_inc(ex_done, 1)
                    if t == 0:
                        weight_his(layer, "ple", 1)
                tile_his(layer, "xt", 0)
                weight_his(layer, "ple", 2)
                weight_his(layer, "ple", 3)
                tile_his(layer, "xt", 1)
                if layer + 1 < DEPTH:
                    for half in range(2):
                        z_his(layer + 1, 0, half)
                for t in range(NT):
                    act.wait_ge(ple_done, NT * layer + t + 1)
                    activation(xn[:, t, :], acc(t).rearrange("p b c -> p (b c)"), ACT.Sigmoid).then_inc(ple_gate, 1)
                    if t == 1 and layer + 1 < DEPTH:
                        tile_his(layer + 1, "pre", 0)
                    act.wait_ge(ple_prod, NT * layer + t + 1)
                    square((layer, "ple", t), xn[:, t, :], junk)
                    if layer + 1 < DEPTH:
                        act.wait_ge(x_done, X_COUNT(layer, 2, t))
                        square((layer + 1, "pre", t), x[:, t, :], junk)

        @block.vector
        def _(dve):
            step = Count(dve_step)
            v = nc.vector

            def link(ins, s=None):
                s = s or step
                s.up(ins)
                s.wait(dve)

            def normed(layer, kind, g, t):
                n, k = 5 * layer + g, STAT[(layer, kind, t)]
                dve.wait_ge(gain_in[n % 2], 16 * (n // 2 + 1))
                dve.wait_ge(rstd_done, k + 1)
                v.scalar_tensor_tensor(out=xn[:, t, :], in0=x[:, t, :], scalar=rstd[:, k:k + 1], in1=gain[:, n % 2, :],
                                       op0=ALU.mult, op1=ALU.mult).then_inc(xn_done, 1)

            def residual(layer, kind, g, t, src, tmp):
                n, k = 5 * layer + g, STAT[(layer, kind, t)]
                dve.wait_ge(gain_in[n % 2], 16 * (n // 2 + 1))
                if kind == "post" or kind == "fpost" and layer % 2 == 0:
                    dve.wait_ge(sq_done, k + 1)
                link(v.tensor_tensor(tmp, src, gain[:, n % 2, :], ALU.mult))
                dve.wait_ge(rstd_done, k + 1)
                v.scalar_tensor_tensor(out=x[:, t, :], in0=tmp, scalar=rstd[:, k:k + 1], in1=x[:, t, :],
                                       op0=ALU.mult, op1=ALU.add).then_inc(x_done, 1)

            def tile_los(layer, kind, t):
                hi, lo = (zT_hi, zT_lo) if kind == "pre" else (hT_hi, hT_lo)
                for b in range(2):
                    dve.wait_ge(tile_hi, tile_number(layer, kind, t, b) + 1)
                    part = (slice(None), slice(4 * b, 4 * b + 4), slice(t * P, (t + 1) * P))
                    v.tensor_tensor(lo[part], acc(t)[:, b, :].rearrange("p (i s) -> p i s", i=4), hi[part], ALU.subtract)\
                        .then_inc(tile_split, 1)

            def z_los(layer, i, half):
                pos = WHERE[(layer, "z") + WIDE_Z[i] + (half,)]
                w = WIDE_Z[i][1]
                wide = lambda a: a.rearrange("p (k c) -> p k c", k=4)[:, :, 0:w]
                dve.wait_ge(z_hi, 8 * layer + 2 * i + half + 1)
                v.tensor_tensor(wide(ring_lo[:, pos % RING, :]), wide(slot_of(pos)), wide(z_hi_w[:, half, :]), ALU.subtract)\
                    .then_inc(z_split, 1)

            def merged_los(layer, u):
                c = u % 8
                dve.wait_ge(merged_hi, NK * layer + c + 1)
                v.tensor_tensor(hT_lo[:, c, :], mergedT[:, c, :], hT_hi[:, c, :], ALU.subtract).then_inc(merged_split, 1)

            def weight_los(layer, kind, i):
                slot = WHERE[(layer, kind, i)] % RING
                dve.wait_ge(weight_hi, weight_number(layer, kind, i) + 1)
                v.tensor_tensor(ring_lo[:, slot, :], ring[:, slot, :], weight_hi_w[:, i, :], ALU.subtract).then_inc(weight_split, 1)

            def rotate(src, dst, table, t, heads, groups):
                width = src.shape[2]
                half = width // groups // 2
                n = heads * width
                cos, sin = tab[table][:, 0, t, :], tab[table][:, 1, t, :]
                a = rot[:, 0, 0:n].rearrange("p (h d) -> p h d", h=heads)
                b = rot[:, 1, 0:n].rearrange("p (h d) -> p h d", h=heads)
                link(v.tensor_tensor(a, src, cos.unsqueeze(1).broadcast_to([P, heads, width]), ALU.mult))
                for g in range(groups):
                    for i in range(2):
                        to = slice((2 * g + i) * half, (2 * g + i + 1) * half)
                        of = slice((2 * g + 1 - i) * half, (2 * g + 2 - i) * half)
                        link(v.tensor_tensor(b[:, :, to], src[:, :, of], sin[:, to].unsqueeze(1).broadcast_to([P, heads, half]), ALU.mult))
                if dst is None:
                    return a, b
                return v.tensor_tensor(dst, a, b, ALU.add)

            def stage(layer, item):
                i = STAGED.index(item)
                n = len(STAGED) * layer + i
                if n >= 2:
                    l0, last = divmod(n - 2, len(STAGED))
                    name = STAGED[last]
                    dve.wait_ge(ex_ready, USE[(l0, "swap", name, 1 if name[0] == "A" else 0)] + 1)
                wait_from(dve, staged_done, n)
                return staged[:, n % 2]

            def rope(layer, item):
                if layer == 0 and item == "Bq":
                    dve.wait_ge(const_in_s, 32)
                r = stage(layer, item)
                b = item[0]
                if b == "A":
                    for t in range(NT):
                        rv = r[:, t, :].rearrange("p (h d) -> p h d", h=A_HEADS)
                        if item == "Aq":
                            if t == 0:
                                dve.wait_ge(ex_done, USE[(layer, "kva", NT - 1)] + 1)
                            src = qa_sb[:, t, :].rearrange("p (h d) -> p h d", h=A_HEADS)
                            link(rotate(src[:, :, A_NOPE:A_QK], rv[:, :, A_NOPE:A_QK], "a", t, A_HEADS, 1))
                            last = v.tensor_copy(rv[:, :, 0:A_NOPE], src[:, :, 0:A_NOPE])
                        else:
                            src = z[:, t, A_Q_RANK + A_KV_RANK:B0].unsqueeze(1)
                            one, two = rotate(src, None, "a", t, 1, 1)
                            link(v.tensor_tensor(rv[:, :, A_NOPE:A_QK], one.broadcast_to([P, A_HEADS, A_ROPE]),
                                                 two.broadcast_to([P, A_HEADS, A_ROPE]), ALU.add))
                            last = v.tensor_copy(rv[:, :, 0:A_NOPE],
                                                 kva[:, t, :].rearrange("p (h d) -> p h d", h=A_HEADS)[:, :, 0:A_NOPE])
                        if t == 0:
                            link(last)
                    last.then_inc(staged_done, 1)
                    return
                heads = 4 if item[-1] == "q" or b == "C" else 2
                if b == "C":
                    col = C0 + int(item[1]) * 12 * HD + (4 * HD if item[2] == "k" else 0)
                    dve.wait_ge(ex_done, Z_DONE[(layer, z_block(col))] + 1)
                else:
                    col = (B0 if b == "B" else D0) + (4 * HD if item[1] == "k" else 0)
                    if b == "D":
                        dve.wait_ge(ex_done, Z_DONE[(layer, D0)] + 1)
                for t in range(NT):
                    src = z[:, t, col:col + heads * HD].rearrange("p (h d) -> p h d", h=heads)
                    one, two = rotate(src, None, "axial" if b == "B" else "full", t, heads, 2 if b == "B" else 1)
                    dst = r[:, t, 0:heads * HD]
                    if b in "BD" and heads == 4:
                        dst = dst.rearrange("p (b x d) -> p x b d", b=2, x=2)
                        one = one.rearrange("p (x b) d -> p x b d", x=2)
                        two = two.rearrange("p (x b) d -> p x b d", x=2)
                    else:
                        dst = dst.rearrange("p (h d) -> p h d", h=heads)
                    last = v.tensor_tensor(dst, one, two, ALU.add)
                    if t == 0:
                        link(last)
                last.then_inc(staged_done, 1)

            def softmax(layer, j, b, h):
                i, n = j % 2, len(JOBS) * layer + j
                scale = (A_QK if b == "A" else HD) ** -0.5
                if n >= 2:
                    l0, jj = divmod(n - 2, len(JOBS))
                    dve.wait_ge(ex_ready, USE[(l0, "turn", jj, NSETS[JOBS[jj][0]] - 1)] + 1)
                for g in range(NSETS[b]):
                    k = SETS * layer + SET0[j] + g
                    dve.wait_ge(scored, k + 1)
                    for t in range(NT):
                        s = ps[:, 4 + k % 2, t * SEQ:(t + 1) * SEQ]
                        e, m = probs[:, i, t, g, :], peak[:, i, t, g:g + 1]
                        if b in "AB":
                            ins = v.tensor_scalar(e, s, 1.0, None, ALU.mult, ALU.max, accum_out=m)
                        else:
                            ins = v.tensor_tensor_reduce(out=e, in0=s, in1=mask[:, g if b == "C" else 3, t, :], scale=1.0,
                                                         scalar=-3.0e38, op0=ALU.add, op1=ALU.max, accum_out=m)
                    ins.then_inc(score_read, 1)
                dve.wait_ge(score_read, SETS * layer + SET0[j + 1])
                src = peak[:, i, :, 0]
                if b == "C":
                    link(v.tensor_reduce(top[:, i, :], peak[:, i, :, :], AX.X, ALU.max))
                    src = top[:, i, :]
                if b == "D":
                    link(v.tensor_scalar(top[:, i, :], src, scale, sink[:, h:h + 1], ALU.mult, ALU.max))
                    v.tensor_scalar(bias[:, i, :], top[:, i, :], -1.0, None, ALU.mult).then_inc(bias_done, 1)
                else:
                    v.tensor_scalar(bias[:, i, :], src, -scale, None, ALU.mult).then_inc(bias_done, 1)
                dve.wait_ge(exp_done, n + 1)
                if b == "D":
                    link(v.tensor_tensor(total[:, i, :], total[:, i, :], sunk[:, i, :], ALU.add))
                link(v.reciprocal(inv[:, i, :], total[:, i, :]))
                for t in range(NT):
                    e = probs[:, i, t, 0:NSETS[b], :]
                    ins = v.tensor_scalar(e, e, inv[:, i, t:t + 1], None, ALU.mult)
                ins.then_inc(prob_done, 1)

            def up_gate_los(i, body):
                for n in range(2):
                    slot = ring_slot(3 * i + n)
                    dve.wait_ge(ffn.up_gate_hi, 4 * body + 2 * i + n + 1)
                    v.tensor_tensor(ring_lo[:, slot, :], ring[:, slot, :], up_gate_hi_w[:, 2 * i + n, :], ALU.subtract)\
                        .then_inc(ffn.up_gate_split, 1)

            def hiddens(body, last=False):
                block0 = body * FF_BLOCKS
                for j in range(FF_BLOCKS):
                    if j % 2 == 0:
                        dve.wait_ge(ffn.down_hi, body * 2 + j // 2 + 1)
                        wait_from(dve, ffn.down_done, block0 + j - 2)
                        v.tensor_tensor(down_lo_w[:, j // 2, :], ring[:, ring_slot(3 * (j // 2) + 2), :], down_hi_w[:, j // 2, :],
                                        ALU.subtract).then_inc(ffn.down_split, 1)
                    h, hi, lo = hidden[:, j % 2, :], hidden_hi[:, j, :], hidden_lo[:, j, :]
                    dve.wait_ge(ffn.silu_ready, block0 + j + 1)
                    wait_from(dve, ffn.down_done, block0 + j - 3)
                    wait_from(dve, ffn.hidden_ready, block0 + j)
                    v.tensor_tensor(h, silu[:, j, :], ps[:, j, 0:SEQ], ALU.mult).then_inc(ffn.hidden_step, 1)
                    steps = block0 * 2 + 2 * j
                    dve.wait_ge(ffn.hidden_step, steps + 1)
                    v.tensor_copy(hi, h).then_inc(ffn.hidden_step, 1)
                    dve.wait_ge(ffn.hidden_step, steps + 2)
                    v.tensor_tensor(lo, h, hi, ALU.subtract).then_inc(ffn.hidden_ready, 1)
                    if j == 0:
                        up_gate_los(1, body)
                    if j == 2 and not last:
                        up_gate_los(0, body + 1)

            def expert_los(run, b, j):
                slot = expert_slot(j)
                if j < 4:
                    dve.wait_ge(run.up_gate_hi, 4 * b + j + 1)
                    v.tensor_tensor(ring_lo[:, slot, :], ring[:, slot, :], up_gate_hi_w[:, j, :], ALU.subtract)\
                        .then_inc(run.up_gate_split, 1)
                else:
                    dve.wait_ge(run.down_hi, 2 * b + j - 3)
                    wait_from(dve, run.down_done, 2 * (b - 1) + j - 3)
                    v.tensor_tensor(down_lo_w[:, j - 4, :], ring[:, slot, :], down_hi_w[:, j - 4, :], ALU.subtract)\
                        .then_inc(run.down_split, 1)

            def expert_hidden(run, b):
                dve.wait_ge(run.silu_ready, b + 1)
                dve.wait_ge(run.up_copied, b + 1)
                wait_from(dve, run.turned, b)
                v.tensor_tensor(e_hidden, e_silu, e_up, ALU.mult).then_inc(run.hidden_ready, 1)

            def turned_los(run, b):
                dve.wait_ge(run.turned_hi, b + 1)
                v.tensor_tensor(hidden_lo[:, :, 0:CAP], TURN_BANK.rearrange("p (j n) -> p j n", j=E_BLOCKS),
                                hidden_hi[:, :, 0:CAP], ALU.subtract).then_inc(run.turned_split, 1)

            def token_los(run, e, half):
                dve.wait_ge(run.tokens_hi, 2 * e + half + 1)
                blocks = slice(4 * half, 4 * half + 4)
                v.tensor_tensor(tokens_lo[:, blocks, :], GATHER[half].rearrange("p (k n) -> p k n", k=4),
                                tokens_hi[:, blocks, :], ALU.subtract).then_inc(run.tokens_split, 1)

            def y_los(run, e):
                dve.wait_ge(run.y_hi_done, e + 1)
                v.scalar_tensor_tensor(out=y_lo[:, :], in0=acc(0).rearrange("p b c -> p (b c)"), scalar=cur_g, in1=y_hi[:, :],
                                       op0=ALU.mult, op1=ALU.subtract).then_inc(run.y_split, 1)

            def add_back(run, e):
                for t in range(NT):
                    dve.wait_ge(run.back, 2 * e + t + 1)
                    v.tensor_tensor(fsum[:, t, :], fsum[:, t, :], BACK[t].rearrange("p b c -> p (b c)"), ALU.add).then_inc(run.added, 1)
                dve.wait_ge(run.added, 2 * e + NT)

            def picks(run, e, i):
                for of, to in ((rank, cur_rank), (chosen, cur_chosen), (weight, cur_weight)):
                    ins = v.tensor_copy(to.unsqueeze(2), of[:, 0:NT, bass.ds(e, 1)])
                ins.then_inc(run.columns, 1)
                dve.wait_ge(run.columns, i + 1)
                for t in range(NT):
                    ins = v.tensor_scalar(pick[:, t, :], iota, cur_rank[:, t:t + 1], cur_chosen[:, t:t + 1], ALU.is_equal, ALU.mult)
                ins.then_inc(run.picked, 1)

            def expert_chunk(run):
                def chunk(b, e, c):
                    no_chunk_before = isinstance(b, int) and b == 0
                    no_expert_before = isinstance(e, int)
                    split_before = no_chunk_before and run is main_pass
                    if c == "last":
                        dve.wait_ge(run.spread_turned, e + 1)
                        dve.wait_ge(run.picked, e + 1)
                        picks(run, (e + 1) % N_EXPERTS, e + 1)
                    if not split_before:
                        expert_los(run, b, 0)
                        expert_los(run, b, 1)
                    if c == 0:
                        token_los(run, e, 0)
                    if c == 1 and not no_expert_before:
                        y_los(run, e - 1)
                    if not no_chunk_before:
                        expert_los(run, b - 1, 4)
                        expert_hidden(run, b - 1)
                    if c == 0:
                        token_los(run, e, 1)
                    if not no_chunk_before:
                        expert_los(run, b - 1, 5)
                        turned_los(run, b - 1)
                    if not split_before:
                        expert_los(run, b, 2)
                    if c == 1 and not no_expert_before:
                        add_back(run, e - 1)
                    if not split_before:
                        expert_los(run, b, 3)
                return chunk

            def expert_pass(run):
                if run is main_pass:
                    dve.wait_ge(ex_done, USE[(1, "rank")] + 1)
                picks(run, 0, 0)
                if run is main_pass:
                    check_overflow()
                    link(v.memset(fsum, 0.0))
                for_chunks(dve, expert_chunk(run))
                last = ALL_CHUNKS - 1
                expert_los(run, last, 4)
                expert_hidden(run, last)
                expert_los(run, last, 5)
                turned_los(run, last)
                y_los(run, N_EXPERTS - 1)
                add_back(run, N_EXPERTS - 1)

            def route():
                bc = lambda a: a.unsqueeze(2).broadcast_to([P, NT, 8])
                r = lambda n: rt[:, n, :]
                dve.wait_ge(ex_done, USE[(1, "logits", NT - 1)] + 1)
                link(v.tensor_tensor(lg, lg, rtr_b[:, :, :], ALU.add))
                for n, onehot in enumerate((first, second)):
                    link(v.tensor_reduce(r(n), lg, AX.X, ALU.max))
                    link(v.tensor_tensor(eq, lg, bc(r(n)), ALU.is_equal))
                    link(v.tensor_scalar(eq, eq, -100.0, 100.0, ALU.mult, ALU.add))
                    link(v.tensor_tensor(idx, eq, iota8, ALU.add))
                    link(v.tensor_reduce(r(4), idx, AX.X, ALU.min))
                    link(v.tensor_tensor(onehot, idx, bc(r(4)), ALU.is_equal))
                    if n == 0:
                        link(v.scalar_tensor_tensor(out=lg, in0=onehot, scalar=-3.0e38, in1=lg, op0=ALU.mult, op1=ALU.add))
                v.tensor_tensor(r(2), r(1), r(0), ALU.subtract).then_inc(route_exp_in, 1)
                dve.wait_ge(route_exp, 1)
                link(v.tensor_scalar(r(5), r(3), 1.0, None, ALU.add))
                link(v.reciprocal(r(6), r(5)))
                link(v.tensor_tensor(r(7), r(3), r(6), ALU.mult))
                link(v.tensor_tensor(weight, first, bc(r(6)), ALU.mult))
                link(v.tensor_tensor(eq, second, bc(r(7)), ALU.mult))
                link(v.tensor_tensor(weight, weight, eq, ALU.add))
                v.tensor_tensor(chosen, first, second, ALU.add).then_inc(routed, 1)
                expert_los(main_pass, 0, 3)

            def check_overflow():
                r = lambda n: rt[:, n, :]
                link(v.tensor_scalar(overflow_f, rank[:, 2, :], float(CAP), None, ALU.is_gt))
                link(v.tensor_reduce(r(0)[:, 0:1], overflow_f, AX.X, ALU.max))
                v.tensor_copy(overflow[:, :], r(0)[:, 0:1]).then_inc(overflow_ready, 1)

            dve.wait_ge(x_in_s[NT - 1], 16)
            for layer in range(DEPTH):
                if layer == 0:
                    for t in range(NT):
                        normed(layer, "pre", 0, t)
                    tile_los(layer, "pre", 0)
                    for half in range(2):
                        z_los(layer, 0, half)
                tile_los(layer, "pre", 1)
                for s in MIXER:
                    if s[0] == "z" and s[1] in WIDE_Z[:-1]:
                        for half in range(2):
                            z_los(layer, WIDE_Z.index(s[1]) + 1, half)
                    if s[0] == "norm_b":
                        dve.wait_ge(ex_done, Z_DONE[(layer, B0)] + 1)
                        dve.wait_ge(params_in, PARAMS(layer))
                        for t in range(NT):
                            q = z[:, t, B0:B0 + 6 * HD]
                            link(v.tensor_tensor(rot[:, 0, :], q, q, ALU.mult))
                            ins = v.tensor_reduce(sumsq_b[:, t, :], rot[:, 0, :].rearrange("p (h d) -> p h d", h=6), AX.X, ALU.add)
                            if t == 0:
                                link(ins)
                        ins.then_inc(sqb_done, 1)
                        dve.wait_ge(rstdb_done, layer + 1)
                        for t in range(NT):
                            q = z[:, t, B0:B0 + 6 * HD].rearrange("p (h d) -> p h d", h=6)
                            link(v.tensor_tensor(q, q, rstd_b[:, t, :].unsqueeze(2).broadcast_to([P, 6, HD]), ALU.mult))
                            link(v.tensor_tensor(q, q, gain_b[:, :, :], ALU.mult))
                    elif s[0] == "norm_a":
                        r = stage(layer, "An")
                        for t in range(NT):
                            for kind, a, w in (("low_q", 0, A_Q_RANK), ("low_kv", A_Q_RANK, A_KV_RANK)):
                                k = STAT[(layer, kind, t)]
                                dve.wait_ge(rstd_done, STAT[(layer, "low_kv", NT - 1)] + 1)
                                ins = v.scalar_tensor_tensor(out=r[:, t, a:a + w], in0=z[:, t, a:a + w], scalar=rstd[:, k:k + 1],
                                                             in1=gain_a[:, a:a + w], op0=ALU.mult, op1=ALU.mult)
                        ins.then_inc(staged_done, 1)
                    elif s[0] == "rope":
                        rope(layer, s[1])
                    elif s[0] == "score":
                        softmax(layer, *s[1:])
                    elif s[0] == "fill":
                        u = s[1]
                        n, c = UNITS * layer + u, u % 8
                        e = egate[:, u % 2, :]
                        dve.wait_ge(egate_done, n + 1)
                        link(v.tensor_scalar(e, e, 1.0, None, ALU.add))
                        link(v.reciprocal(e, e))
                        up = ps[:, 6 + u % 2, SEQ:2 * SEQ]
                        if u < 8:
                            v.tensor_tensor(mergedT[:, c, :], up, e, ALU.mult).then_inc(unit_done, 1)
                        else:
                            link(v.tensor_tensor(e, up, e, ALU.mult))
                            v.tensor_tensor(mergedT[:, c, :], mergedT[:, c, :], e, ALU.add).then_inc(unit_done, 1)
                        if u > UNITS - NK:
                            merged_los(layer, u - 1)
                        if u in OUT_SPLITS:
                            weight_los(layer, "out", OUT_SPLITS.index(u))
                merged_los(layer, UNITS - 1)
                weight_los(layer, "out", 3)
                if layer % 2 == 0:
                    up_gate_los(0, 0)
                else:
                    for j in (0, 1):
                        expert_los(main_pass, 0, j)
                flat = lambda t: acc(t).rearrange("p b c -> p (b c)")
                for t in range(NT):
                    dve.wait_ge(mix_done, NT * layer + t + 1)
                    residual(layer, "post", 1, t, flat(t), post_tmp[:, t, :])
                    if t == 1 and layer % 2 == 0:
                        tile_los(layer, "fpre", 0)
                    normed(layer, "fpre", 2, t)
                if layer % 2 == 0:
                    tile_los(layer, "fpre", 1)
                    hiddens(0)
                    with dve.Fori(1, FF_BODIES - 1) as body:
                        hiddens(body)
                    hiddens(FF_BODIES - 1, last=True)
                    dve.wait_ge(ffn.down_done, N_FFN_BLOCKS)
                    for t in range(NT):
                        residual(layer, "fpost", 3, t, flat(t), post_tmp[:, t, :])
                else:
                    expert_los(main_pass, 0, 2)
                    route()
                    expert_pass(main_pass)
                    more = dve.value_load(overflow[0:1, 0:1], min_val=0, max_val=1)
                    with dve.If(more > 0):
                        v.tensor_scalar(rank, rank, float(-CAP), None, ALU.add).then_inc(over_ranked, 1)
                        dve.wait_ge(over_ranked, 1)
                        expert_pass(over_pass)
                    v.memset(overflow_f, 0.0).then_inc(moe_done, 1)
                    for t in range(NT):
                        residual(layer, "fpost", 3, t, fsum[:, t, :], xn[:, t, :])
                weight_los(layer, "ple", 0)
                weight_los(layer, "ple", 1)
                tile_los(layer, "xt", 0)
                weight_los(layer, "ple", 2)
                weight_los(layer, "ple", 3)
                tile_los(layer, "xt", 1)
                if layer + 1 < DEPTH:
                    for half in range(2):
                        z_los(layer + 1, 0, half)
                for t in range(NT):
                    n = NT * layer + t
                    dve.wait_ge(ple_gate, n + 1)
                    e = xn[:, t, :]
                    v.tensor_tensor(e, e, proj[:, t, :], ALU.mult).then_inc(ple_prod, 1)
                    dve.wait_ge(ple_prod, n + 1)
                    if t == 1 and layer + 1 < DEPTH:
                        tile_los(layer + 1, "pre", 0)
                    residual(layer, "ple", 4, t, e, ple_tmp[:, t, :])
                    if layer + 1 < DEPTH:
                        normed(layer + 1, "pre", 0, t)


_INS = ["x", "p", "w_in", "a_qa_g", "a_kva_g", "a_w_uq", "a_w_ukv", "b_q_g", "b_k_g", "d_sink", "w_branch", "w_out",
        "mix_pre_g", "mix_post_g", "ffn_pre_g", "ffn_post_g", "ffn_w_gate", "ffn_w_up", "ffn_w_down",
        "router_w", "router_b", "moe_w_gate", "moe_w_up", "moe_w_down", "ple_w_proj", "ple_w_gate", "ple_post_g"]


def kernel(**inputs):
    import concourse.bacc as bacc
    from concourse.bass_utils import run_bass_kernel_spmd as run

    nc = bacc.Bacc("TRN2", target_bir_lowering=False, num_devices=1)
    arrays, args = {}, []
    for name in _INS:
        a = np.ascontiguousarray(inputs[name])
        arrays[f"in_{name}_dram"] = a
        args.append(nc.dram_tensor(f"in_{name}_dram", a.shape, mybir.dt.from_np(a.dtype), kind="ExternalInput").ap())
    arrays["in_const_dram"] = constants()
    args.append(nc.dram_tensor("in_const_dram", (P, CONST_W), F32, kind="ExternalInput").ap())
    args.append(nc.dram_tensor("out_0_dram", (1, SEQ, D_MODEL), F32, kind="ExternalOutput").ap())
    trunk(nc, args)
    r = run(nc, [arrays], core_ids=[0])
    return r.results[0]["out_0_dram"]
```
